# Optimizing a Trainium2 kernel written in Bass

```python
import math
import numpy as np
import jax
import jax.numpy as jnp
from jax import lax
import jax, jax.numpy as jnp

D_MODEL = 1024
BATCH = 1
SEQ = 512
DEPTH = 2

NORM_EPS = 1e-6
N_MOD = 6
Q_BLOCK = 128
NEG_INF = -1e30

SSD_HEADS = 16
SSD_HEAD_DIM = 64
SSD_INNER = SSD_HEADS * SSD_HEAD_DIM
SSD_STATE = 128
SSD_GROUPS = 2
SSD_CONV = 4
SSD_CONV_CH = SSD_INNER + 2 * SSD_GROUPS * SSD_STATE
SSD_CHUNK = 128

MLA_HEADS = 8
MLA_Q_RANK = 384
MLA_KV_RANK = 256
MLA_NOPE = 64
MLA_ROPE = 32
MLA_V = 64
ROPE_THETA = 10000.0

GLA_HEADS = 4
GLA_DK = 128
GLA_DV = 256
GLA_GATE_RANK = 16
GLA_GATE_NORM = 16.0
GLA_CHUNK = 64

NSA_HEADS = 8
NSA_GROUPS = 2
NSA_HEAD_DIM = 64
NSA_CMP_BLOCK = 32
NSA_CMP_STRIDE = 16
NSA_CMP_HIDDEN = 256
NSA_SEL_BLOCK = 64
NSA_N_SEL = 16
NSA_WINDOW = 512
NSA_FORCE = 1e4

FFN_HIDDEN = -(-8 * D_MODEL // (3 * 256)) * 256

L0_SIZES = (SSD_INNER, SSD_CONV_CH, SSD_HEADS, MLA_Q_RANK, MLA_KV_RANK, MLA_ROPE)
L0_IN = sum(L0_SIZES)
L0_CAT = SSD_INNER + MLA_HEADS * MLA_V
L1_SIZES = (GLA_HEADS * GLA_DK, GLA_HEADS * GLA_DK, GLA_HEADS * GLA_DV, GLA_GATE_RANK,
            GLA_HEADS * GLA_DV, NSA_HEADS * NSA_HEAD_DIM, 6 * NSA_GROUPS * NSA_HEAD_DIM, 3 * NSA_HEADS)
L1_IN = sum(L1_SIZES)
L1_CAT = GLA_HEADS * GLA_DV + NSA_HEADS * NSA_HEAD_DIM


def rmsnorm(x, g):
    xf = x.astype(jnp.float32)
    y = xf * lax.rsqrt(jnp.mean(xf * xf, axis=-1, keepdims=True) + NORM_EPS)
    return (y * g.astype(jnp.float32)).astype(x.dtype)

def split_cols(h, sizes):
    return jnp.split(h, [int(v) for v in np.cumsum(sizes)[:-1]], axis=-1)

def masked_softmax(s, mask):
    s = jnp.where(mask, s.astype(jnp.float32), NEG_INF)
    m = jnp.max(s, axis=-1, keepdims=True)
    e = jnp.where(mask, jnp.exp(s - m), 0.0)
    return e / jnp.maximum(jnp.sum(e, axis=-1, keepdims=True), 1e-30)

def alibi_slopes(n):
    return jnp.asarray(2.0 ** (-8.0 * np.arange(1, n + 1) / n), jnp.float32)

def rope_cos_sin(positions, dim):
    inv = jnp.asarray(ROPE_THETA ** (-np.arange(0, dim, 2) / dim), jnp.float32)
    ang = positions.astype(jnp.float32)[..., None] * inv
    return jnp.cos(ang), jnp.sin(ang)

def apply_rope(x, cos, sin):
    x1, x2 = jnp.split(x, 2, axis=-1)
    return jnp.concatenate([x1 * cos - x2 * sin, x2 * cos + x1 * sin], axis=-1).astype(x.dtype)

def causal_depthwise_conv(x, w, b):
    k_w, ch = w.shape
    y = lax.conv_general_dilated(x, w[:, None, :].astype(x.dtype), window_strides=(1,),
                                 padding=[(k_w - 1, 0)], dimension_numbers=('NWC', 'WIO', 'NWC'),
                                 feature_group_count=ch)
    return y + b

def segsum(a):
    n = a.shape[-1]
    cs = jnp.cumsum(a, axis=-1)
    diff = cs[..., :, None] - cs[..., None, :]
    return jnp.where(jnp.tril(jnp.ones((n, n), bool)), diff, -jnp.inf)

def ssd_chunked(x, dt, a, bmat, cmat):
    b, t, nh, p = x.shape
    g, n = bmat.shape[2], bmat.shape[3]
    hg = nh // g
    L = SSD_CHUNK
    c = t // L
    xd = (x.astype(jnp.float32) * dt[..., None]).reshape(b, c, L, g, hg, p)
    adt = (dt * a).reshape(b, c, L, g, hg).transpose(0, 3, 4, 1, 2)
    bm = bmat.astype(jnp.float32).reshape(b, c, L, g, n)
    cm = cmat.astype(jnp.float32).reshape(b, c, L, g, n)
    a_cs = jnp.cumsum(adt, axis=-1)
    lmat = jnp.exp(segsum(adt))
    y_diag = jnp.einsum('bclgn,bcsgn,bghcls,bcsghp->bclghp', cm, bm, lmat, xd)
    decay_states = jnp.exp(a_cs[..., -1:] - a_cs)
    states = jnp.einsum('bcsgn,bghcs,bcsghp->bcghpn', bm, decay_states, xd)
    states = jnp.concatenate([jnp.zeros_like(states[:, :1]), states], axis=1)
    a_chunk = jnp.pad(a_cs[..., -1], ((0, 0), (0, 0), (0, 0), (1, 0)))
    decay_chunk = jnp.exp(segsum(a_chunk))
    states = jnp.einsum('bghzc,bcghpn->bzghpn', decay_chunk, states)[:, :-1]
    y_off = jnp.einsum('bclgn,bcghpn,bghcl->bclghp', cm, states, jnp.exp(a_cs))
    return (y_diag + y_off).reshape(b, t, nh, p)

def gla_chunked(q, k, v, log_a):
    b, t, nh, dk = q.shape
    dv = v.shape[-1]
    L = GLA_CHUNK
    c = t // L

    def to_chunks(z):
        return z.astype(jnp.float32).reshape(b, c, L, nh, -1).transpose(1, 0, 3, 2, 4)

    qc = to_chunks(q) * (dk ** -0.5)
    kc, vc = to_chunks(k), to_chunks(v)
    bc = jnp.cumsum(to_chunks(log_a), axis=3)
    causal = jnp.tril(jnp.ones((L, L), bool))[:, :, None]

    def step(state, inp):
        qi, ki, vi, bi = inp
        o_inter = jnp.einsum('bhtk,bhkv->bhtv', qi * jnp.exp(bi), state)
        decay = jnp.exp(jnp.where(causal, bi[:, :, :, None, :] - bi[:, :, None, :, :], -jnp.inf))
        att = jnp.einsum('bhtk,bhsk,bhtsk->bhts', qi, ki, decay)
        o = o_inter + jnp.einsum('bhts,bhsv->bhtv', att, vi)
        b_last = bi[:, :, -1]
        state = jnp.exp(b_last)[..., None] * state + jnp.einsum(
            'bhsk,bhsv->bhkv', ki * jnp.exp(b_last[:, :, None] - bi), vi)
        return state, o

    s0 = jnp.zeros((b, nh, dk, dv), jnp.float32)
    _, o = lax.scan(step, s0, (qc, kc, vc, bc))
    return o.transpose(1, 0, 3, 2, 4).reshape(b, t, nh, dv)

def causal_block_attention(q, k, v, scale):
    b, t, nh, _ = q.shape
    dv = v.shape[-1]
    key_pos = jnp.arange(t)

    def one_block(i):
        q0 = i * Q_BLOCK
        qb = lax.dynamic_slice_in_dim(q, q0, Q_BLOCK, 1)
        qpos = q0 + jnp.arange(Q_BLOCK)
        s = jnp.einsum('bqhd,bkhd->bhqk', qb, k) * scale
        p = masked_softmax(s, key_pos[None, :] <= qpos[:, None])
        return jnp.einsum('bhqk,bkhd->bqhd', p.astype(v.dtype), v)

    out = lax.map(one_block, jnp.arange(t // Q_BLOCK))
    return out.transpose(1, 0, 2, 3, 4).reshape(b, t, nh * dv)

def nsa_attention(nq, nkv, ngate, cmp_pos, cmp_k_w1, cmp_k_w2, cmp_v_w1, cmp_v_w2):
    b, t, _ = nq.shape
    g, hg, dh = NSA_GROUPS, NSA_HEADS // NSA_GROUPS, NSA_HEAD_DIM
    q = nq.reshape(b, t, g, hg, dh)
    kc, vc, ks, vs, kw, vw = [z.reshape(b, t, g, dh) for z in split_cols(nkv, (g * dh,) * 6)]
    gates = jax.nn.sigmoid(ngate.astype(jnp.float32)).reshape(b, t, g, hg, 3)
    slopes = alibi_slopes(NSA_HEADS).reshape(g, hg)
    scale = dh ** -0.5

    n_cmp = (t - NSA_CMP_BLOCK) // NSA_CMP_STRIDE + 1
    win_idx = np.arange(n_cmp)[:, None] * NSA_CMP_STRIDE + np.arange(NSA_CMP_BLOCK)[None, :]

    def compress(z, w1, w2):
        zb = z[:, win_idx] + cmp_pos[None, None, :, None, :]
        zb = zb.transpose(0, 1, 3, 2, 4).reshape(b, n_cmp, g, NSA_CMP_BLOCK * dh)
        return jax.nn.silu(zb @ w1) @ w2

    k_cmp = compress(kc, cmp_k_w1, cmp_k_w2)
    v_cmp = compress(vc, cmp_v_w1, cmp_v_w2)
    cmp_end = np.arange(n_cmp) * NSA_CMP_STRIDE + NSA_CMP_BLOCK - 1

    n_slc = t // NSA_SEL_BLOCK
    n_sel = min(NSA_N_SEL, n_slc)
    c_start = np.arange(n_cmp) * NSA_CMP_STRIDE
    s_start = np.arange(n_slc) * NSA_SEL_BLOCK
    overlap = jnp.asarray((c_start[:, None] < s_start[None, :] + NSA_SEL_BLOCK)
                          & (c_start[:, None] + NSA_CMP_BLOCK > s_start[None, :]), jnp.float32)
    ks_blk = ks.reshape(b, n_slc, NSA_SEL_BLOCK, g, dh).transpose(0, 3, 1, 2, 4)
    vs_blk = vs.reshape(b, n_slc, NSA_SEL_BLOCK, g, dh).transpose(0, 3, 1, 2, 4)
    gather = jax.vmap(jax.vmap(lambda blocks, ix: blocks[ix]))

    pad = ((0, 0), (NSA_WINDOW, 0), (0, 0), (0, 0))
    kw_pad, vw_pad = jnp.pad(kw, pad), jnp.pad(vw, pad)
    blk = jnp.arange(n_slc)
    m_sel = n_sel * NSA_SEL_BLOCK

    def one_block(i):
        q0 = i * Q_BLOCK
        qpos = q0 + jnp.arange(Q_BLOCK)
        qb = lax.dynamic_slice_in_dim(q, q0, Q_BLOCK, 1)
        gb = lax.dynamic_slice_in_dim(gates, q0, Q_BLOCK, 1)
        dist_c = (qpos[:, None] - cmp_end[None, :]).astype(jnp.float32)
        s_c = jnp.einsum('bqghd,bngd->bghqn', qb, k_cmp) * scale - slopes[:, :, None, None] * dist_c
        p_c = masked_softmax(s_c, dist_c >= 0)
        o_c = jnp.einsum('bghqn,bngd->bqghd', p_c, v_cmp)
        imp = jnp.einsum('bghqn,nj->bgqj', p_c, overlap)
        forced = (blk[None, :] == 0) | (blk[None, :] == (qpos // NSA_SEL_BLOCK)[:, None])
        avail = blk[None, :] * NSA_SEL_BLOCK <= qpos[:, None]
        imp = jnp.where(forced, NSA_FORCE, jnp.where(avail, imp, -1.0))
        _, idx = lax.top_k(imp, n_sel)
        k_sel = gather(ks_blk, idx).reshape(b, g, Q_BLOCK, m_sel, dh)
        v_sel = gather(vs_blk, idx).reshape(b, g, Q_BLOCK, m_sel, dh)
        spos = (idx[..., None] * NSA_SEL_BLOCK + jnp.arange(NSA_SEL_BLOCK)).reshape(b, g, 1, Q_BLOCK, m_sel)
        dist_s = (qpos[:, None] - spos).astype(jnp.float32)
        s_s = jnp.einsum('bqghd,bgqmd->bghqm', qb, k_sel) * scale - slopes[None, :, :, None, None] * dist_s
        p_s = masked_softmax(s_s, dist_s >= 0)
        o_s = jnp.einsum('bghqm,bgqmd->bqghd', p_s, v_sel)
        kwb = lax.dynamic_slice_in_dim(kw_pad, q0, NSA_WINDOW + Q_BLOCK, 1)
        vwb = lax.dynamic_slice_in_dim(vw_pad, q0, NSA_WINDOW + Q_BLOCK, 1)
        kpos = q0 - NSA_WINDOW + jnp.arange(NSA_WINDOW + Q_BLOCK)
        dist_w = qpos[:, None] - kpos[None, :]
        mask_w = (dist_w >= 0) & (dist_w < NSA_WINDOW) & (kpos[None, :] >= 0)
        s_w = jnp.einsum('bqghd,bkgd->bghqk', qb, kwb) * scale - slopes[:, :, None, None] * dist_w.astype(jnp.float32)
        p_w = masked_softmax(s_w, mask_w)
        o_w = jnp.einsum('bghqk,bkgd->bqghd', p_w, vwb)
        o = gb[..., 0:1] * o_c + gb[..., 1:2] * o_s + gb[..., 2:3] * o_w
        return o.reshape(b, Q_BLOCK, NSA_HEADS * dh)

    out = lax.map(one_block, jnp.arange(t // Q_BLOCK))
    return out.transpose(1, 0, 2, 3).reshape(b, t, NSA_HEADS * dh)

def mixer_ssd_mla(h, positions, w_in, conv_w, conv_b, dt_bias, a_log, d_skip, ssm_norm_g,
                  q_a_norm_g, w_q_b, kv_a_norm_g, w_kv_b, w_out):
    b, t, _ = h.shape
    z, xbc, dt_raw, q_a, kv_a, k_pe = split_cols(h @ w_in, L0_SIZES)
    xbc = jax.nn.silu(causal_depthwise_conv(xbc, conv_w, conv_b))
    xs, bmat, cmat = split_cols(xbc, (SSD_INNER, SSD_GROUPS * SSD_STATE, SSD_GROUPS * SSD_STATE))
    dt = jax.nn.softplus(dt_raw.astype(jnp.float32) + dt_bias.astype(jnp.float32))
    a = -jnp.exp(a_log.astype(jnp.float32))
    xs = xs.reshape(b, t, SSD_HEADS, SSD_HEAD_DIM)
    y = ssd_chunked(xs, dt, a, bmat.reshape(b, t, SSD_GROUPS, SSD_STATE),
                    cmat.reshape(b, t, SSD_GROUPS, SSD_STATE))
    y = y + d_skip.astype(jnp.float32)[:, None] * xs.astype(jnp.float32)
    gsz = SSD_INNER // SSD_GROUPS
    y = y.reshape(b, t, SSD_GROUPS, gsz) * jax.nn.silu(z.astype(jnp.float32).reshape(b, t, SSD_GROUPS, gsz))
    y_ssd = rmsnorm(y, ssm_norm_g.reshape(SSD_GROUPS, gsz)).reshape(b, t, SSD_INNER).astype(h.dtype)
    cos, sin = rope_cos_sin(positions, MLA_ROPE)
    q = (rmsnorm(q_a, q_a_norm_g) @ w_q_b).reshape(b, t, MLA_HEADS, MLA_NOPE + MLA_ROPE)
    q = jnp.concatenate([q[..., :MLA_NOPE],
                         apply_rope(q[..., MLA_NOPE:], cos[:, :, None], sin[:, :, None])], axis=-1)
    kv = (rmsnorm(kv_a, kv_a_norm_g) @ w_kv_b).reshape(b, t, MLA_HEADS, MLA_NOPE + MLA_V)
    k_rot = apply_rope(k_pe, cos, sin)
    k = jnp.concatenate([kv[..., :MLA_NOPE],
                         jnp.broadcast_to(k_rot[:, :, None], (b, t, MLA_HEADS, MLA_ROPE))], axis=-1)
    o_mla = causal_block_attention(q, k, kv[..., MLA_NOPE:], (MLA_NOPE + MLA_ROPE) ** -0.5).astype(h.dtype)
    return jnp.concatenate([y_ssd, o_mla], axis=-1) @ w_out

def mixer_gla_nsa(h, w_in, w_gk2, b_gk, gla_norm_g, cmp_pos, cmp_k_w1, cmp_k_w2, cmp_v_w1, cmp_v_w2, w_out):
    b, t, _ = h.shape
    gq, gk, gv, glr, gg, nq, nkv, ngate = split_cols(h @ w_in, L1_SIZES)
    log_a = jax.nn.log_sigmoid((glr @ w_gk2 + b_gk).astype(jnp.float32)) / GLA_GATE_NORM
    o = gla_chunked(gq.reshape(b, t, GLA_HEADS, GLA_DK), gk.reshape(b, t, GLA_HEADS, GLA_DK),
                    gv.reshape(b, t, GLA_HEADS, GLA_DV), log_a.reshape(b, t, GLA_HEADS, GLA_DK))
    o = rmsnorm(o, gla_norm_g) * jax.nn.silu(gg.astype(jnp.float32).reshape(b, t, GLA_HEADS, GLA_DV))
    o_gla = o.reshape(b, t, GLA_HEADS * GLA_DV).astype(h.dtype)
    o_nsa = nsa_attention(nq, nkv, ngate, cmp_pos, cmp_k_w1, cmp_k_w2, cmp_v_w1, cmp_v_w2).astype(h.dtype)
    return jnp.concatenate([o_gla, o_nsa], axis=-1) @ w_out

def swiglu(h, w_gate, w_up, w_down):
    return (jax.nn.silu(h @ w_gate) * (h @ w_up)) @ w_down

def adaln_modulation(c, w, b):
    mod = jax.nn.silu(c) @ w + b
    return [m[:, None, :] for m in jnp.split(mod, N_MOD, axis=-1)]

def first_inputs(seed: int = 0) -> dict:
    key = jax.random.key(seed)
    keys = jax.random.split(key, 64)
    counter = [0]
    f32 = jnp.float32
    D = D_MODEL

    def nk():
        counter[0] += 1
        return keys[counter[0] - 1]

    def nrm(shape, fan_in):
        return jax.random.normal(nk(), shape, f32) * (fan_in ** -0.5)

    def gain(n):
        return 1.0 + 0.05 * jax.random.normal(nk(), (n,), f32)

    def small(shape):
        return 0.01 * jax.random.normal(nk(), shape, f32)

    x = jax.random.normal(nk(), (BATCH, SEQ, D), f32)
    c = jax.random.normal(nk(), (BATCH, D), f32)
    offset = jax.random.randint(nk(), (BATCH, 1), 0, 1024, jnp.int32)
    positions = (offset + jnp.arange(SEQ, dtype=jnp.int32)[None, :]).astype(jnp.int32)
    dt0 = jnp.exp(jax.random.uniform(nk(), (SSD_HEADS,), f32) * (math.log(0.1) - math.log(0.001)) + math.log(0.001))
    dt_bias = dt0 + jnp.log(-jnp.expm1(-dt0))
    a_log = jnp.log(jax.random.uniform(nk(), (SSD_HEADS,), f32, minval=1.0, maxval=16.0))
    return {
        'x': x, 'c': c, 'positions': positions,
        'l0_ada_w': nrm((D, N_MOD * D), D), 'l0_ada_b': small((N_MOD * D,)),
        'l0_mix_pre_g': gain(D), 'l0_mix_post_g': gain(D),
        'l0_w_in': nrm((D, L0_IN), D),
        'l0_conv_w': nrm((SSD_CONV, SSD_CONV_CH), SSD_CONV), 'l0_conv_b': small((SSD_CONV_CH,)),
        'l0_dt_bias': dt_bias, 'l0_a_log': a_log,
        'l0_d_skip': 1.0 + 0.1 * jax.random.normal(nk(), (SSD_HEADS,), f32),
        'l0_ssm_norm_g': gain(SSD_INNER),
        'l0_q_a_norm_g': gain(MLA_Q_RANK),
        'l0_w_q_b': nrm((MLA_Q_RANK, MLA_HEADS * (MLA_NOPE + MLA_ROPE)), MLA_Q_RANK),
        'l0_kv_a_norm_g': gain(MLA_KV_RANK),
        'l0_w_kv_b': nrm((MLA_KV_RANK, MLA_HEADS * (MLA_NOPE + MLA_V)), MLA_KV_RANK),
        'l0_w_out': nrm((L0_CAT, D), L0_CAT),
        'l0_ffn_pre_g': gain(D), 'l0_ffn_post_g': gain(D),
        'l0_w_gate': nrm((D, FFN_HIDDEN), D), 'l0_w_up': nrm((D, FFN_HIDDEN), D),
        'l0_w_down': nrm((FFN_HIDDEN, D), FFN_HIDDEN),
        'l1_ada_w': nrm((D, N_MOD * D), D), 'l1_ada_b': small((N_MOD * D,)),
        'l1_mix_pre_g': gain(D), 'l1_mix_post_g': gain(D),
        'l1_w_in': nrm((D, L1_IN), D),
        'l1_w_gk2': nrm((GLA_GATE_RANK, GLA_HEADS * GLA_DK), GLA_GATE_RANK),
        'l1_b_gk': small((GLA_HEADS * GLA_DK,)),
        'l1_gla_norm_g': gain(GLA_DV),
        'l1_cmp_pos': 0.1 * jax.random.normal(nk(), (NSA_CMP_BLOCK, NSA_HEAD_DIM), f32),
        'l1_cmp_k_w1': nrm((NSA_CMP_BLOCK * NSA_HEAD_DIM, NSA_CMP_HIDDEN), NSA_CMP_BLOCK * NSA_HEAD_DIM),
        'l1_cmp_k_w2': nrm((NSA_CMP_HIDDEN, NSA_HEAD_DIM), NSA_CMP_HIDDEN),
        'l1_cmp_v_w1': nrm((NSA_CMP_BLOCK * NSA_HEAD_DIM, NSA_CMP_HIDDEN), NSA_CMP_BLOCK * NSA_HEAD_DIM),
        'l1_cmp_v_w2': nrm((NSA_CMP_HIDDEN, NSA_HEAD_DIM), NSA_CMP_HIDDEN),
        'l1_w_out': nrm((L1_CAT, D), L1_CAT),
        'l1_ffn_pre_g': gain(D), 'l1_ffn_post_g': gain(D),
        'l1_w_gate': nrm((D, FFN_HIDDEN), D), 'l1_w_up': nrm((D, FFN_HIDDEN), D),
        'l1_w_down': nrm((FFN_HIDDEN, D), FFN_HIDDEN),
    }

def first_block(x, c, positions,
              l0_ada_w, l0_ada_b, l0_mix_pre_g, l0_mix_post_g, l0_w_in, l0_conv_w, l0_conv_b,
              l0_dt_bias, l0_a_log, l0_d_skip, l0_ssm_norm_g, l0_q_a_norm_g, l0_w_q_b,
              l0_kv_a_norm_g, l0_w_kv_b, l0_w_out, l0_ffn_pre_g, l0_ffn_post_g,
              l0_w_gate, l0_w_up, l0_w_down,
              l1_ada_w, l1_ada_b, l1_mix_pre_g, l1_mix_post_g, l1_w_in, l1_w_gk2, l1_b_gk,
              l1_gla_norm_g, l1_cmp_pos, l1_cmp_k_w1, l1_cmp_k_w2, l1_cmp_v_w1, l1_cmp_v_w2,
              l1_w_out, l1_ffn_pre_g, l1_ffn_post_g, l1_w_gate, l1_w_up, l1_w_down):
    ada = ((l0_ada_w, l0_ada_b), (l1_ada_w, l1_ada_b))
    norms = ((l0_mix_pre_g, l0_mix_post_g, l0_ffn_pre_g, l0_ffn_post_g),
             (l1_mix_pre_g, l1_mix_post_g, l1_ffn_pre_g, l1_ffn_post_g))
    ffns = ((l0_w_gate, l0_w_up, l0_w_down), (l1_w_gate, l1_w_up, l1_w_down))
    mixers = (
        lambda h: mixer_ssd_mla(h, positions, l0_w_in, l0_conv_w, l0_conv_b, l0_dt_bias, l0_a_log,
                                l0_d_skip, l0_ssm_norm_g, l0_q_a_norm_g, l0_w_q_b, l0_kv_a_norm_g,
                                l0_w_kv_b, l0_w_out),
        lambda h: mixer_gla_nsa(h, l1_w_in, l1_w_gk2, l1_b_gk, l1_gla_norm_g, l1_cmp_pos,
                                l1_cmp_k_w1, l1_cmp_k_w2, l1_cmp_v_w1, l1_cmp_v_w2, l1_w_out),
    )
    for layer in range(DEPTH):
        shift_m, scale_m, gate_m, shift_f, scale_f, gate_f = adaln_modulation(c, *ada[layer])
        pre_m, post_m, pre_f, post_f = norms[layer]
        h = rmsnorm(x, pre_m) * (1.0 + scale_m) + shift_m
        x = x + gate_m * rmsnorm(mixers[layer](h), post_m)
        h = rmsnorm(x, pre_f) * (1.0 + scale_f) + shift_f
        x = x + gate_f * rmsnorm(swiglu(h, *ffns[layer]), post_f)
    return x


DEPTH_2 = 1

HEAD_DIM = 64
HEADS_PER_GROUP = 4
ATTN_PAIRS = ((128, 1), (512, 4), (2048, 16))
N_GROUPS = 3
N_ATTN_HEADS = N_GROUPS * HEADS_PER_GROUP
ATTN_WIDTH = N_ATTN_HEADS * HEAD_DIM
ATTN_OUT_WIDTH = HEADS_PER_GROUP * HEAD_DIM
ATTN_BLOCK = 128
ALIBI_MAX_EXP = 8.0
CONF_WIDTH = 768
CONF_KERNEL = 31
SC_WIDTH = 768
SC_KERNEL = 3
N_BRANCHES = 3
D_FF = 2816
FFN_KERNEL = 3
IN_WIDTHS = (ATTN_WIDTH, ATTN_WIDTH, ATTN_WIDTH, CONF_WIDTH, CONF_WIDTH, SC_WIDTH, SC_WIDTH, SC_WIDTH, N_BRANCHES * D_MODEL)
IN_WIDTH = 3 * ATTN_WIDTH + 2 * CONF_WIDTH + 3 * SC_WIDTH + N_BRANCHES * D_MODEL


def rms_norm(x, g):
    xf = x.astype(jnp.float32)
    y = xf * lax.rsqrt(jnp.mean(xf * xf, axis=-1, keepdims=True) + NORM_EPS)
    return (y * g.astype(jnp.float32)).astype(x.dtype)

def layer_norm(x, g, b):
    xf = x.astype(jnp.float32)
    mu = jnp.mean(xf, axis=-1, keepdims=True)
    xc = xf - mu
    y = xc * lax.rsqrt(jnp.mean(xc * xc, axis=-1, keepdims=True) + NORM_EPS)
    return (y * g.astype(jnp.float32) + b.astype(jnp.float32)).astype(x.dtype)

def causal_dwconv(x, w):
    K, C = w.shape
    return lax.conv_general_dilated(
        x, w[:, None, :].astype(x.dtype), window_strides=(1,), padding=[(K - 1, 0)],
        dimension_numbers=('NWC', 'WIO', 'NWC'), feature_group_count=C)

def dilated_window_attention(q, k, v, window, dilation, slopes):
    B, S, H, hd = q.shape
    L = S // dilation
    span = window // dilation
    nb = -(-L // ATTN_BLOCK)
    Lp = nb * ATTN_BLOCK

    def to_sub(t):
        return t.reshape(B, L, dilation, H, hd).transpose(0, 2, 3, 1, 4)

    qb = jnp.pad(to_sub(q), ((0, 0), (0, 0), (0, 0), (0, Lp - L), (0, 0)))
    qb = qb.reshape(B, dilation, H, nb, ATTN_BLOCK, hd)

    def key_windows(t):
        tp = jnp.pad(to_sub(t), ((0, 0), (0, 0), (0, 0), (ATTN_BLOCK, Lp - L), (0, 0)))
        tp = tp.reshape(B, dilation, H, nb + 1, ATTN_BLOCK, hd)
        return jnp.concatenate([tp[:, :, :, :-1], tp[:, :, :, 1:]], axis=4)

    kw = key_windows(k)
    vw = key_windows(v)
    s = jnp.einsum('brhnqd,brhnkd->brhnqk', qb, kw, preferred_element_type=jnp.float32)
    s = s * (hd ** -0.5)
    qi = jnp.arange(ATTN_BLOCK)[:, None]
    ki = jnp.arange(2 * ATTN_BLOCK)[None, :]
    steps = qi + ATTN_BLOCK - ki
    blk = jnp.arange(nb)[:, None, None]
    valid = (steps >= 0) & (steps <= span) & (blk * ATTN_BLOCK + ki - ATTN_BLOCK >= 0)
    dist = (steps * dilation).astype(jnp.float32)
    s = s - slopes.astype(jnp.float32)[None, None, :, None, None, None] * dist
    s = jnp.where(valid, s, -jnp.inf)
    m = jnp.max(s, axis=-1, keepdims=True)
    p = jnp.exp(s - m)
    l = jnp.sum(p, axis=-1, keepdims=True)
    o = jnp.einsum('brhnqk,brhnkd->brhnqd', p, vw.astype(jnp.float32)) / l
    lse = (m + jnp.log(l))[..., 0]

    def from_sub(t):
        t = t.reshape((B, dilation, H, Lp) + t.shape[5:])[:, :, :, :L]
        t = jnp.moveaxis(t, 3, 1)
        return t.reshape((B, S, H) + t.shape[4:])

    return from_sub(o), from_sub(lse)

def hybrid_layer(x, norm1_g, w_in, conf_dw_w, conf_dw_b, conf_ln_g, conf_ln_b, w_conf_out,
                 sc_dw_w, w_sc_out, w_attn_out, w_o, norm2_g, w_up, ffn_dw_w, w_down):
    B, S, D = x.shape
    h = rms_norm(x, norm1_g)
    u = h @ w_in
    split_points = [int(c) for c in np.cumsum(IN_WIDTHS)[:-1]]
    q, k, v, conf_a, conf_gate, sc_b, sc_c, sc_x, gates = jnp.split(u, split_points, axis=-1)

    q = q.reshape(B, S, N_GROUPS, HEADS_PER_GROUP, HEAD_DIM)
    k = k.reshape(B, S, N_GROUPS, HEADS_PER_GROUP, HEAD_DIM)
    v = v.reshape(B, S, N_GROUPS, HEADS_PER_GROUP, HEAD_DIM)
    slopes = jnp.exp2(-ALIBI_MAX_EXP * jnp.arange(1, N_ATTN_HEADS + 1, dtype=jnp.float32) / N_ATTN_HEADS)
    slopes = slopes.reshape(N_GROUPS, HEADS_PER_GROUP)
    outs, lses = [], []
    for gi, (window, dilation) in enumerate(ATTN_PAIRS):
        o_g, lse_g = dilated_window_attention(q[:, :, gi], k[:, :, gi], v[:, :, gi], window, dilation, slopes[gi])
        outs.append(o_g)
        lses.append(lse_g)
    wts = jax.nn.softmax(jnp.stack(lses, axis=0), axis=0)
    o = jnp.sum(wts[..., None] * jnp.stack(outs, axis=0), axis=0)
    attn = o.reshape(B, S, ATTN_OUT_WIDTH).astype(x.dtype) @ w_attn_out

    a = conf_a * jax.nn.sigmoid(conf_gate)
    a = causal_dwconv(a, conf_dw_w) + conf_dw_b
    a = jax.nn.silu(layer_norm(a, conf_ln_g, conf_ln_b))
    conf = a @ w_conf_out

    short = (sc_b * causal_dwconv(sc_c * sc_x, sc_dw_w)) @ w_sc_out

    g = jax.nn.sigmoid(gates.reshape(B, S, N_BRANCHES, D))
    mixed = g[:, :, 0] * attn + g[:, :, 1] * conf + g[:, :, 2] * short
    x = x + mixed @ w_o

    h = rms_norm(x, norm2_g)
    up = causal_dwconv(h @ w_up, ffn_dw_w)
    f_gate, f_val = jnp.split(up, 2, axis=-1)
    return x + (jax.nn.silu(f_gate) * f_val) @ w_down

def second_inputs(seed: int = 0) -> dict:
    key = jax.random.key(seed)
    ks = jax.random.split(key, 20)
    f32 = jnp.float32

    def dense(k_, shape, fan_in):
        return jax.random.normal(k_, shape, f32) * (fan_in ** -0.5)

    def gain(k_, shape):
        return 1.0 + 0.01 * jax.random.normal(k_, shape, f32)

    return {
        'x': jax.random.normal(ks[0], (BATCH, SEQ, D_MODEL), f32),
        'norm1_g': gain(ks[1], (DEPTH_2, D_MODEL)),
        'w_in': dense(ks[2], (DEPTH_2, D_MODEL, IN_WIDTH), D_MODEL),
        'conf_dw_w': dense(ks[3], (DEPTH_2, CONF_KERNEL, CONF_WIDTH), CONF_KERNEL),
        'conf_dw_b': 0.01 * jax.random.normal(ks[4], (DEPTH_2, CONF_WIDTH), f32),
        'conf_ln_g': gain(ks[5], (DEPTH_2, CONF_WIDTH)),
        'conf_ln_b': 0.01 * jax.random.normal(ks[6], (DEPTH_2, CONF_WIDTH), f32),
        'w_conf_out': dense(ks[7], (DEPTH_2, CONF_WIDTH, D_MODEL), CONF_WIDTH),
        'sc_dw_w': dense(ks[8], (DEPTH_2, SC_KERNEL, SC_WIDTH), SC_KERNEL),
        'w_sc_out': dense(ks[9], (DEPTH_2, SC_WIDTH, D_MODEL), SC_WIDTH),
        'w_attn_out': dense(ks[10], (DEPTH_2, ATTN_OUT_WIDTH, D_MODEL), ATTN_OUT_WIDTH),
        'w_o': dense(ks[11], (DEPTH_2, D_MODEL, D_MODEL), D_MODEL),
        'norm2_g': gain(ks[12], (DEPTH_2, D_MODEL)),
        'w_up': dense(ks[13], (DEPTH_2, D_MODEL, 2 * D_FF), D_MODEL),
        'ffn_dw_w': dense(ks[14], (DEPTH_2, FFN_KERNEL, 2 * D_FF), FFN_KERNEL),
        'w_down': dense(ks[15], (DEPTH_2, D_FF, D_MODEL), D_FF),
        'final_g': gain(ks[16], (D_MODEL,)),
    }

def second_block(x, norm1_g, w_in, conf_dw_w, conf_dw_b, conf_ln_g, conf_ln_b, w_conf_out,
              sc_dw_w, w_sc_out, w_attn_out, w_o, norm2_g, w_up, ffn_dw_w, w_down, final_g):
    for layer in range(DEPTH_2):
        x = hybrid_layer(x, norm1_g[layer], w_in[layer], conf_dw_w[layer], conf_dw_b[layer],
                         conf_ln_g[layer], conf_ln_b[layer], w_conf_out[layer], sc_dw_w[layer],
                         w_sc_out[layer], w_attn_out[layer], w_o[layer], norm2_g[layer], w_up[layer],
                         ffn_dw_w[layer], w_down[layer])
    return rms_norm(x, final_g)


_first_inputs = second_inputs


def second_inputs(seed=0):
    import zlib

    import numpy as np

    out = dict(_first_inputs(seed))
    spreads = {}
    factors = {'norm1_g': 5.414,
     'conf_dw_b': 64.0,
     'conf_ln_g': 64.0,
     'conf_ln_b': 64.0,
     'norm2_g': 64.0,
     'final_g': 32.639}
    for name, (base, spread) in spreads.items():
        noise = np.random.default_rng([zlib.crc32(name.encode()), seed]).standard_normal(out[name].shape)
        drawn = base * np.exp(spread * noise) if base else spread * noise
        out[name] = __import__('jax').numpy.asarray(drawn.astype(out[name].dtype))
    for name, factor in factors.items():
        out[name] = (out[name] * factor).astype(out[name].dtype)
    return out


_narrow_inputs = second_inputs


def second_inputs(seed=0):

    out = dict(_narrow_inputs(seed))
    wider = {'conf_ln_g': 12.0, 'conf_ln_b': 12.0, 'norm2_g': 4.6, 'final_g': 6.43}
    for name, times in wider.items():
        mean = out[name].mean()
        out[name] = (mean + times * (out[name] - mean)).astype(out[name].dtype)
    return out


DEPTH_3 = 1

CHUNK = 64
RWKV_HEADS = 8
RWKV_HEAD_DIM = 64
RWKV_WIDTH = RWKV_HEADS * RWKV_HEAD_DIM
DECAY_LORA = 64
ICLR_LORA = 64
GATE_LORA = 128
GDN_HEADS = 4
GDN_HEAD_DIM = 128
GDN_WIDTH = GDN_HEADS * GDN_HEAD_DIM
GDN_CONV = 4
FFN_HIDDEN_3 = 2816
FFN_CONV = 3
L2_EPS = 1e-6
RWKV_GN_EPS = 64e-5

RWKV_SHIFT_WIDTH = 3 * RWKV_WIDTH + DECAY_LORA + ICLR_LORA + GATE_LORA
IN_SPLITS = (RWKV_SHIFT_WIDTH, 3 * GDN_WIDTH, GDN_WIDTH, GDN_HEADS, GDN_HEADS, D_MODEL, D_MODEL)
IN_WIDTH_3 = RWKV_SHIFT_WIDTH + 4 * GDN_WIDTH + 2 * GDN_HEADS + 2 * D_MODEL


def _split(t, sizes):
    cuts = [int(c) for c in np.cumsum(sizes)[:-1]]
    return jnp.split(t, cuts, axis=-1)

def rms_norm_3(t, gain, eps=NORM_EPS):
    tf = t.astype(jnp.float32)
    y = tf * lax.rsqrt(jnp.mean(tf * tf, axis=-1, keepdims=True) + eps)
    return (y * gain.astype(jnp.float32)).astype(t.dtype)

def l2norm(t):
    tf = t.astype(jnp.float32)
    return (tf * lax.rsqrt(jnp.sum(tf * tf, axis=-1, keepdims=True) + L2_EPS)).astype(t.dtype)

def causal_depthwise_conv_3(t, w):
    width = w.shape[0]
    T = t.shape[1]
    tp = jnp.pad(t, ((0, 0), (width - 1, 0), (0, 0)))
    out = tp[:, 0:T] * w[0]
    for i in range(1, width):
        out = out + tp[:, i:i + T] * w[i]
    return out

def token_shift(t):
    return jnp.pad(t, ((0, 0), (1, 0), (0, 0)))[:, :-1]

def group_norm_heads(y, w, b):
    yf = y.astype(jnp.float32)
    mean = jnp.mean(yf, axis=-1, keepdims=True)
    var = jnp.mean(jnp.square(yf - mean), axis=-1, keepdims=True)
    yn = (yf - mean) * lax.rsqrt(var + RWKV_GN_EPS)
    H, D = y.shape[-2], y.shape[-1]
    return (yn * w.reshape(H, D) + b.reshape(H, D)).astype(y.dtype)

def wkv7_scan(r, w, k, v, a, b):
    dtype = r.dtype
    B, T, H, D = r.shape
    xs = tuple(jnp.moveaxis(t.astype(jnp.float32), 1, 0) for t in (r, w, k, v, a, b))

    def step(S, inp):
        r_t, w_t, k_t, v_t, a_t, b_t = inp
        sa = jnp.einsum('bhvk,bhk->bhv', S, a_t)
        S = S * w_t[:, :, None, :] + sa[..., None] * b_t[:, :, None, :] + v_t[..., None] * k_t[:, :, None, :]
        y = jnp.einsum('bhvk,bhk->bhv', S, r_t)
        return S, y

    S0 = jnp.zeros((B, H, D, D), jnp.float32)
    _, y = lax.scan(step, S0, xs)
    return jnp.moveaxis(y, 0, 1).astype(dtype)

def rwkv7_mix(p, mu, w0, w2, a0, a2, g2, k_k, k_a, r_k, ln_w, ln_b):
    B, T, _ = p.shape
    p = p + (token_shift(p) - p) * mu
    r, k, v, wl, al, gl = _split(p, (RWKV_WIDTH, RWKV_WIDTH, RWKV_WIDTH, DECAY_LORA, ICLR_LORA, GATE_LORA))
    w_log = -jax.nn.softplus(-(w0 + jnp.tanh(wl) @ w2)) - 0.5
    a = jax.nn.sigmoid(a0 + al @ a2)
    g = jax.nn.sigmoid(gl) @ g2

    def heads(t):
        return t.reshape(B, T, RWKV_HEADS, RWKV_HEAD_DIM)

    kk = l2norm(heads(k * k_k))
    k = k * (1 + (a - 1) * k_a)
    r_h, k_h, v_h, a_h = heads(r), heads(k), heads(v), heads(a)
    decay = jnp.exp(-jnp.exp(heads(w_log).astype(jnp.float32)))
    y = wkv7_scan(r_h, decay, k_h, v_h, -kk, kk * a_h)
    y = group_norm_heads(y, ln_w, ln_b)
    y = y + jnp.sum(r_h * k_h * r_k, axis=-1, keepdims=True) * v_h
    return y.reshape(B, T, RWKV_WIDTH) * g

def chunk_gated_delta_rule(q, k, v, g, beta):
    dtype = v.dtype
    B, T, H, Dk = q.shape
    Dv = v.shape[-1]
    N = T // CHUNK

    def to_chunks(t):
        t = t.astype(jnp.float32).reshape((B, N, CHUNK, H) + t.shape[3:])
        return jnp.moveaxis(t, 3, 1)

    q = to_chunks(q) * (Dk ** -0.5)
    k, v, g, beta = to_chunks(k), to_chunks(v), to_chunks(g), to_chunks(beta)
    gc = jnp.cumsum(g, axis=-1)
    causal = jnp.tril(jnp.ones((CHUNK, CHUNK), bool))
    strict = jnp.tril(jnp.ones((CHUNK, CHUNK), bool), -1)
    diff = gc[..., :, None] - gc[..., None, :]
    decay = jnp.where(causal, jnp.exp(jnp.where(causal, diff, 0.0)), 0.0)
    k_beta = k * beta[..., None]
    v_beta = v * beta[..., None]
    Lmat = jnp.where(strict, jnp.einsum('bhncd,bhnsd->bhncs', k_beta, k) * decay, 0.0)
    eye = jnp.eye(CHUNK, dtype=jnp.float32)
    Tinv = lax.linalg.triangular_solve(Lmat + eye, jnp.broadcast_to(eye, Lmat.shape),
                                       left_side=True, lower=True, unit_diagonal=True)
    u = jnp.einsum('bhncs,bhnsd->bhncd', Tinv, v_beta)
    wk = jnp.einsum('bhncs,bhnsd->bhncd', Tinv, k_beta * jnp.exp(gc)[..., None])
    attn = jnp.where(causal, jnp.einsum('bhncd,bhnsd->bhncs', q, k) * decay, 0.0)
    q_dec = q * jnp.exp(gc)[..., None]
    g_last = gc[..., -1]
    k_dec = k * jnp.exp(g_last[..., None] - gc)[..., None]
    xs = (jnp.moveaxis(q_dec, 2, 0), jnp.moveaxis(wk, 2, 0), jnp.moveaxis(u, 2, 0),
          jnp.moveaxis(attn, 2, 0), jnp.moveaxis(k_dec, 2, 0), jnp.moveaxis(g_last, 2, 0))

    def step(S, inp):
        q_n, w_n, u_n, attn_n, k_n, gl_n = inp
        v_new = u_n - jnp.einsum('bhcd,bhde->bhce', w_n, S)
        o = jnp.einsum('bhcd,bhde->bhce', q_n, S) + jnp.einsum('bhcs,bhse->bhce', attn_n, v_new)
        S = S * jnp.exp(gl_n)[..., None, None] + jnp.einsum('bhcd,bhce->bhde', k_n, v_new)
        return S, o

    S0 = jnp.zeros((B, H, Dk, Dv), jnp.float32)
    _, o = lax.scan(step, S0, xs)
    o = jnp.transpose(o, (1, 0, 3, 2, 4)).reshape(B, T, H, Dv)
    return o.astype(dtype)

def gated_deltanet_mix(qkv, z, a_raw, b_raw, conv_w, a_log, dt_bias, norm_w):
    B, T, _ = qkv.shape
    qkv = jax.nn.silu(causal_depthwise_conv_3(qkv, conv_w))
    q, k, v = _split(qkv, (GDN_WIDTH, GDN_WIDTH, GDN_WIDTH))
    q = l2norm(q.reshape(B, T, GDN_HEADS, GDN_HEAD_DIM))
    k = l2norm(k.reshape(B, T, GDN_HEADS, GDN_HEAD_DIM))
    v = v.reshape(B, T, GDN_HEADS, GDN_HEAD_DIM)
    beta = jax.nn.sigmoid(b_raw)
    g = -jnp.exp(a_log.astype(jnp.float32)) * jax.nn.softplus(a_raw.astype(jnp.float32) + dt_bias.astype(jnp.float32))
    o = chunk_gated_delta_rule(q, k, v, g, beta)
    o = rms_norm_3(o, norm_w) * jax.nn.silu(z.reshape(B, T, GDN_HEADS, GDN_HEAD_DIM))
    return o.reshape(B, T, GDN_WIDTH)

def third_inputs(seed: int = 0) -> dict:
    key = jax.random.key(seed)
    ks = jax.random.split(key, 32)
    L = DEPTH_3

    def nrm(k, shape, scale):
        return jax.random.normal(k, shape, jnp.float32) * scale

    dt = jnp.exp(jax.random.uniform(ks[17], (L, GDN_HEADS), minval=float(np.log(1e-3)), maxval=float(np.log(1e-1))))
    return {
        'x': nrm(ks[0], (BATCH, SEQ, D_MODEL), 1.0),
        'norm1_g': 1.0 + nrm(ks[1], (L, D_MODEL), 0.02),
        'w_in': nrm(ks[2], (L, D_MODEL, IN_WIDTH_3), D_MODEL ** -0.5),
        'rwkv_mu': jax.random.uniform(ks[3], (L, RWKV_SHIFT_WIDTH)),
        'rwkv_w0': jax.random.uniform(ks[4], (L, RWKV_WIDTH), minval=-6.5, maxval=-1.0),
        'rwkv_w2': nrm(ks[5], (L, DECAY_LORA, RWKV_WIDTH), 0.5 * DECAY_LORA ** -0.5),
        'rwkv_a0': nrm(ks[6], (L, RWKV_WIDTH), 0.1),
        'rwkv_a2': nrm(ks[7], (L, ICLR_LORA, RWKV_WIDTH), 0.5 * ICLR_LORA ** -0.5),
        'rwkv_g2': nrm(ks[8], (L, GATE_LORA, RWKV_WIDTH), GATE_LORA ** -0.5),
        'rwkv_k_k': 0.85 + nrm(ks[9], (L, RWKV_WIDTH), 0.05),
        'rwkv_k_a': 1.0 + nrm(ks[10], (L, RWKV_WIDTH), 0.05),
        'rwkv_r_k': nrm(ks[11], (L, RWKV_HEADS, RWKV_HEAD_DIM), 0.1),
        'rwkv_ln_w': 1.0 + nrm(ks[12], (L, RWKV_WIDTH), 0.02),
        'rwkv_ln_b': nrm(ks[13], (L, RWKV_WIDTH), 0.02),
        'rwkv_proj': nrm(ks[14], (L, RWKV_WIDTH, D_MODEL), RWKV_WIDTH ** -0.5),
        'gdn_conv_w': nrm(ks[15], (L, GDN_CONV, 3 * GDN_WIDTH), GDN_CONV ** -0.5),
        'gdn_a_log': jnp.log(jax.random.uniform(ks[16], (L, GDN_HEADS), minval=1.0, maxval=16.0)),
        'gdn_dt_bias': dt + jnp.log(-jnp.expm1(-dt)),
        'gdn_norm_w': 1.0 + nrm(ks[18], (L, GDN_HEAD_DIM), 0.02),
        'gdn_proj': nrm(ks[19], (L, GDN_WIDTH, D_MODEL), GDN_WIDTH ** -0.5),
        'w_out': nrm(ks[20], (L, D_MODEL, D_MODEL), D_MODEL ** -0.5),
        'norm2_g': 1.0 + nrm(ks[21], (L, D_MODEL), 0.02),
        'ffn_up': nrm(ks[22], (L, D_MODEL, 2 * FFN_HIDDEN_3), D_MODEL ** -0.5),
        'ffn_conv_w': nrm(ks[23], (L, FFN_CONV, 2 * FFN_HIDDEN_3), FFN_CONV ** -0.5),
        'ffn_down': nrm(ks[24], (L, FFN_HIDDEN_3, D_MODEL), FFN_HIDDEN_3 ** -0.5),
        'final_g': 1.0 + nrm(ks[25], (D_MODEL,), 0.02),
    }

def third_block(x, norm1_g, w_in, rwkv_mu, rwkv_w0, rwkv_w2, rwkv_a0, rwkv_a2, rwkv_g2, rwkv_k_k,
              rwkv_k_a, rwkv_r_k, rwkv_ln_w, rwkv_ln_b, rwkv_proj, gdn_conv_w, gdn_a_log, gdn_dt_bias,
              gdn_norm_w, gdn_proj, w_out, norm2_g, ffn_up, ffn_conv_w, ffn_down, final_g):
    for l in range(DEPTH_3):
        u = rms_norm_3(x, norm1_g[l])
        p = u @ w_in[l]
        p_rwkv, qkv, z, a_raw, b_raw, gate_a, gate_b = _split(p, IN_SPLITS)
        y_a = rwkv7_mix(p_rwkv, rwkv_mu[l], rwkv_w0[l], rwkv_w2[l], rwkv_a0[l], rwkv_a2[l], rwkv_g2[l],
                        rwkv_k_k[l], rwkv_k_a[l], rwkv_r_k[l], rwkv_ln_w[l], rwkv_ln_b[l]) @ rwkv_proj[l]
        y_b = gated_deltanet_mix(qkv, z, a_raw, b_raw, gdn_conv_w[l], gdn_a_log[l], gdn_dt_bias[l],
                                 gdn_norm_w[l]) @ gdn_proj[l]
        mixed = jax.nn.sigmoid(gate_a) * y_a + jax.nn.sigmoid(gate_b) * y_b
        x = x + mixed @ w_out[l]
        h = rms_norm_3(x, norm2_g[l]) @ ffn_up[l]
        h = causal_depthwise_conv_3(h, ffn_conv_w[l])
        h_gate, h_up = _split(h, (FFN_HIDDEN_3, FFN_HIDDEN_3))
        x = x + (jax.nn.silu(h_gate) * h_up) @ ffn_down[l]
    return rms_norm_3(x, final_g)


_first_inputs_3 = third_inputs


def third_inputs(seed=0):
    import zlib

    import numpy as np

    out = dict(_first_inputs_3(seed))
    spreads = {}
    factors = {'norm1_g': 3.236,
     'rwkv_w2': 8.0,
     'rwkv_a0': 4.353,
     'rwkv_k_k': 29.672,
     'rwkv_k_a': 3.278,
     'rwkv_ln_w': 64.0,
     'rwkv_ln_b': 64.0,
     'gdn_norm_w': 23.694,
     'norm2_g': 11.733,
     'final_g': 7.832}
    for name, (base, spread) in spreads.items():
        noise = np.random.default_rng([zlib.crc32(name.encode()), seed]).standard_normal(out[name].shape)
        drawn = base * np.exp(spread * noise) if base else spread * noise
        out[name] = __import__('jax').numpy.asarray(drawn.astype(out[name].dtype))
    for name, factor in factors.items():
        out[name] = (out[name] * factor).astype(out[name].dtype)
    return out


_narrow_inputs_3 = third_inputs


def third_inputs(seed=0):

    out = dict(_narrow_inputs_3(seed))
    wider = {'rwkv_k_k': 3.72,
     'rwkv_ln_w': 3.88,
     'rwkv_ln_b': 3.86,
     'gdn_norm_w': 3.13,
     'final_g': 3.15}
    for name, times in wider.items():
        mean = out[name].mean()
        out[name] = (mean + times * (out[name] - mean)).astype(out[name].dtype)
    return out


def setup_inputs(seed=0):
    out = dict(first_inputs(seed))
    for name, value in second_inputs(seed + 1).items():
        if name != "x":
            out[name + "_2"] = value
    for name, value in third_inputs(seed + 2).items():
        if name != "x":
            out[name + "_3"] = value
    return out


def reference(
    x, c, positions, l0_ada_w, l0_ada_b, l0_mix_pre_g, l0_mix_post_g, l0_w_in, l0_conv_w,
    l0_conv_b, l0_dt_bias, l0_a_log, l0_d_skip, l0_ssm_norm_g, l0_q_a_norm_g, l0_w_q_b,
    l0_kv_a_norm_g, l0_w_kv_b, l0_w_out, l0_ffn_pre_g, l0_ffn_post_g, l0_w_gate, l0_w_up,
    l0_w_down, l1_ada_w, l1_ada_b, l1_mix_pre_g, l1_mix_post_g, l1_w_in, l1_w_gk2, l1_b_gk,
    l1_gla_norm_g, l1_cmp_pos, l1_cmp_k_w1, l1_cmp_k_w2, l1_cmp_v_w1, l1_cmp_v_w2, l1_w_out,
    l1_ffn_pre_g, l1_ffn_post_g, l1_w_gate, l1_w_up, l1_w_down, norm1_g_2, w_in_2, conf_dw_w_2,
    conf_dw_b_2, conf_ln_g_2, conf_ln_b_2, w_conf_out_2, sc_dw_w_2, w_sc_out_2, w_attn_out_2,
    w_o_2, norm2_g_2, w_up_2, ffn_dw_w_2, w_down_2, final_g_2, norm1_g_3, w_in_3, rwkv_mu_3,
    rwkv_w0_3, rwkv_w2_3, rwkv_a0_3, rwkv_a2_3, rwkv_g2_3, rwkv_k_k_3, rwkv_k_a_3, rwkv_r_k_3,
    rwkv_ln_w_3, rwkv_ln_b_3, rwkv_proj_3, gdn_conv_w_3, gdn_a_log_3, gdn_dt_bias_3,
    gdn_norm_w_3, gdn_proj_3, w_out_3, norm2_g_3, ffn_up_3, ffn_conv_w_3, ffn_down_3, final_g_3,
):
    x = first_block(
        x, c, positions, l0_ada_w, l0_ada_b, l0_mix_pre_g, l0_mix_post_g, l0_w_in, l0_conv_w,
        l0_conv_b, l0_dt_bias, l0_a_log, l0_d_skip, l0_ssm_norm_g, l0_q_a_norm_g, l0_w_q_b,
        l0_kv_a_norm_g, l0_w_kv_b, l0_w_out, l0_ffn_pre_g, l0_ffn_post_g, l0_w_gate, l0_w_up,
        l0_w_down, l1_ada_w, l1_ada_b, l1_mix_pre_g, l1_mix_post_g, l1_w_in, l1_w_gk2, l1_b_gk,
        l1_gla_norm_g, l1_cmp_pos, l1_cmp_k_w1, l1_cmp_k_w2, l1_cmp_v_w1, l1_cmp_v_w2, l1_w_out,
        l1_ffn_pre_g, l1_ffn_post_g, l1_w_gate, l1_w_up, l1_w_down,
    )
    x = second_block(
        x, norm1_g_2, w_in_2, conf_dw_w_2, conf_dw_b_2, conf_ln_g_2, conf_ln_b_2, w_conf_out_2,
        sc_dw_w_2, w_sc_out_2, w_attn_out_2, w_o_2, norm2_g_2, w_up_2, ffn_dw_w_2, w_down_2,
        final_g_2,
    )
    return third_block(
        x, norm1_g_3, w_in_3, rwkv_mu_3, rwkv_w0_3, rwkv_w2_3, rwkv_a0_3, rwkv_a2_3, rwkv_g2_3,
        rwkv_k_k_3, rwkv_k_a_3, rwkv_r_k_3, rwkv_ln_w_3, rwkv_ln_b_3, rwkv_proj_3, gdn_conv_w_3,
        gdn_a_log_3, gdn_dt_bias_3, gdn_norm_w_3, gdn_proj_3, w_out_3, norm2_g_3, ffn_up_3,
        ffn_conv_w_3, ffn_down_3, final_g_3,
    )


_drawn_inputs = setup_inputs


def setup_inputs(seed=0):
    import zlib

    import numpy as np

    out = dict(_drawn_inputs(seed))
    spreads = {}
    factors = {'l0_q_a_norm_g': 3.103}
    for name, (base, spread) in spreads.items():
        noise = np.random.default_rng([zlib.crc32(name.encode()), seed]).standard_normal(out[name].shape)
        drawn = base * np.exp(spread * noise) if base else spread * noise
        out[name] = jnp.asarray(drawn.astype(out[name].dtype))
    for name, factor in factors.items():
        out[name] = (out[name] * factor).astype(out[name].dtype)
    return out
```

```python
import math
from contextlib import ExitStack, contextmanager

import numpy as np
import concourse.bass as bass
from concourse import mybir

F32 = mybir.dt.float32
F32R = mybir.dt.float32r
I32 = mybir.dt.int32
ALU = mybir.AluOpType
ACT = mybir.ActivationFunctionType
X_AXIS = mybir.AxisListType.X

P = 128
T = 512
NT = T // P
D = 1024
KD = D // P
BANKS = 8
RING = 2
SLAB = 2816
EPS = 1e-6
MASKED = -1e30


class Core:

    def __init__(self, nc, ctx, dram, plan, columns):
        self.nc, self.dram, self.plan, self.columns = nc, dram, plan, columns
        self.used = []
        self.slabs = [(name, s, kt * cols) for name, n, kt, cols, _ in plan for s in range(n)]
        self.linears = 0
        self.first_slab = 0
        self.psum = ctx.enter_context(nc.psum_tensor("banks", [P, BANKS, 512], F32))
        self.ring = ctx.enter_context(nc.sbuf_tensor("weight_ring", [P, RING, SLAB], F32))
        self.slab_loaded = [ctx.enter_context(nc.semaphore(f"slab_loaded{s}")) for s in range(RING)]
        ncol = sum(n for _, n in columns.values())
        self.cols = ctx.enter_context(nc.sbuf_tensor("columns", [P, ncol], F32))
        self.ident = ctx.enter_context(nc.sbuf_tensor("ident", [P, P], F32))
        self.ones = ctx.enter_context(nc.sbuf_tensor("ones", [P, P], F32))

    def bank(self, b):
        return self.psum[:, b, :]

    def col(self, name, i=0):
        return self.cols[:, self.columns[name][0] + i:self.columns[name][0] + i + 1] if isinstance(i, int) \
            else self.cols[:, bass.ds(i + self.columns[name][0], 1)]

    def colblock(self, name):
        a, n = self.columns[name]
        return self.cols[:, a:a + n]

    @contextmanager
    def stage(self, name):
        nc = self.nc
        with ExitStack() as ctx:
            st = Stage(nc, ctx, name)
            st.block = ctx.enter_context(nc.Block())
            old, self.used = self.used, st.semaphores

            @st.block.gpsimd
            def _(pool):
                for handle in old:
                    pool.sem_clear(handle)

            yield st
        for handle in old:
            nc.release_semaphore(handle)

    def load_slab(self, eng, number):
        if number >= len(self.slabs):
            return
        name, s, words = self.slabs[number]
        eng.dma_start(self.ring[:, number % RING, 0:words], self.dram[name][s]
                      ).then_inc(self.slab_loaded[number % RING], 16)


class Stage:
    def __init__(self, nc, ctx, name):
        self.nc, self.ctx, self.name, self.semaphores = nc, ctx, name, []

    def sb(self, name, shape, dtype=F32):
        return self.ctx.enter_context(self.nc.sbuf_tensor(f"{self.name}_{name}", shape, dtype))

    def sem(self, name):
        handle = self.nc.alloc_semaphore(f"{self.name}_{name}")
        self.semaphores.append(handle)
        return handle


class Marks:

    def __init__(self, semaphore):
        self.semaphore, self.count = semaphore, 0

    def mark(self, instruction):
        instruction.then_inc(self.semaphore, 1)
        self.count += 1
        return self.count


def in_turns(eng, count, lead, body):
    turns = (count - 1) // lead - 1
    if turns < 4:
        for i in range(count):
            body(i, i, None)
        return
    for i in range(lead):
        body(i, i, None)
    with eng.Fori(1, turns + 1) as turn:
        for i in range(lead):
            body(turn * lead + i, lead + i, turn)
    for i in range(lead * (turns + 1), count):
        body(i, i, None)


def skewed(n, depth):
    for s in range(n + depth - 1):
        for phase in reversed(range(depth)):
            if 0 <= s - phase < n:
                yield phase, s - phase


def linear(core, name, source, epilogue, by_tokens=False, width=T, raw=False):
    nc = core.nc
    weights, nslab, kt, cols, gcols = core.plan[core.linears]
    assert weights == name, (weights, name)
    first = core.first_slab
    per = NT if by_tokens else cols // gcols
    lead = max(RING * per, 2)
    banks = min(BANKS, lead)
    assert lead % banks == 0
    count = nslab * per
    cut = raw or isinstance(source, Pair)
    unit = per if by_tokens else 1
    units, ucols = count // unit, (cols if by_tokens else gcols)
    assert not cut or lead % (2 * unit) == 0

    def slab_count(at, turn):
        seen = 16 * ((first + at // per) // RING + 1)
        if turn is None:
            return seen
        return (turn - 1) * (16 * (lead // per) // RING) + seen

    with core.stage(name) as st:
        group_done = st.sem("group_done")
        bank_free = st.sem("bank_free")
        high_cut = st.sem("high_cut")
        low_cut = st.sem("low_cut")
        tile_high, tile_low = st.sem("tile_high"), st.sem("tile_low")
        if cut:
            w_high = st.sb("w_high", [P, 2, kt * ucols], F32R)
            w_low = st.sb("w_low", [P, 2, kt * ucols], F32R)
        if raw:
            pair = Pair(st.sb("high", [P, kt, width], F32R), st.sb("low", [P, kt, width], F32R))
        else:
            pair = source

        def slab_columns(at):
            w = core.ring[:, (first + at // per) % RING, 0:kt * cols].rearrange("p (k c) -> p k c", k=kt)
            f = at % per
            return w if by_tokens else w[:, :, f * gcols:(f + 1) * gcols]

        def piece(t, at):
            return t[:, at // unit % 2, :].rearrange("p (k c) -> p k c", k=kt)

        @st.block.sync
        def _(sp):
            def refill(s, at, turn):
                if cut:
                    sp.wait_ge(high_cut, (s + 1) * (per // unit))
                    sp.wait_ge(low_cut, (s + 1) * (per // unit))
                else:
                    sp.wait_ge(group_done, (s + 1) * per)
                if turn is None:
                    core.load_slab(sp, first + at + RING)
                else:
                    slot = (first + at) % RING
                    sp.dma_start(core.ring[:, slot, 0:kt * cols], core.dram[weights][bass.ds(s + RING, 1)]
                                 ).then_inc(core.slab_loaded[slot], 16)

            inside = max(0, nslab - RING)
            in_turns(sp, inside, RING, refill)
            for s in range(inside, nslab):
                refill(s, s, None)

        def cut_high(act, i, at, turn):
            u = i if unit == 1 else i // unit
            act.wait_ge(core.slab_loaded[(first + at // per) % RING], slab_count(at, turn))
            if at >= 2 * unit:
                act.wait_ge(group_done, (u - 1) * unit)
            nc.scalar.activation(piece(w_high, at), slab_columns(at), ACT.Copy).then_inc(high_cut, 1)

        if raw:
            @st.block.scalar
            def _(act):
                for k in range(kt):
                    nc.scalar.activation(pair.high[:, k, :], source(k), ACT.Copy).then_inc(tile_high, 1)

            @st.block.vector
            def _(dve):
                for k in range(kt):
                    dve.wait_ge(tile_high, k + 1)
                    nc.vector.tensor_tensor(pair.low[:, k, :], source(k), pair.high[:, k, :], ALU.subtract
                                            ).then_inc(tile_low, 1)
        if cut:
            @st.block.scalar
            def _(act):
                cut_high(act, 0, 0, None)

            @st.block.gpsimd
            def _(pool):
                def cut_low(i, at, turn):
                    u = i
                    pool.wait_ge(high_cut, u + 1)
                    if at >= 2:
                        pool.wait_ge(group_done, (u - 1) * unit)
                    g = at * unit
                    nc.gpsimd.tensor_tensor(piece(w_low, g), slab_columns(g), piece(w_high, g), ALU.subtract
                                            ).then_inc(low_cut, 1)
                in_turns(pool, units, lead // unit, cut_low)

        @st.block.tensor
        def _(pe):
            def group(i, at, turn):
                f, b = at % per, at % banks
                if at >= banks:
                    pe.wait_ge(bank_free, i - (banks - 1))
                if by_tokens:
                    out = core.psum[:, b, 0:cols]
                    tokens = slice(f * P, (f + 1) * P)
                else:
                    out = core.psum[0:gcols, b, 0:width]
                if not cut:
                    if f == 0:
                        pe.wait_ge(core.slab_loaded[(first + at // per) % RING], slab_count(at, turn))
                    w = slab_columns(at)
                    for k in range(kt):
                        lhs, rhs = (source(k)[:, tokens], w[:, k, :]) if by_tokens else (w[:, k, :], source(k))
                        mm = nc.tensor.matmul(out, lhs, rhs, start=(k == 0), stop=(k == kt - 1))
                    mm.then_inc(group_done, 1)
                    return
                u = i if unit == 1 else i // unit
                starts_unit = at % unit == 0
                if starts_unit:
                    pe.wait_ge(high_cut, u + 1)
                for n, (w, x) in enumerate(((w_high, pair.high), (w_high, pair.low), (w_low, pair.high))):
                    if n == 2 and starts_unit:
                        pe.wait_ge(low_cut, u + 1)
                    w = piece(w, at)
                    for k in range(kt):
                        if raw and at == 0 and n < 2:
                            pe.wait_ge(tile_low if n else tile_high, k + 1)
                        lhs, rhs = (x[:, k, tokens], w[:, k, :]) if by_tokens else (w[:, k, :], x[:, k, :])
                        mm = nc.tensor.matmul(out, lhs, rhs, start=(n == 0 and k == 0), stop=(n == 2 and k == kt - 1))
                mm.then_inc(group_done, 1)

            in_turns(pe, count, lead, group)

        g = Groups(core, count, lead, banks, cols if by_tokens else width, gcols if not by_tokens else P,
                   group_done, bank_free, unit, cut_high if cut else None)
        epilogue(core, st, g)
        if cut and not g.high_cut_run:
            @st.block.scalar
            def _(act):
                g.run_scalar(act, lambda i, at, turn: None)
    core.linears += 1
    core.first_slab += nslab


class Pair:

    def __init__(self, high, low):
        self.high, self.low = high, low


class Groups:

    def __init__(self, core, count, lead, banks, width, rows, done, free, unit, cut_high):
        self.core, self.count, self.lead, self.banks = core, count, lead, banks
        self.width, self.rows, self.done, self.free = width, rows, done, free
        self.unit, self.cut_high, self.high_cut_run = unit, cut_high, False

    def bank(self, at):
        return self.core.psum[0:self.rows, at % self.banks, 0:self.width]

    def run(self, eng, body):
        in_turns(eng, self.count, self.lead, body)

    def run_scalar(self, act, body):
        self.high_cut_run = True

        def step(i, at, turn):
            if self.cut_high and at % self.unit == 0 and (turn is not None or at + self.unit < self.count):
                self.cut_high(act, i + self.unit, at + self.unit, turn)
            body(i, at, turn)
        in_turns(act, self.count, self.lead, step)


def stored(dst, func=ACT.Copy, bias=None):
    def epilogue(core, st, g):
        @st.block.scalar
        def _(act):
            def take(i, at, turn):
                act.wait_ge(g.done, i + 1)
                if bias is None:
                    ins = core.nc.scalar.activation(dst(i, at), g.bank(at), func)
                else:
                    ins = core.nc.scalar.activation(dst(i, at), g.bank(at), func, bias=bias(i))
                ins.then_inc(g.free, 1)
            g.run_scalar(act, take)
    return epilogue


def convolved(taps, weight, bias, dst, mu=False):
    def epilogue(core, st, g):
        nc = core.nc
        pad = taps - 1
        raw = st.sb("raw", [P, 2, pad + T])
        acc = st.sb("acc", [P, 2, T])
        tap_done, conv_done, silu_done, zeroed = (st.sem(n) for n in ("tap_done", "conv_done", "silu_done", "zeroed"))

        @st.block.scalar
        def _(act):
            def take(i, at, turn):
                act.wait_ge(g.done, i + 1)
                if at >= 2:
                    act.wait_ge(conv_done, i - 1)
                nc.scalar.activation(raw[:, at % 2, pad:], g.bank(at), ACT.Copy).then_inc(g.free, 1)
                act.wait_ge(conv_done, i + 1)
                nc.scalar.activation(dst(i, at), acc[:, at % 2, :], ACT.Silu, bias=bias(i)).then_inc(silu_done, 1)
            g.run_scalar(act, take)

        @st.block.vector
        def _(dve):
            nc.vector.memset(raw[:, :, 0:pad], 0.0).then_inc(zeroed, 1)
            dve.wait_ge(zeroed, 1)

            def conv(i, at, turn):
                dve.wait_ge(g.free, i + 1)
                if at >= 2:
                    dve.wait_ge(silu_done, i - 1)
                a = acc[:, at % 2, :]
                for j in range(taps):
                    x = raw[:, at % 2, j:j + T]
                    if j == 0:
                        ins = nc.vector.tensor_scalar(a, x, weight(i, 0), None, ALU.mult)
                    else:
                        dve.wait_ge(tap_done, i * (taps - 1) + j)
                        ins = nc.vector.scalar_tensor_tensor(out=a, in0=x, scalar=weight(i, j), in1=a,
                                                             op0=ALU.mult, op1=ALU.add)
                    ins.then_inc(conv_done if j == taps - 1 else tap_done, 1)
            g.run(dve, conv)
    return epilogue


def added(dst, scale=None):
    def epilogue(core, st, g):
        nc = core.nc
        scaled = st.sem("scaled")

        if scale is not None:
            tmp = st.sb("scaled_group", [P, 2, T])

        @st.block.vector
        def _(dve):
            def take(i, at, turn):
                dve.wait_ge(g.done, i + 1)
                if scale is None:
                    nc.vector.tensor_tensor(dst(i), g.bank(at), dst(i), ALU.add).then_inc(g.free, 1)
                else:
                    nc.vector.tensor_tensor(tmp[:, at % 2, :], g.bank(at), scale(i), ALU.mult).then_inc(g.free, 1)
                    dve.wait_ge(g.free, i + 1)
                    nc.vector.tensor_tensor(dst(i), tmp[:, at % 2, :], dst(i), ALU.add).then_inc(scaled, 1)
            g.run(dve, take)
    return epilogue


def gated(dst, func, taps=0, weight=None):
    def epilogue(core, st, g):
        nc = core.nc
        gate = st.sb("gate", [P, 2, T])
        gate_done, product_done = st.sem("gate_done"), st.sem("product_done")
        high_cut, low_cut = st.sem("result_high_cut"), st.sem("result_low_cut")
        product_ = st.sb("product", [P, 2, T])

        def cut_high(act, h, slot):
            if taps:
                act.wait_ge(product_done, h + 1)
            else:
                act.wait_ge(g.free, 2 * h + 2)
            nc.scalar.activation(row(dst.high, h), product_[:, slot, :], ACT.Copy).then_inc(high_cut, 1)

        def cut_low(dve, h, slot):
            dve.wait_ge(high_cut, h + 1)
            nc.vector.tensor_tensor(row(dst.low, h), product_[:, slot, :], row(dst.high, h), ALU.subtract).then_inc(low_cut, 1)

        if not taps:
            @st.block.scalar
            def _(act):
                def take(i, at, turn):
                    if at % 2 == 0:
                        act.wait_ge(g.done, i + 1)
                        if at >= 4:
                            act.wait_ge(g.free, i - 2)
                        nc.scalar.activation(gate[:, at // 2 % 2, :], g.bank(at), func).then_inc(gate_done, 1)
                        if at >= 2:
                            cut_high(act, half(i, at, turn, g.lead) - 1, (at // 2 + 1) % 2)
                g.run_scalar(act, take)
                cut_high(act, g.count // 2 - 1, (g.count // 2 - 1) % 2)

            @st.block.vector
            def _(dve):
                def take(i, at, turn):
                    if at % 2:
                        h = half(i, at, turn, g.lead)
                        dve.wait_ge(g.done, i + 1)
                        dve.wait_ge(gate_done, h + 1)
                        if at >= 4:
                            dve.wait_ge(low_cut, h - 1)
                        nc.vector.tensor_tensor(product_[:, at // 2 % 2, :], g.bank(at), gate[:, at // 2 % 2, :], ALU.mult
                                                ).then_inc(g.free, 2)
                        if at >= 2:
                            cut_low(dve, h - 1, (at // 2 + 1) % 2)
                g.run(dve, take)
                cut_low(dve, g.count // 2 - 1, (g.count // 2 - 1) % 2)
            return

        pad = taps - 1
        raw = st.sb("raw", [P, 2, pad + T])
        acc = st.sb("acc", [P, 2, T])
        tap_done, conv_done, zeroed = (st.sem(n) for n in ("tap_done", "conv_done", "zeroed"))

        @st.block.scalar
        def _(act):
            def take(i, at, turn):
                act.wait_ge(g.done, i + 1)
                if at >= 2:
                    act.wait_ge(conv_done, i - 1)
                nc.scalar.activation(raw[:, at % 2, pad:], g.bank(at), ACT.Copy).then_inc(g.free, 1)
                if at % 2 == 0:
                    act.wait_ge(conv_done, i + 1)
                    if at >= 4:
                        act.wait_ge(product_done, half(i, at, turn, g.lead) - 1)
                    nc.scalar.activation(gate[:, at // 2 % 2, :], acc[:, 0, :], func).then_inc(gate_done, 1)
                    if at >= 2:
                        cut_high(act, half(i, at, turn, g.lead) - 1, (at // 2 + 1) % 2)
            g.run_scalar(act, take)
            cut_high(act, g.count // 2 - 1, (g.count // 2 - 1) % 2)

        @st.block.vector
        def _(dve):
            nc.vector.memset(raw[:, :, 0:pad], 0.0).then_inc(zeroed, 1)
            dve.wait_ge(zeroed, 1)

            def conv(i, at, turn):
                h = half(i, at, turn, g.lead)
                dve.wait_ge(g.free, i + 1)
                a = acc[:, at % 2, :]
                if at >= 2:
                    if at % 2 == 0:
                        dve.wait_ge(gate_done, h)
                    else:
                        dve.wait_ge(product_done, h)
                for j in range(taps):
                    x = raw[:, at % 2, j:j + T]
                    if j == 0:
                        ins = nc.vector.tensor_scalar(a, x, weight(i, 0), None, ALU.mult)
                    else:
                        dve.wait_ge(tap_done, i * (taps - 1) + j)
                        ins = nc.vector.scalar_tensor_tensor(out=a, in0=x, scalar=weight(i, j), in1=a,
                                                             op0=ALU.mult, op1=ALU.add)
                    ins.then_inc(conv_done if j == taps - 1 else tap_done, 1)
                if at % 2:
                    dve.wait_ge(gate_done, h + 1)
                    dve.wait_ge(conv_done, i + 1)
                    if at >= 4:
                        dve.wait_ge(low_cut, h - 1)
                    nc.vector.tensor_tensor(product_[:, at // 2 % 2, :], a, gate[:, at // 2 % 2, :], ALU.mult
                                            ).then_inc(product_done, 1)
                    if at >= 2:
                        cut_low(dve, h - 1, (at // 2 + 1) % 2)
            g.run(dve, conv)
            cut_low(dve, g.count // 2 - 1, (g.count // 2 - 1) % 2)
    return epilogue


def half(i, at, turn, lead):
    return at // 2 if turn is None else turn * (lead // 2) + (at - lead) // 2


def norm(core, name, x, sets, stat, out, eps, gain=None, shift=None, times=None, residual=False, center=None,
         last=ACT.Identity, pair=None):
    nc = core.nc
    tiles = [i for s in sets for i in s]
    n = len(tiles)
    where = {i: s for s, ts in enumerate(sets) for i in ts}
    with core.stage(name) as st:
        sq = st.sb("squares", [P, n, T])
        rstd = st.sb("rstd", [P, len(sets), T])
        xc = st.sb("centred", [P, n, T]) if center is not None else None
        squared, summed, logged, inverted, scaled, stored_, shifted, meaned, centred, high_cut, low_cut = (
            st.sem(s) for s in ("squared", "summed", "logged", "inverted", "scaled", "stored", "shifted", "meaned",
                                "centred", "high_cut", "low_cut"))
        src = (lambda i: xc[:, tiles.index(i), :]) if center is not None else x

        @st.block.tensor
        def _(pe):
            if center is not None:
                for s, ts in enumerate(sets):
                    if s >= 4:
                        pe.wait_ge(centred, sum(len(q) for q in sets[:s - 3]))
                    for j, i in enumerate(ts):
                        mm = nc.tensor.matmul(core.bank(4 + s % 4), center, x(i), start=(j == 0), stop=(j == len(ts) - 1))
                    mm.then_inc(meaned, 1)
            m = 0
            for s, ts in enumerate(sets):
                if s >= 4:
                    pe.wait_ge(logged, s - 3)
                for j, i in enumerate(ts):
                    m += 1
                    pe.wait_ge(squared, m)
                    mm = nc.tensor.matmul(core.bank(s % 4), stat, sq[:, m - 1, :], start=(j == 0), stop=(j == len(ts) - 1))
                mm.then_inc(summed, 1)

        @st.block.scalar
        def _(act):
            for m, i in enumerate(tiles):
                if center is not None:
                    act.wait_ge(centred, m + 1)
                nc.scalar.activation(sq[:, m, :], src(i), ACT.Square).then_inc(squared, 1)
            for s in range(len(sets)):
                act.wait_ge(summed, s + 1)
                nc.scalar.activation(rstd[:, s, :], core.bank(s % 4), ACT.Sqrt, bias=eps).then_inc(logged, 1)
            if pair is not None:
                for m, i in enumerate(tiles):
                    act.wait_ge(scaled, m + 1)
                    kw = {} if shift is None else {"bias": shift(i)}
                    nc.scalar.activation(pair.high[:, i, :], sq[:, m, :], ACT.Copy if shift is None else ACT.Identity, **kw
                                         ).then_inc(high_cut, 1)
            elif shift is not None:
                for m, i in enumerate(tiles):
                    act.wait_ge(stored_, m + 1)
                    nc.scalar.activation(out(i), out(i), last, bias=shift(i)).then_inc(shifted, 1)

        @st.block.vector
        def _(dve):
            if center is not None:
                for m, i in enumerate(tiles):
                    dve.wait_ge(meaned, where[i] + 1)
                    nc.vector.tensor_tensor(xc[:, m, :], x(i), core.bank(4 + where[i] % 4), ALU.subtract).then_inc(centred, 1)
            def cut_low(m):
                i = tiles[m]
                dve.wait_ge(high_cut, m + 1)
                if shift is None:
                    ins = nc.vector.tensor_tensor(pair.low[:, i, :], sq[:, m, :], pair.high[:, i, :], ALU.subtract)
                else:
                    ins = nc.vector.scalar_tensor_tensor(out=pair.low[:, i, :], in0=sq[:, m, :], scalar=shift(i),
                                                         in1=pair.high[:, i, :], op0=ALU.add, op1=ALU.subtract)
                ins.then_inc(low_cut, 1)

            last = -1
            for m, i in enumerate(tiles):
                s = where[i]
                if s != last:
                    last = s
                    if center is not None:
                        dve.wait_ge(centred, n)
                    dve.wait_ge(logged, s + 1)
                    nc.vector.reciprocal(rstd[:, s, :], rstd[:, s, :]).then_inc(inverted, 1)
                    dve.wait_ge(inverted, s + 1)
                plain = times is None and not residual and pair is None
                dst = out(i) if plain else sq[:, m, :]
                if not plain:
                    dve.wait_ge(summed, s + 1)
                if gain is None:
                    ins = nc.vector.tensor_tensor(dst, src(i), rstd[:, s, :], ALU.mult)
                else:
                    ins = nc.vector.scalar_tensor_tensor(out=dst, in0=src(i), scalar=gain(i), in1=rstd[:, s, :],
                                                         op0=ALU.mult, op1=ALU.mult)
                ins.then_inc(stored_ if plain else scaled, 1)
                if pair is not None:
                    if m >= 2:
                        cut_low(m - 2)
                elif not plain:
                    dve.wait_ge(scaled, m + 1)
                    nc.vector.tensor_tensor(out(i), sq[:, m, :], out(i) if residual else times(i),
                                            ALU.add if residual else ALU.mult).then_inc(stored_, 1)
            if pair is not None:
                for m in range(max(0, n - 2), n):
                    cut_low(m)


def row(t, i):
    return t[:, i, :]


def turned(core, name, jobs, times=None):
    nc = core.nc
    with core.stage(name) as st:
        turned_, copied = st.sem("turned"), st.sem("copied")

        @st.block.tensor
        def _(pe):
            for i, (sources, _) in enumerate(jobs):
                if i >= BANKS:
                    pe.wait_ge(copied, i - BANKS + 1)
                for j, src in enumerate(sources):
                    mm = nc.tensor.transpose(core.psum[:, i % BANKS, j * P:(j + 1) * P], src, core.ident[:])
                mm.then_inc(turned_, 1)

        @st.block.scalar
        def _(act):
            for i, (sources, out) in enumerate(jobs):
                act.wait_ge(turned_, i + 1)
                nc.scalar.activation(out, core.psum[:, i % BANKS, 0:len(sources) * P], ACT.Copy).then_inc(copied, 1)


class Keys:

    def __init__(self, q, k, v, n, bias, scale, slope=1.0, gate=None, valid=None):
        self.q, self.k, self.v, self.n, self.bias = q, k, v, n, bias
        self.scale, self.slope, self.gate, self.valid = scale, slope, gate, valid
        self.blocks = -(-n // P)


def attention(core, name, units, dv=64, joint=False):
    nc = core.nc
    ns = len(units[0][0])
    n_units = len(units)
    masked_sets = [j for j in range(ns) if units[0][0][j].valid is not None]
    nm = len(masked_sets)
    sloped = any(s.slope != 1.0 for s in units[0][0])
    with core.stage(name) as st:
        probs = st.sb("probs", [P, 2, ns, 512])
        turned_p = st.sb("turned_p", [P, 2, ns, 512])
        top = st.sb("top", [P, 2, ns])
        total = st.sb("total", [P, 2, ns])
        inv = st.sb("inv", [P, 2, ns])
        (scored, biased, topped, exped, valid_done, summed, inverted, weighed, normed, turned_, copied, mixed,
         stored_, zeroed) = (st.sem(s) for s in (
             "scored", "biased", "topped", "exped", "valid_done", "summed", "inverted", "weighed", "normed",
             "turned", "copied", "mixed", "stored", "zeroed"))
        DEPTH = 3

        @st.block.tensor
        def _(pe):
            for phase, u in skewed(n_units, DEPTH):
                sets, out = units[u]
                for j, s in enumerate(sets):
                    m = u * ns + j
                    if phase == 0:
                        if m >= 3:
                            pe.wait_ge(biased, m - 2)
                        nc.tensor.matmul(core.psum[:, m % 3, 0:s.n], s.q, s.k, start=True, stop=True).then_inc(scored, 1)
                    elif phase == 1:
                        if j == 0:
                            pe.wait_ge(normed, u + 1)
                        if m >= 3:
                            pe.wait_ge(copied, m - 2)
                        for b in range(s.blocks):
                            mm = nc.tensor.transpose(core.psum[:, 3 + m % 3, b * P:(b + 1) * P],
                                                     probs[:, u % 2, j, b * P:(b + 1) * P], core.ident[:])
                        mm.then_inc(turned_, 1)
                    else:
                        pe.wait_ge(copied, m + 1)
                        if j == 0 and u >= 2:
                            pe.wait_ge(stored_, u - 1)
                        base = out.base_partition()
                        for b in range(s.blocks):
                            mm = nc.tensor.matmul(core.psum[base:base + dv, 6 + u % 2, 0:P], s.v(b),
                                                  turned_p[:, u % 2, j, b * P:(b + 1) * P],
                                                  start=(j == 0 and b == 0), stop=(j == ns - 1 and b == s.blocks - 1))
                        if j == ns - 1:
                            mm.then_inc(mixed, 1)

        @st.block.vector
        def _(dve):
            nc.vector.memset(probs[:], 0.0).then_inc(zeroed, 1)
            dve.wait_ge(zeroed, 1)
            for phase, u in skewed(n_units, DEPTH):
                sets, out = units[u]
                if phase == 0:
                    if u >= 2:
                        dve.wait_ge(turned_, (u - 1) * ns)
                    for j, s in enumerate(sets):
                        m = u * ns + j
                        dve.wait_ge(scored, m + 1)
                        nc.vector.scalar_tensor_tensor(
                            out=probs[:, u % 2, j, 0:s.n], in0=core.psum[:, m % 3, 0:s.n], scalar=s.scale / s.slope,
                            in1=s.bias, op0=ALU.mult, op1=ALU.add).then_inc(biased, 1)
                    if joint:
                        n = sets[0].n
                        dve.wait_ge(biased, (u + 1) * ns)
                        nc.vector.tensor_reduce(top[:, u % 2, 0:1], probs[:, u % 2, :, 0:n], mybir.AxisListType.XY, ALU.max,
                                                negate=True).then_inc(topped, 1)
                    else:
                        for j, s in enumerate(sets):
                            m = u * ns + j
                            dve.wait_ge(biased, m + 1)
                            if u >= 2 and j == 0:
                                dve.wait_ge(exped, (u - 1) * ns)
                            nc.vector.tensor_reduce(top[:, u % 2, j:j + 1], probs[:, u % 2, j, 0:s.n], X_AXIS, ALU.max,
                                                    negate=True).then_inc(topped, 1)
                        if sloped:
                            dve.wait_ge(topped, (u + 1) * ns + u)
                            nc.vector.tensor_scalar(top[:, u % 2, :], top[:, u % 2, :], sets[0].slope, None, ALU.mult
                                                    ).then_inc(topped, 1)
                elif phase == 1:
                    dve.wait_ge(exped, (u + 1) * ns)
                    for i, j in enumerate(masked_sets):
                        s = sets[j]
                        nc.vector.tensor_tensor(probs[:, u % 2, j, 0:s.n], probs[:, u % 2, j, 0:s.n], s.valid, ALU.mult
                                                ).then_inc(valid_done, 1)
                        dve.wait_ge(valid_done, 2 * (u * nm + i) + 1)
                        nc.vector.tensor_reduce(total[:, u % 2, j:j + 1], probs[:, u % 2, j, 0:s.n], X_AXIS, ALU.add
                                                ).then_inc(valid_done, 1)
                        dve.wait_ge(valid_done, 2 * (u * nm + i) + 2)
                    if joint:
                        nc.vector.tensor_reduce(inv[:, u % 2, 0:1], total[:, u % 2, :], X_AXIS, ALU.add).then_inc(summed, 1)
                        dve.wait_ge(summed, u + 1)
                        nc.vector.reciprocal(inv[:, u % 2, 0:1], inv[:, u % 2, 0:1]).then_inc(inverted, 1)
                    else:
                        nc.vector.tensor_scalar(total[:, u % 2, :], total[:, u % 2, :], 1e-30, None, ALU.max).then_inc(summed, 1)
                        dve.wait_ge(summed, u + 1)
                        nc.vector.reciprocal(inv[:, u % 2, :], total[:, u % 2, :]).then_inc(inverted, 1)
                    dve.wait_ge(inverted, u + 1)
                    if joint:
                        n = sets[0].n
                        nc.vector.tensor_scalar(probs[:, u % 2, :, 0:n], probs[:, u % 2, :, 0:n], inv[:, u % 2, 0:1], None,
                                                ALU.mult).then_inc(normed, 1)
                    else:
                        for j, s in enumerate(sets):
                            x = probs[:, u % 2, j, 0:s.n]
                            if s.gate is None:
                                ins = nc.vector.tensor_scalar(x, x, inv[:, u % 2, j:j + 1], None, ALU.mult)
                            else:
                                ins = nc.vector.tensor_scalar(x, x, inv[:, u % 2, j:j + 1], s.gate, ALU.mult, ALU.mult)
                            ins.then_inc(normed if j == ns - 1 else weighed, 1)

        @st.block.scalar
        def _(act):
            for phase, u in skewed(n_units, DEPTH):
                sets, out = units[u]
                if phase == 0:
                    if u >= 2:
                        act.wait_ge(inverted, u - 1)
                    for j, s in enumerate(sets):
                        if joint:
                            act.wait_ge(topped, u + 1)
                        elif sloped:
                            act.wait_ge(topped, (u + 1) * (ns + 1))
                        else:
                            act.wait_ge(topped, u * ns + j + 1)
                        t = 0 if joint else j
                        nc.scalar.activation(probs[:, u % 2, j, 0:s.n], probs[:, u % 2, j, 0:s.n], ACT.Exp,
                                             bias=top[:, u % 2, t:t + 1], scale=s.slope,
                                             accum_out=total[:, u % 2, j:j + 1]).then_inc(exped, 1)
                elif phase == 1:
                    for j, s in enumerate(sets):
                        m = u * ns + j
                        act.wait_ge(turned_, m + 1)
                        if u >= 2 and j == 0:
                            act.wait_ge(mixed, u - 1)
                        nc.scalar.activation(turned_p[:, u % 2, j, 0:s.blocks * P], core.psum[:, 3 + m % 3, 0:s.blocks * P],
                                             ACT.Copy).then_inc(copied, 1)
                else:
                    base = out.base_partition()
                    act.wait_ge(mixed, u + 1)
                    nc.scalar.activation(out, core.psum[base:base + dv, 6 + u % 2, 0:P], ACT.Copy).then_inc(stored_, 1)


SSD_H, SSD_P = 16, 64


def ssd(core, pool, xbc, dt_raw, y):
    nc = core.nc
    H, HG = SSD_H, SSD_H // 2
    dt = pool.sb("ssd_dt", [P, NT * H])
    dta = pool.sb("ssd_dta", [P, NT * H])
    acs = pool.sb("ssd_acs", [P, NT * H])
    dec = pool.sb("ssd_dec", [P, NT * H])
    etot = pool.sb("ssd_etot", [P, NT * H])
    xd = pool.sb("ssd_xd", [P, NT, 1024])
    btok = pool.sb("ssd_btok", [P, NT, 256])
    upper = pool.sb("ssd_upper", [P, P])
    masked = pool.sb("ssd_masked", [P, P])
    gt = pool.sb("ssd_gt", [P, NT, 2, P])

    with core.stage("ssd_dt") as st:
        tmp = st.sb("tmp", [P, NT * H])
        rate = st.sb("rate", [P, NT * H])
        tables, dve_done, act_done, pe_done = (st.sem(s) for s in ("tables", "dve_done", "act_done", "pe_done"))

        @st.block.sync
        def _(sp):
            sp.dma_start(upper[:], core.dram["upper"]).then_inc(tables, 16)
            sp.dma_start(masked[:], core.dram["lower_masked"]).then_inc(tables, 16)

        @st.block.vector
        def _(dve):
            nc.vector.tensor_tensor(dt[:], dt_raw[:], core.colblock("l0_dt_bias"), ALU.add).then_inc(dve_done, 1)
            dve.wait_ge(act_done, 4)
            nc.vector.scalar_tensor_tensor(out=dt[:], in0=dt[:], scalar=0.0, in1=tmp[:], op0=ALU.max, op1=ALU.add
                                           ).then_inc(dve_done, 1)
            dve.wait_ge(dve_done, 2)
            nc.vector.scalar_tensor_tensor(out=dta[:], in0=rate[:], scalar=-1.0, in1=dt[:], op0=ALU.mult, op1=ALU.mult
                                           ).then_inc(dve_done, 1)
            dve.wait_ge(pe_done, 2)
            nc.vector.tensor_copy(acs[:], core.psum[:, 0, 0:NT * H]).then_inc(dve_done, 1)
            dve.wait_ge(dve_done, 4)
            nc.vector.tensor_tensor(dec[:], core.psum[:, 1, 0:NT * H], acs[:], ALU.subtract).then_inc(dve_done, 1)

        @st.block.scalar
        def _(act):
            nc.scalar.activation(rate[:], core.colblock("l0_a_log"), ACT.Exp).then_inc(act_done, 1)
            act.wait_ge(dve_done, 1)
            nc.scalar.activation(tmp[:], dt[:], ACT.Abs).then_inc(act_done, 1)
            act.wait_ge(act_done, 2)
            nc.scalar.activation(tmp[:], tmp[:], ACT.Exp, scale=-1.0).then_inc(act_done, 1)
            act.wait_ge(act_done, 3)
            nc.scalar.activation(tmp[:], tmp[:], ACT.Ln, bias=core.col("one")).then_inc(act_done, 1)
            act.wait_ge(dve_done, 5)
            nc.scalar.activation(dec[:], dec[:], ACT.Exp).then_inc(act_done, 1)
            nc.scalar.activation(etot[:], core.psum[:, 1, 0:NT * H], ACT.Exp).then_inc(act_done, 1)

        @st.block.tensor
        def _(pe):
            pe.wait_ge(tables, 32)
            pe.wait_ge(dve_done, 3)
            nc.tensor.matmul(core.psum[:, 0, 0:NT * H], upper[:], dta[:], start=True, stop=True).then_inc(pe_done, 1)
            nc.tensor.matmul(core.psum[:, 1, 0:NT * H], core.ones[:], dta[:], start=True, stop=True).then_inc(pe_done, 1)

    with core.stage("ssd_turn") as st:
        turned_, taken, products, gt_out = (st.sem(s) for s in ("turned", "taken", "products", "gt_out"))

        @st.block.tensor
        def _(pe):
            for i in range(3 * NT):
                c, part = i // 3, i % 3
                if i >= 6:
                    pe.wait_ge(taken, i - 5)
                tiles = [4 * part + f for f in range(4)] if part < 2 else [8, 9]
                for j, f in enumerate(tiles):
                    mm = nc.tensor.transpose(core.psum[:, i % 6, j * P:(j + 1) * P], xbc[:, f, c * P:(c + 1) * P], core.ident[:])
                mm.then_inc(turned_, 1)
            for c in range(NT):
                if c >= 2:
                    pe.wait_ge(gt_out, c - 1)
                for g in range(2):
                    mm = nc.tensor.matmul(core.psum[:, 6 + c % 2, g * P:(g + 1) * P], xbc[:, 8 + g, c * P:(c + 1) * P],
                                          xbc[:, 10 + g, c * P:(c + 1) * P], start=True, stop=True)
                mm.then_inc(products, 1)

        @st.block.vector
        def _(dve):
            for i in range(3 * NT):
                c, part = i // 3, i % 3
                dve.wait_ge(turned_, i + 1)
                if part < 2:
                    rates = dt[:, c * H + part * HG:c * H + (part + 1) * HG].unsqueeze(2).to_broadcast([P, HG, SSD_P])
                    nc.vector.tensor_tensor(xd[:, c, part * 512:(part + 1) * 512].rearrange("p (h d) -> p h d", h=HG),
                                            core.psum[:, i % 6, :].rearrange("p (h d) -> p h d", h=HG), rates, ALU.mult
                                            ).then_inc(taken, 1)
                else:
                    nc.vector.tensor_copy(btok[:, c, :], core.psum[:, i % 6, 0:256]).then_inc(taken, 1)

        @st.block.scalar
        def _(act):
            for c in range(NT):
                act.wait_ge(products, c + 1)
                nc.scalar.activation(gt[:, c, :, :].rearrange("p g l -> p (g l)"), core.psum[:, 6 + c % 2, 0:256], ACT.Copy
                                     ).then_inc(gt_out, 1)

    with core.stage("ssd_scan") as st:
        R = 3
        decay_in = st.sb("decay_in", [P, R, P])
        lmat = st.sb("lmat", [P, R, P])
        mt = st.sb("mt", [P, R, P])
        cdec = st.sb("cdec", [P, R, P])
        state = st.sb("state", [P, 1024])
        xdd = st.sb("xdd", [P, 2, 1024])
        (sums, diffed, grown, decayed, mixed_m, mixed_c, products, stored_, decayed_x, updated, grew, zeroed, state_scaled) = (
            st.sem(s) for s in ("sums", "diffed", "grown", "decayed", "mixed_m", "mixed_c", "products", "stored",
                                "decayed_x", "updated", "grew", "zeroed", "state_scaled"))
        U = NT * H

        @st.block.tensor
        def _(pe):
            for phase, u in skewed(U, 3):
                c, h = u // H, u % H
                if phase == 0:
                    if u >= 2:
                        pe.wait_ge(grown, u - 1)
                    nc.tensor.matmul(core.psum[:, u % 2, 0:P], dta[:, u:u + 1].to_broadcast([P, P]), upper[:],
                                     start=True, stop=True).then_inc(sums, 1)
                elif phase == 2:
                    b, half_ = 2 + (u // 2) % 2, 64 * (h % 2)
                    if h % 2 == 0 and u >= 4:
                        pe.wait_ge(stored_, u // 2 - 1)
                    pe.wait_ge(mixed_m, u + 1)
                    mm = nc.tensor.matmul(core.psum[half_:half_ + 64, b, 0:P], xd[:, c, h * 64:(h + 1) * 64], mt[:, u % R, :],
                                          start=True, stop=(c == 0))
                    if c > 0:
                        pe.wait_ge(mixed_c, (c - 1) * H + h + 1)
                        pe.wait_ge(grew, 2 * c)
                        mm = nc.tensor.matmul(core.psum[half_:half_ + 64, b, 0:P], state[:, h * 64:(h + 1) * 64],
                                              cdec[:, u % R, :], start=False, stop=True)
                    mm.then_inc(products, 1)
                    if h == H - 1 and c < NT - 1:
                        pe.wait_ge(decayed_x, c + 1)
                        for g in range(2):
                            nc.tensor.matmul(core.psum[:, 4 + g, :], btok[:, c, g * P:(g + 1) * P],
                                             xdd[:, c % 2, g * 512:(g + 1) * 512], start=True, stop=True).then_inc(updated, 1)

        @st.block.vector
        def _(dve):
            nc.vector.memset(state[:], 0.0).then_inc(zeroed, 1)
            for phase, u in skewed(U, 3):
                c, h = u // H, u % H
                if phase == 0:
                    dve.wait_ge(sums, u + 1)
                    if u >= R:
                        dve.wait_ge(mixed_m, u - R + 1)
                    nc.vector.scalar_tensor_tensor(out=lmat[:, u % R, :], in0=core.psum[:, u % 2, 0:P], scalar=acs[:, u:u + 1],
                                                   in1=masked[:], op0=ALU.subtract, op1=ALU.add).then_inc(diffed, 1)
                    if h == 0 and c < NT - 1:
                        if c >= 2:
                            dve.wait_ge(updated, 2 * (c - 1))
                        nc.vector.tensor_tensor(xdd[:, c % 2, :].rearrange("p (h d) -> p h d", h=H),
                                                xd[:, c, :].rearrange("p (h d) -> p h d", h=H),
                                                dec[:, c * H:(c + 1) * H].unsqueeze(2).to_broadcast([P, H, SSD_P]), ALU.mult
                                                ).then_inc(decayed_x, 1)
                elif phase == 1:
                    dve.wait_ge(decayed, u + 1)
                    if u >= R:
                        dve.wait_ge(products, u - R + 1)
                    nc.vector.tensor_tensor(mt[:, u % R, :], gt[:, c, h // HG, :], lmat[:, u % R, :], ALU.mult
                                            ).then_inc(mixed_m, 1)
                elif h % 2 == 1:
                    dve.wait_ge(products, u + 1)
                    nc.vector.scalar_tensor_tensor(
                        out=y[:, h // 2, c * P:(c + 1) * P], in0=xbc[:, h // 2, c * P:(c + 1) * P],
                        scalar=core.col("l0_d_skip", h // 2), in1=core.psum[:, 2 + (u // 2) % 2, 0:P],
                        op0=ALU.mult, op1=ALU.add).then_inc(stored_, 1)
                    if h == H - 1 and c < NT - 1:
                        dve.wait_ge(zeroed, 1)
                        if c > 0:
                            dve.wait_ge(grew, 2 * c)
                        by_head = state[:].rearrange("p (h d) -> p h d", h=H)
                        nc.vector.tensor_tensor(by_head, by_head, etot[:, c * H:(c + 1) * H].unsqueeze(2).to_broadcast([P, H, SSD_P]),
                                                ALU.mult).then_inc(state_scaled, 1)
                        dve.wait_ge(state_scaled, c + 1)
                        for g in range(2):
                            dve.wait_ge(updated, 2 * c + g + 1)
                            s = state[:, g * 512:(g + 1) * 512]
                            nc.vector.tensor_tensor(s, core.psum[:, 4 + g, :], s, ALU.add).then_inc(grew, 1)

        @st.block.scalar
        def _(act):
            for phase, u in skewed(U, 2):
                c, h = u // H, u % H
                if phase == 0:
                    act.wait_ge(diffed, u + 1)
                    if u - R >= H:
                        act.wait_ge(mixed_c, u - R - H + 1)
                    nc.scalar.activation(decay_in[:, u % R, :], core.psum[:, u % 2, 0:P], ACT.Exp).then_inc(grown, 1)
                    nc.scalar.activation(lmat[:, u % R, :], lmat[:, u % R, :], ACT.Exp).then_inc(decayed, 1)

        @st.block.gpsimd
        def _(pool_):
            for u in range(H, U):
                c, h = u // H, u % H
                pool_.wait_ge(grown, u + 1)
                if u >= H + R:
                    pool_.wait_ge(products, u - R + 1)
                nc.gpsimd.tensor_tensor(cdec[:, u % R, :], xbc[:, 10 + h // HG, c * P:(c + 1) * P], decay_in[:, u % R, :],
                                        ALU.mult).then_inc(mixed_c, 1)


class Pool:

    def __init__(self, nc, ctx):
        self.nc, self.ctx = nc, ctx

    def sb(self, name, shape, dtype=F32):
        return self.ctx.enter_context(self.nc.sbuf_tensor(name, shape, dtype))

    def pair(self, name, n):
        return Pair(self.sb(name + "_high", [P, n, T], F32R), self.sb(name + "_low", [P, n, T], F32R))


@contextmanager
def buffers(core):
    with ExitStack() as ctx:
        yield Pool(core.nc, ctx)


def product(core, name, n, out, a, b):
    nc = core.nc
    with core.stage(name) as st:
        dve_done, pool_done = st.sem("dve_done"), st.sem("pool_done")

        @st.block.vector
        def _(dve):
            for i in range(n):
                if i % 3 != 2:
                    nc.vector.tensor_tensor(out(i), a(i), b(i), ALU.mult).then_inc(dve_done, 1)

        @st.block.gpsimd
        def _(pool):
            for i in range(2, n, 3):
                nc.gpsimd.tensor_tensor(out(i), a(i), b(i), ALU.mult).then_inc(pool_done, 1)


def modulation(core, name, mod, silu_c, pre_m, post_m, pre_f, post_f):
    nc = core.nc

    def dst(i, at):
        return mod[:, i:i + 1] if isinstance(i, int) else mod[:, bass.ds(i, 1)]

    linear(core, name + "_ada", lambda k: silu_c[:, k:k + 1],
           stored(dst, ACT.Identity, bias=lambda i: core.col(name + "_ada_b", i)), width=1)
    with core.stage(name + "_mod") as st:
        done = st.sem("done")

        @st.block.vector
        def _(dve):
            for at, pre, post in ((0, pre_m, post_m), (24, pre_f, post_f)):
                scale, gate = mod[:, at + 8:at + 16], mod[:, at + 16:at + 24]
                nc.vector.scalar_tensor_tensor(out=scale, in0=scale, scalar=1.0, in1=core.colblock(pre), op0=ALU.add,
                                               op1=ALU.mult).then_inc(done, 1)
                nc.vector.tensor_tensor(gate, gate, core.colblock(post), ALU.mult).then_inc(done, 1)


def swiglu(core, name, xT, mod, mean):
    with buffers(core) as b:
        a = b.pair(name + "_act", 22)
        with buffers(core) as c:
            h = c.pair(name + "_fh", KD)
            norm(core, name + "_fpre", lambda i: xT[:, i, :], [list(range(KD))], mean, None, core.col("eps"),
                 gain=lambda i: mod[:, 32 + i:33 + i], shift=lambda i: mod[:, 24 + i:25 + i], pair=h)
            linear(core, name + "_up", h, gated(a, ACT.Silu))
        y = b.sb(name + "_y", [P, KD, T])
        linear(core, name + "_down", a, stored(lambda i, at: y[:, i, :]))
        norm(core, name + "_fpost", lambda i: y[:, i, :], [list(range(KD))], mean, lambda i: xT[:, i, :], core.col("eps"),
             gain=lambda i: mod[:, 40 + i:41 + i], residual=True)


def rope_table(core, cs):
    nc = core.nc
    H, Q = slice(64, 128), slice(96, 128)
    with core.stage("rope") as st:
        pos_i = st.sb("pos_i", [P, T], I32)
        ang = st.sb("ang", [P, T])
        turns = st.sb("turns", [P, T])
        loaded, done, looked = st.sem("loaded"), st.sem("done"), st.sem("looked")

        @st.block.sync
        def _(sp):
            sp.dma_start(pos_i[:], core.dram["positions"]).then_inc(loaded, 16)

        @st.block.vector
        def _(dve):
            d = Marks(done)

            def after(ins):
                dve.wait_ge(done, d.mark(ins))

            dve.wait_ge(loaded, 16)
            a, n = ang[H, :], turns[H, :]
            after(nc.vector.tensor_copy(a, pos_i[H, :]))
            after(nc.vector.tensor_scalar(a, a, core.col("rope_inv")[H, :], None, ALU.mult))
            after(nc.vector.tensor_scalar(n, a, 1.0 / (2.0 * math.pi), 12582912.0, ALU.mult, ALU.add))
            after(nc.vector.tensor_scalar(n, n, 12582912.0, None, ALU.subtract))
            first, second = 6.28125, 0.001934051513671875
            third = 2.0 * math.pi - first - second
            for part in (first, second, third):
                after(nc.vector.scalar_tensor_tensor(out=a, in0=n, scalar=-part, in1=a, op0=ALU.mult, op1=ALU.add))
            after(nc.vector.tensor_scalar(a, a, 3.1415925, -3.1415925, ALU.min, ALU.max))
            c = ang[64:96, :]
            after(nc.vector.tensor_scalar(turns[64:96, :], c, -1.0, None, ALU.mult))
            after(nc.vector.tensor_tensor(c, c, turns[64:96, :], ALU.max))
            after(nc.vector.tensor_scalar(c, c, -1.0, math.pi / 2.0, ALU.mult, ALU.add))
            after(nc.vector.tensor_scalar(ang[Q, :], ang[Q, :], core.col("rope_sign")[Q, :], None, ALU.mult))

        @st.block.scalar
        def _(act):
            act.wait_ge(done, 12)
            nc.scalar.activation(cs[H, :], ang[H, :], ACT.Sin).then_inc(looked, 1)


def layer0(core, xT, silu_c, mean):
    nc = core.nc
    with buffers(core) as outer:
        mod = outer.sb("l0_modulation", [P, 48])
        modulation(core, "l0", mod, silu_c, "l0_mix_pre_g", "l0_mix_post_g", "l0_ffn_pre_g", "l0_ffn_post_g")
        with buffers(core) as b:
            catT = b.sb("l0_cat", [P, 12, T])
            lowT = b.sb("l0_lowT", [P, 6, T])
            with buffers(core) as c:
                xbc = c.sb("l0_xbcT", [P, 12, T])
                zT = c.sb("l0_zT", [P, KD, T])
                dt_raw = c.sb("l0_dt_raw", [P, NT * 16])
                with buffers(core) as e:
                    h = e.pair("l0_h", KD)
                    norm(core, "l0_pre", lambda i: xT[:, i, :], [list(range(KD))], mean, None, core.col("eps"),
                         gain=lambda i: mod[:, 8 + i:9 + i], shift=lambda i: mod[:, i:i + 1], pair=h)
                    linear(core, "l0_xbc", h, convolved(4, lambda i, j: core.col("l0_conv_w", 4 * i + j),
                                                        lambda i: core.col("l0_conv_b", i), lambda i, at: xbc[:, i, :]))
                    linear(core, "l0_z", h, stored(lambda i, at: zT[:, i, :], ACT.Silu))
                    linear(core, "l0_low", h, stored(lambda i, at: lowT[:, i, :]))
                    linear(core, "l0_dt", h, stored(lambda i, at: dt_raw[:, i * 16:(i + 1) * 16]), by_tokens=True)
                with buffers(core) as e:
                    ssd(core, e, xbc, dt_raw, catT)
                product(core, "l0_gate", KD, lambda i: catT[:, i, :], lambda i: catT[:, i, :], lambda i: zT[:, i, :])
                with buffers(core) as e:
                    m512 = e.sb("mean512", [P, P])
                    fill(core, "l0_m512", [(m512, 1.0 / 512)])
                    norm(core, "l0_ssm", lambda i: catT[:, i, :], [[0, 1, 2, 3], [4, 5, 6, 7]], m512[:],
                         lambda i: catT[:, i, :], core.col("eps"), gain=lambda i: core.col("l0_ssm_norm_g", i))
            with buffers(core) as c:
                m384, m256 = c.sb("mean384", [P, P]), c.sb("mean256", [P, P])
                cs, fold, causal = c.sb("rope_cs", [P, T]), c.sb("fold", [P, P]), c.sb("causal", [P, T])
                fill(core, "l0_means", [(m384, 1.0 / 384), (m256, 1.0 / 256)], [(fold, "fold"), (causal, "causal")])
                rope_table(core, cs)
                qT, kT, vt = c.sb("mla_q", [P, 8, T]), c.sb("mla_k", [P, 8, T]), c.sb("mla_v", [P, NT, 512])
                low = lambda i: lowT[:, i, :]
                norm(core, "l0_qa", low, [[0, 1, 2]], m384[:], low, core.col("eps"), gain=lambda i: core.col("l0_q_a_norm_g", i))
                norm(core, "l0_kva", low, [[3, 4]], m256[:], low, core.col("eps"), gain=lambda i: core.col("l0_kv_a_norm_g", i - 3))

                def rotated(core, st, g):
                    rows_done = st.sem("rows_done")

                    @st.block.scalar
                    def _(act):
                        def take(i, at, turn):
                            act.wait_ge(g.done, i + 1)
                            nc.scalar.activation(qT[0:64, i, :], g.bank(i)[0:64, :], ACT.Copy).then_inc(rows_done, 1)
                        g.run_scalar(act, take)

                    @st.block.vector
                    def _(dve):
                        for i in range(g.count):
                            dve.wait_ge(rows_done, i + 1)
                            nc.vector.tensor_tensor(qT[64:128, i, :], g.bank(i)[64:128, :], cs[64:128, :], ALU.mult
                                                    ).then_inc(g.free, 1)

                linear(core, "l0_q", low, rotated, raw=True)
                linear(core, "l0_k", lambda k: lowT[:, 3 + k, :], stored(lambda i, at: kT[0:64, i, :]))
                linear(core, "l0_v", lambda k: lowT[:, 3 + k, :], stored(lambda i, at: vt[:, i, :]), by_tokens=True)
                with core.stage("l0_krope") as st:
                    rotated_k, folded, spread = st.sem("rotated"), st.sem("folded"), st.sem("spread")

                    @st.block.vector
                    def _(dve):
                        nc.vector.tensor_tensor(lowT[64:128, 5, :], lowT[64:128, 5, :], cs[64:128, :], ALU.mult
                                                ).then_inc(rotated_k, 1)

                    @st.block.tensor
                    def _(pe):
                        pe.wait_ge(rotated_k, 1)
                        nc.tensor.matmul(core.bank(0), fold[64:128, :], lowT[64:128, 5, :], start=True, stop=True
                                         ).then_inc(folded, 1)

                    @st.block.scalar
                    def _(act):
                        act.wait_ge(folded, 1)
                        for i in range(8):
                            nc.scalar.activation(kT[64:128, i, :], core.psum[64:128, 0, :], ACT.Copy).then_inc(spread, 1)
                units = []
                for i in range(8):
                    for q in range(NT):
                        n = (q + 1) * P
                        keys = Keys(qT[:, i, q * P:n], kT[:, i, 0:n], lambda kb, i=i: vt[:, kb, 64 * i:64 * i + 64], n,
                                    causal[:, T - n:T], 96.0 ** -0.5)
                        units.append(([keys], catT[64 * (i % 2):64 * (i % 2) + 64, 8 + i // 2, q * P:n]))
                attention(core, "mla", units)
            mixT = b.sb("l0_mixT", [P, KD, T])
            linear(core, "l0_out", lambda k: catT[:, k, :], stored(lambda i, at: mixT[:, i, :]), raw=True)
            norm(core, "l0_post", lambda i: mixT[:, i, :], [list(range(KD))], mean, lambda i: xT[:, i, :], core.col("eps"),
                 gain=lambda i: mod[:, 16 + i:17 + i], residual=True)
        swiglu(core, "l0", xT, mod, mean)


def fill(core, name, constants, tables=()):
    nc = core.nc
    with core.stage(name) as st:
        filled, loaded = st.sem("filled"), st.sem("loaded")

        @st.block.vector
        def _(dve):
            for buf, value in constants:
                nc.vector.memset(buf[:], value).then_inc(filled, 1)

        @st.block.sync
        def _(sp):
            for buf, table in tables:
                src = core.dram[table] if isinstance(table, str) else table
                sp.dma_start(buf[:], src).then_inc(loaded, 16)
            if tables:
                sp.wait_ge(loaded, 16 * len(tables))


GLA_H = 4
SUB = 32
NSUB = P // SUB
CMP = 31


def gla_decays(core, lr, cum):
    nc = core.nc
    with core.stage("gla_decays") as st:
        gk2 = st.sb("gk2", [16, T])
        z = st.sb("z", [P, GLA_H, T])
        soft = st.sb("soft", [P, GLA_H, T])
        loaded, logits, raw, looked, low, scaled, scanned = (st.sem(s) for s in (
            "loaded", "logits", "raw", "looked", "low", "scaled", "scanned"))

        @st.block.sync
        def _(sp):
            sp.dma_start(gk2[:], core.dram["gk2"]).then_inc(loaded, 16)

        @st.block.tensor
        def _(pe):
            pe.wait_ge(loaded, 16)
            for i in range(GLA_H):
                nc.tensor.matmul(core.bank(i), gk2[:, i * P:(i + 1) * P], lr[:], start=True, stop=True).then_inc(logits, 1)

        @st.block.scalar
        def _(act):
            for i in range(GLA_H):
                act.wait_ge(logits, i + 1)
                nc.scalar.activation(z[:, i, :], core.bank(i), ACT.Identity, bias=core.col("l1_b_gk", i)).then_inc(raw, 1)
            for n, (func, scale, bias) in enumerate(((ACT.Abs, 1.0, None), (ACT.Exp, -1.0, None), (ACT.Ln, 1.0, core.col("one")))):
                for i in range(GLA_H):
                    act.wait_ge(raw, i + 1)
                    if n:
                        act.wait_ge(looked, (n - 1) * GLA_H + i + 1)
                    src = z[:, i, :] if n == 0 else soft[:, i, :]
                    kw = {} if bias is None else {"bias": bias}
                    nc.scalar.activation(soft[:, i, :], src, func, scale=scale, **kw).then_inc(looked, 1)

        @st.block.vector
        def _(dve):
            for i in range(GLA_H):
                dve.wait_ge(looked, 2 * GLA_H + i + 1)
                nc.vector.scalar_tensor_tensor(out=z[:, i, :], in0=z[:, i, :], scalar=0.0, in1=soft[:, i, :], op0=ALU.min,
                                               op1=ALU.subtract).then_inc(low, 1)
                dve.wait_ge(low, i + 1)
                nc.vector.tensor_scalar(z[:, i, :], z[:, i, :], 1.0 / 16.0, None, ALU.mult).then_inc(scaled, 1)
                dve.wait_ge(scaled, i + 1)
                for c in range(NT):
                    s = slice(c * P, (c + 1) * P)
                    nc.vector.tensor_tensor_scan(cum[:, i, s], core.ones[:], z[:, i, s], 0.0, ALU.mult, ALU.add
                                                 ).then_inc(scanned, 1)


def gla(core, qk, v, cum, y):
    nc = core.nc
    H = GLA_H
    scale = 128.0 ** -0.5
    with core.stage("gla") as st:
        R = 3
        near = st.sb("near", [P, R, P])
        end = st.sb("end", [P, R, P])
        far = st.sb("far", [P, R, 192])
        near_k = st.sb("near_k", [P, R, P])
        start_q = st.sb("start_q", [P, R, P])
        q_in = st.sb("q_in", [P, R, P])
        left = st.sb("left", [P, R, P])
        left_tok = st.sb("left_tok", [P, R, P])
        att = st.sb("att", [P, R, P])
        upper = st.sb("upper", [P, P])
        state = st.sb("state", [P, H, 256])
        (tables, zeroed, diffed, clamped, grown, q_scaled, k_scaled, scored, left_turned, left_out, masked, mixed, stored_,
         added_, updated) = (st.sem(s) for s in (
             "tables", "zeroed", "diffed", "clamped", "grown", "q_scaled", "k_scaled", "scored", "left_turned", "left_out",
             "masked", "mixed", "stored", "added", "updated"))
        U = NT * H
        off = [0, 96, 160]

        def of(u):
            return u // H, u % H, slice(u // H * P, (u // H + 1) * P)

        @st.block.sync
        def _(sp):
            sp.dma_start(upper[:], core.dram["upper"]).then_inc(tables, 16)

        @st.block.tensor
        def _(pe):
            for phase, u in skewed(U, 3):
                c, h, s = of(u)
                if phase == 1:
                    pe.wait_ge(q_scaled, 5 * (u + 1))
                    pe.wait_ge(k_scaled, 3 * (u + 1))
                    if u >= 2:
                        pe.wait_ge(masked, 4 * (u - 1))
                    for j in range(NSUB):
                        a, b = SUB * j, SUB * (j + 1)
                        mm = nc.tensor.matmul(core.psum[a:b, u % 2, a:b], near_k[:, u % R, a:b], near[:, u % R, a:b],
                                              start=True, stop=True)
                        if j < NSUB - 1:
                            mm = nc.tensor.matmul(core.psum[a:b, u % 2, b:P], end[:, u % R, a:b],
                                                  far[:, u % R, off[j]:off[j] + P - b], start=True, stop=True)
                    mm.then_inc(scored, 1)
                    if u >= 2:
                        pe.wait_ge(left_out, u - 1)
                    nc.tensor.transpose(core.psum[:, 2 + u % 2, 0:P], left[:, u % R, :], core.ident[:]).then_inc(left_turned, 1)
                elif phase == 2:
                    pe.wait_ge(masked, 4 * (u + 1))
                    if u >= 2:
                        pe.wait_ge(stored_, u - 1)
                    if c > 0:
                        pe.wait_ge(updated, u - H + 1)
                    for n in range(2):
                        out = core.psum[:, 4 + u % 2, n * P:(n + 1) * P]
                        if c > 0:
                            nc.tensor.matmul(out, state[:, h, n * P:(n + 1) * P], q_in[:, u % R, :], start=True, stop=False)
                        mm = nc.tensor.matmul(out, v[:, c, h * 256 + n * P:h * 256 + (n + 1) * P], att[:, u % R, :],
                                              start=(c == 0), stop=True)
                    mm.then_inc(mixed, 1)
                    pe.wait_ge(left_out, u + 1)
                    if u >= 2:
                        pe.wait_ge(updated, u - 1)
                    nc.tensor.matmul(core.psum[:, 6 + u % 2, 0:256], left_tok[:, u % R, :], v[:, c, h * 256:(h + 1) * 256],
                                     start=True, stop=True).then_inc(added_, 1)

        @st.block.vector
        def _(dve):
            nc.vector.memset(att[:], 0.0).then_inc(zeroed, 1)
            nc.vector.memset(state[:], 0.0).then_inc(zeroed, 1)
            dve.wait_ge(zeroed, 2)
            dve.wait_ge(tables, 16)
            for phase, u in skewed(U, 3):
                c, h, s = of(u)
                b = cum[:, h, s].rearrange("p (j t) -> p j t", t=SUB)
                if phase == 0:
                    if u >= R:
                        dve.wait_ge(scored, u - R + 1)
                    slot = lambda x: x[:, u % R, :].rearrange("p (j t) -> p j t", t=SUB)
                    mid, last = b[:, :, 15:16].to_broadcast([P, NSUB, SUB]), b[:, :, 31:32].to_broadcast([P, NSUB, SUB])
                    nc.vector.tensor_tensor(slot(near), b, mid, ALU.subtract).then_inc(clamped, 1)
                    nc.vector.tensor_tensor(slot(end), last, b, ALU.subtract).then_inc(diffed, 1)
                    for j in range(NSUB - 1):
                        a, z = SUB * (j + 1), off[j]
                        nc.vector.tensor_scalar(far[:, u % R, z:z + P - a], cum[:, h, c * P + a:(c + 1) * P],
                                                cum[:, h, c * P + a - 1:c * P + a], None, ALU.subtract).then_inc(diffed, 1)
                    dve.wait_ge(clamped, u + 1)
                    nc.vector.tensor_scalar(near[:, u % R, :], near[:, u % R, :], 80.0, -80.0, ALU.min, ALU.max
                                            ).then_inc(diffed, 1)
                elif phase == 1:
                    dve.wait_ge(grown, 6 * (u + 1))
                    if u >= R:
                        dve.wait_ge(mixed, u - R + 1)
                    q = qk[:, h, s]

                    def scaled(out, x, e):
                        nc.vector.scalar_tensor_tensor(out=out, in0=x, scalar=scale, in1=e, op0=ALU.mult, op1=ALU.mult
                                                       ).then_inc(q_scaled, 1)

                    scaled(near[:, u % R, :], q, near[:, u % R, :])
                    for j in range(NSUB - 1):
                        f = far[:, u % R, off[j]:off[j] + P - SUB * (j + 1)]
                        scaled(f, qk[:, h, c * P + SUB * (j + 1):(c + 1) * P], f)
                    scaled(q_in[:, u % R, :], q, start_q[:, u % R, :])
                else:
                    dve.wait_ge(scored, u + 1)
                    for j in range(NSUB):
                        a, z = SUB * j, SUB * (j + 1)
                        nc.vector.tensor_tensor(att[a:z, u % R, a:P], core.psum[a:z, u % 2, a:P], upper[a:z, a:P], ALU.mult
                                                ).then_inc(masked, 1)
                    dve.wait_ge(added_, u + 1)
                    if u >= H:
                        dve.wait_ge(updated, u - H + 1)
                    nc.vector.scalar_tensor_tensor(out=state[:, h, :], in0=state[:, h, :], scalar=start_q[:, u % R, P - 1:P],
                                                   in1=core.psum[:, 6 + u % 2, 0:256], op0=ALU.mult, op1=ALU.add
                                                   ).then_inc(updated, 1)

        @st.block.scalar
        def _(act):
            for phase, u in skewed(U, 3):
                c, h, s = of(u)
                if phase == 0:
                    act.wait_ge(diffed, 5 * (u + 1))
                    if u >= R:
                        act.wait_ge(updated, u - R + 1)
                        act.wait_ge(left_turned, u - R + 1)
                        act.wait_ge(scored, u - R + 1)
                        act.wait_ge(q_scaled, 5 * (u - R + 1))
                    b = cum[:, h, s]
                    for out, src, sc, bias in ((near_k, near, -1.0, None), (near, near, 1.0, None), (end, end, 1.0, None),
                                               (far, far, 1.0, None), (start_q, None, 1.0, None), (left, None, -1.0, 1)):
                        x = b if src is None else src[:, u % R, :]
                        kw = {"bias": cum[:, h, (c + 1) * P - 1:(c + 1) * P]} if bias else {}
                        if out is near:
                            act.wait_ge(grown, 6 * u + 1)
                        nc.scalar.activation(out[:, u % R, :], x, ACT.Exp, scale=sc, **kw).then_inc(grown, 1)
                elif phase == 1:
                    act.wait_ge(left_turned, u + 1)
                    if u >= R:
                        act.wait_ge(added_, u - R + 1)
                    nc.scalar.activation(left_tok[:, u % R, :], core.psum[:, 2 + u % 2, 0:P], ACT.Copy).then_inc(left_out, 1)
                else:
                    act.wait_ge(mixed, u + 1)
                    nc.scalar.activation(y[:, 2 * h:2 * h + 2, s], core.psum[:, 4 + u % 2, 0:256].rearrange(
                        "p (n t) -> p n t", n=2), ACT.Copy).then_inc(stored_, 1)

        @st.block.gpsimd
        def _(pool):
            for u in range(U):
                c, h, s = of(u)
                pool.wait_ge(grown, 6 * (u + 1))
                for x in (near_k, end, left):
                    nc.gpsimd.tensor_tensor(x[:, u % R, :], qk[:, 4 + h, s], x[:, u % R, :], ALU.mult).then_inc(k_scaled, 1)


def windows(core, name, src, z):
    nc = core.nc
    with core.stage(name) as st:
        copied, placed = st.sem("copied"), st.sem("placed")

        @st.block.scalar
        def _(act):
            for g in range(2):
                for odd in range(2):
                    rows = src[64 * g:64 * g + 64, :].rearrange("p (n l) -> p l n", l=16)
                    for far in range(2):
                        nc.scalar.activation(z[64 * odd:64 * odd + 64, 8 * far:8 * far + 8, g * CMP:(g + 1) * CMP],
                                             rows[:, odd:16:2, far:far + CMP], ACT.Copy).then_inc(copied, 1)

        @st.block.vector
        def _(dve):
            dve.wait_ge(copied, 8)
            nc.vector.tensor_tensor(z[:], z[:], core.colblock("l1_cmp_pos").unsqueeze(2).to_broadcast([P, 16, 2 * CMP]), ALU.add
                                    ).then_inc(placed, 1)


def layer1(core, xT, silu_c, mean):
    nc = core.nc
    with buffers(core) as outer:
        mod = outer.sb("l1_modulation", [P, 48])
        modulation(core, "l1", mod, silu_c, "l1_mix_pre_g", "l1_mix_post_g", "l1_ffn_pre_g", "l1_ffn_post_g")
        with buffers(core) as b:
            catT = b.sb("l1_cat", [P, 12, T])
            nfT = b.sb("nsa_f", [P, 8, T])
            ntk = b.sb("nsa_t", [P, NT, 280])
            with buffers(core) as c:
                qk, gv, gg, lr = c.sb("gla_qk", [P, 8, T]), c.sb("gla_v", [P, NT, 1024]), c.sb("gla_g", [P, 8, T]), c.sb("gla_lr", [16, T])
                with buffers(core) as e:
                    h = e.pair("l1_h", KD)
                    norm(core, "l1_pre", lambda i: xT[:, i, :], [list(range(KD))], mean, None, core.col("eps"),
                         gain=lambda i: mod[:, 8 + i:9 + i], shift=lambda i: mod[:, i:i + 1], pair=h)
                    linear(core, "l1_qk", h, stored(lambda i, at: qk[:, i, :]))
                    linear(core, "l1_v", h, stored(lambda i, at: gv[:, i % NT, i // NT * 256:(i // NT + 1) * 256]), by_tokens=True)
                    linear(core, "l1_lr", h, stored(lambda i, at: lr[:, :]))
                    linear(core, "l1_gg", h, stored(lambda i, at: gg[:, i, :], ACT.Silu))
                    linear(core, "l1_nf", h, stored(lambda i, at: nfT[:, i, :]))
                    linear(core, "l1_nt", h, stored(lambda i, at: ntk[:, i, :]), by_tokens=True)
                with buffers(core) as e:
                    cum = e.sb("gla_cum", [P, GLA_H, T])
                    gla_decays(core, lr, cum)
                    gla(core, qk, gv, cum, catT)
                with buffers(core) as e:
                    m256 = e.sb("mean256_l1", [P, P])
                    fill(core, "l1_m256", [(m256, 1.0 / 256)])
                    norm(core, "l1_gla", lambda i: catT[:, i, :], [[0, 1], [2, 3], [4, 5], [6, 7]], m256[:],
                         lambda i: catT[:, i, :], core.col("eps"), gain=lambda i: core.col("l1_gla_norm_g", i % 2),
                         times=lambda i: gg[:, i, :])
            with buffers(core) as c:
                alibi, cmp_bias, cmp_valid = c.sb("alibi", [P, T]), c.sb("cmp_bias", [P, NT, CMP]), c.sb("cmp_valid", [P, NT, CMP])
                w2 = c.sb("cmp_w2", [P, 4, 64])
                hid = c.sb("cmp_hidden", [P, 2, 2, 2 * CMP])
                k_cmp, v_cmp = c.sb("k_cmp", [P, CMP]), c.sb("v_cmp", [P, 2, 64])
                fill(core, "nsa_tables", [(v_cmp, 0.0)], [(alibi, "alibi"), (cmp_bias, "cmp_bias"), (cmp_valid, "cmp_valid"),
                                                          (w2, "cmp_w2")])
                with buffers(core) as e:
                    z = [e.sb(f"windows{n}", [P, 16, 2 * CMP]) for n in range(2)]
                    for n, kind in enumerate("kv"):
                        windows(core, f"cmp_{kind}_windows", nfT[:, 4 + n, :], z[n])
                        linear(core, f"l1_cmp_{kind}", lambda k, n=n: z[n][:, k, :],
                               stored(lambda i, at, n=n: hid[:, n, i, :], ACT.Silu), width=2 * CMP)
                with core.stage("cmp_out") as st:
                    multiplied, out_done, gates_done = st.sem("multiplied"), st.sem("out_done"), st.sem("gates_done")

                    @st.block.tensor
                    def _(pe):
                        for g in range(2):
                            cols = slice(g * CMP, (g + 1) * CMP)
                            for k in range(2):
                                mm = nc.tensor.matmul(core.psum[64 * g:64 * g + 64, g, 0:CMP], w2[:, k, :], hid[:, 0, k, cols],
                                                      start=(k == 0), stop=(k == 1))
                            mm.then_inc(multiplied, 1)
                            for k in range(2):
                                mm = nc.tensor.matmul(core.psum[0:CMP, 2 + g, 0:64], hid[:, 1, k, cols], w2[:, 2 + k, :],
                                                      start=(k == 0), stop=(k == 1))
                            mm.then_inc(multiplied, 1)

                    @st.block.scalar
                    def _(act):
                        nc.scalar.activation(ntk[:, :, 256:280], ntk[:, :, 256:280], ACT.Sigmoid).then_inc(gates_done, 1)
                        for g in range(2):
                            act.wait_ge(multiplied, 2 * g + 2)
                            nc.scalar.activation(k_cmp[64 * g:64 * g + 64, :], core.psum[64 * g:64 * g + 64, g, 0:CMP], ACT.Copy
                                                 ).then_inc(out_done, 1)
                            nc.scalar.activation(v_cmp[0:CMP, g, :], core.psum[0:CMP, 2 + g, 0:64], ACT.Copy).then_inc(out_done, 1)
                units = []
                for g in range(2):
                    for j in range(4):
                        rows, head = slice(64 * g, 64 * g + 64), 4 * g + j
                        slope = 2.0 ** -(head + 1)
                        for q in range(NT):
                            n = (q + 1) * P
                            query = nfT[rows, j, q * P:n]
                            gate = lambda s: ntk[:, q, 256 + 3 * head + s:257 + 3 * head + s]
                            bias = alibi[:, T - n:T]
                            sets = [
                                Keys(query, k_cmp[rows, :], lambda kb, g=g: v_cmp[:, g, :], CMP, cmp_bias[:, q, :], 0.125,
                                     slope, gate(0), cmp_valid[:, q, :]),
                                Keys(query, nfT[rows, 6, 0:n], lambda kb, g=g: ntk[:, kb, 64 * g:64 * g + 64], n, bias, 0.125,
                                     slope, gate(1)),
                                Keys(query, nfT[rows, 7, 0:n], lambda kb, g=g: ntk[:, kb, 128 + 64 * g:192 + 64 * g], n, bias,
                                     0.125, slope, gate(2)),
                            ]
                            units.append((sets, catT[rows, 8 + j, q * P:n]))
                attention(core, "nsa", units)
            mixT = b.sb("l1_mixT", [P, KD, T])
            linear(core, "l1_out", lambda k: catT[:, k, :], stored(lambda i, at: mixT[:, i, :]), raw=True)
            norm(core, "l1_post", lambda i: mixT[:, i, :], [list(range(KD))], mean, lambda i: xT[:, i, :], core.col("eps"),
                 gain=lambda i: mod[:, 16 + i:17 + i], residual=True)
        swiglu(core, "l1", xT, mod, mean)


def glu_convolved(taps, weight, bias, dst):
    def epilogue(core, st, g):
        nc = core.nc
        pad = taps - 1
        gate = st.sb("gate", [P, 2, T])
        raw = st.sb("raw", [P, 2, pad + T])
        acc = st.sb("acc", [P, 2, T])
        gate_done, tap_done, tile_done, zeroed = (st.sem(n) for n in (
            "gate_done", "tap_done", "tile_done", "zeroed"))
        tiles = g.count // 2

        @st.block.scalar
        def _(act):
            def finished(t):
                act.wait_ge(tap_done, (t + 1) * taps)
                nc.scalar.activation(dst(t), acc[:, t % 2, :], ACT.Identity, bias=bias(t)).then_inc(tile_done, 1)

            def take(i, at, turn):
                if at % 2:
                    return
                act.wait_ge(g.done, i + 1)
                if at >= 4:
                    act.wait_ge(g.free, i - 2)
                nc.scalar.activation(gate[:, at // 2 % 2, :], g.bank(at), ACT.Sigmoid).then_inc(gate_done, 1)
                if at >= 4:
                    finished(at // 2 - 2)
            g.run_scalar(act, take)
            finished(tiles - 2)
            finished(tiles - 1)

        @st.block.vector
        def _(dve):
            nc.vector.memset(raw[:, :, 0:pad], 0.0).then_inc(zeroed, 1)
            dve.wait_ge(zeroed, 1)
            for i in range(tiles):
                dve.wait_ge(g.done, 2 * i + 2)
                dve.wait_ge(gate_done, i + 1)
                nc.vector.tensor_tensor(raw[:, i % 2, pad:], g.bank(2 * i + 1), gate[:, i % 2, :], ALU.mult).then_inc(g.free, 2)
                dve.wait_ge(g.free, 2 * i + 2)
                if i >= 2:
                    dve.wait_ge(tile_done, i - 1)
                for j in range(taps):
                    x, a = raw[:, i % 2, j:j + T], acc[:, i % 2, :]
                    if j == 0:
                        ins = nc.vector.tensor_scalar(a, x, weight(i, 0), None, ALU.mult)
                    else:
                        dve.wait_ge(tap_done, i * taps + j)
                        ins = nc.vector.scalar_tensor_tensor(out=a, in0=x, scalar=weight(i, j), in1=a, op0=ALU.mult, op1=ALU.add)
                    ins.then_inc(tap_done, 1)
    return epilogue


def short_convolved(taps, weight, dst):
    def epilogue(core, st, g):
        nc = core.nc
        pad = taps - 1
        gate = st.sb("gate", [P, 2, T])
        raw = st.sb("raw", [P, 2, pad + T])
        acc = st.sb("acc", [P, 2, T])
        gate_done, product_done, tap_done, zeroed = (st.sem(n) for n in ("gate_done", "product_done", "tap_done", "zeroed"))

        @st.block.scalar
        def _(act):
            def take(at):
                if at % 3:
                    return
                i = at // 3
                act.wait_ge(g.done, at + 1)
                if i >= 2:
                    act.wait_ge(product_done, i - 1)
                nc.scalar.activation(gate[:, i % 2, :], g.bank(at), ACT.Copy).then_inc(gate_done, 1)
            g.run_scalar(act, lambda i, at, turn: take(at))

        @st.block.vector
        def _(dve):
            nc.vector.memset(raw[:, :, 0:pad], 0.0).then_inc(zeroed, 1)
            dve.wait_ge(zeroed, 1)
            for i in range(g.count // 3):
                dve.wait_ge(g.done, 3 * i + 2)
                dve.wait_ge(gate_done, i + 1)
                nc.vector.tensor_tensor(raw[:, i % 2, pad:], g.bank(3 * i + 1), gate[:, i % 2, :], ALU.mult).then_inc(product_done, 1)
                dve.wait_ge(product_done, i + 1)
                if i >= 2:
                    dve.wait_ge(g.free, 3 * (i - 1))
                for j in range(taps):
                    x, a = raw[:, i % 2, j:j + T], acc[:, i % 2, :]
                    if j == 0:
                        ins = nc.vector.tensor_scalar(a, x, weight(i, 0), None, ALU.mult)
                    else:
                        dve.wait_ge(tap_done, i * taps + j)
                        ins = nc.vector.scalar_tensor_tensor(out=a, in0=x, scalar=weight(i, j), in1=a, op0=ALU.mult, op1=ALU.add)
                    ins.then_inc(tap_done, 1)
                dve.wait_ge(tap_done, (i + 1) * taps)
                dve.wait_ge(g.done, 3 * i + 3)
                nc.vector.tensor_tensor(dst(i), g.bank(3 * i + 2), acc[:, i % 2, :], ALU.mult).then_inc(g.free, 3)
    return epilogue


def scaled_to(dst, scale):
    def epilogue(core, st, g):
        @st.block.vector
        def _(dve):
            for i in range(g.count):
                dve.wait_ge(g.done, i + 1)
                core.nc.vector.tensor_tensor(dst(i), g.bank(i), scale(i), ALU.mult).then_inc(g.free, 1)
    return epilogue


def conv_ffn(core, name, xT, mean):
    with buffers(core) as b:
        a = b.pair(name + "_act", 22)

        def tap(i, j):
            return core.col(name + "_ffn_dw_w", i * 3 + j)

        with buffers(core) as c:
            h = c.pair(name + "_fh", KD)
            norm(core, name + "_fpre", lambda i: xT[:, i, :], [list(range(KD))], mean, None, core.col("eps"),
                 gain=lambda i: core.col(name + "_norm2_g", i), pair=h)
            linear(core, name + "_up", h, gated(a, ACT.Silu, 3, tap))
        linear(core, name + "_down", a, added(lambda i: xT[:, i, :]))
        norm(core, name + "_final", lambda i: xT[:, i, :], [list(range(KD))], mean, lambda i: xT[:, i, :], core.col("eps"),
             gain=lambda i: core.col(name + "_final_g", i))


def block2(core, xT, mean):
    nc = core.nc
    with buffers(core) as b:
        h = b.pair("b2_h", KD)
        attT, confT, shortT = b.sb("b2_att", [P, 2, T]), b.sb("b2_confT", [P, 6, T]), b.sb("b2_short", [P, 6, T])
        norm(core, "b2_pre", lambda i: xT[:, i, :], [list(range(KD))], mean, None, core.col("eps"),
             gain=lambda i: core.col("b2_norm1_g", i), pair=h)
        with buffers(core) as c:
            qk, v, bias = c.sb("b2_q_k", [P, 12, T]), c.sb("b2_v_t", [P, NT, 768]), c.sb("b2_bias", [P, 12, T])
            fill(core, "b2_tables", [], [(bias, "dilated")])
            linear(core, "b2_qk", h, stored(lambda i, at: qk[:, i, :]))
            linear(core, "b2_v", h, stored(lambda i, at: v[:, i % NT, i // NT * 256:(i // NT + 1) * 256]), by_tokens=True)
            units = []
            for hd in range(4):
                rows = slice(64 * (hd % 2), 64 * (hd % 2) + 64)
                for q in range(NT):
                    n = (q + 1) * P
                    sets = [Keys(qk[rows, 2 * g + hd // 2, q * P:n], qk[rows, 6 + 2 * g + hd // 2, 0:n],
                                 lambda kb, g=g, hd=hd: v[:, kb, 256 * g + 64 * hd:256 * g + 64 * hd + 64], n,
                                 bias[:, 4 * g + hd, T - n:T], 0.125) for g in range(3)]
                    units.append((sets, attT[rows, hd // 2, q * P:n]))
            attention(core, "dilated", units, joint=True)
        linear(core, "b2_conf", h, glu_convolved(31, lambda i, j: core.col("b2_conf_w", 31 * i + j),
                                                 lambda i: core.col("b2_conf_b", i), lambda i: confT[:, i, :]))
        linear(core, "b2_sc", h, short_convolved(3, lambda i, j: core.col("b2_sc_w", 3 * i + j), lambda i: shortT[:, i, :]))
        with buffers(core) as c:
            m768 = c.sb("mean768", [P, P])
            fill(core, "b2_m768", [(m768, 1.0 / 768)])
            norm(core, "b2_ln", lambda i: confT[:, i, :], [list(range(6))], m768[:], lambda i: confT[:, i, :], core.col("eps"),
                 gain=lambda i: core.col("b2_ln_g", i), shift=lambda i: core.col("b2_ln_b", i), center=m768[:], last=ACT.Silu)
        with buffers(core) as c:
            gT, mixed = c.sb("b2_gates", [P, KD, T]), c.sb("b2_mixed", [P, KD, T])
            gate, mix = (lambda i: gT[:, i, :]), (lambda i: mixed[:, i, :])
            for n, (branch, src) in enumerate((("b2_attn_out", attT), ("b2_conf_out", confT), ("b2_sc_out", shortT))):
                linear(core, f"b2_gate{n}", h, stored(lambda i, at: gT[:, i, :], ACT.Sigmoid))
                linear(core, branch, lambda k, src=src: src[:, k, :], added(mix, gate) if n else scaled_to(mix, gate),
                       raw=True)
            linear(core, "b2_o", lambda k: mixed[:, k, :], added(lambda i: xT[:, i, :]), raw=True)
    conv_ffn(core, "b2", xT, mean)


LEVELS = 7


def token_shifted(mu, dst):
    def epilogue(core, st, g):
        nc = core.nc
        raw = st.sb("raw", [P, 2, 1 + T])
        diff = st.sb("diff", [P, 2, T])
        diffed, moved, zeroed = st.sem("diffed"), st.sem("moved"), st.sem("zeroed")

        @st.block.scalar
        def _(act):
            def take(i, at, turn):
                act.wait_ge(g.done, i + 1)
                if at >= 2:
                    act.wait_ge(moved, i - 1)
                nc.scalar.activation(raw[:, at % 2, 1:], g.bank(at), ACT.Copy).then_inc(g.free, 1)
            g.run_scalar(act, take)

        @st.block.vector
        def _(dve):
            nc.vector.memset(raw[:, :, 0:1], 0.0).then_inc(zeroed, 1)
            dve.wait_ge(zeroed, 1)
            for i in range(g.count):
                dve.wait_ge(g.free, i + 1)
                x = raw[:, i % 2, 1:]
                nc.vector.tensor_tensor(diff[:, i % 2, :], raw[:, i % 2, 0:T], x, ALU.subtract).then_inc(diffed, 1)
                dve.wait_ge(diffed, i + 1)
                nc.vector.scalar_tensor_tensor(out=dst(i), in0=diff[:, i % 2, :], scalar=mu(i), in1=x, op0=ALU.mult,
                                               op1=ALU.add).then_inc(moved, 1)
    return epilogue


def solve(core, name, n, lt, xt, sign):
    nc = core.nc
    LANES = 4
    assert n % LANES == 0
    with core.stage(name) as st:
        joins = st.sb("joins", [P, LEVELS, P])
        mt = st.sb("mt", [P, LANES, 2, P])
        y = st.sb("y", [P, LANES, P])
        x = st.sb("x", [P, LANES, 2, P])
        tables, masked, multiplied, copied, squared, grown, finished = (st.sem(s) for s in (
            "tables", "masked", "multiplied", "copied", "squared", "grown", "finished"))
        steps = [(w, k, lane) for w in range(n // LANES) for k in range(LEVELS) for lane in range(LANES)]
        op = ALU.subtract if sign > 0 else ALU.add

        @st.block.sync
        def _(sp):
            sp.dma_start(joins[:], core.dram["joins"]).then_inc(tables, 16)

        @st.block.gpsimd
        def _(pool):
            pool.wait_ge(tables, 16)
            for i, (w, k, lane) in enumerate(steps):
                if i >= 2 * LANES:
                    pool.wait_ge(multiplied, i - 2 * LANES + 1)
                    pool.wait_ge(grown, i - 2 * LANES + 1)
                nc.gpsimd.tensor_tensor(mt[:, lane, k % 2 if w % 2 == 0 else (k + 1) % 2, :], lt(w * LANES + lane),
                                        joins[:, k, :], ALU.mult).then_inc(masked, 1)

        def slot(w, k):
            return (w * LEVELS + k) % 2

        @st.block.tensor
        def _(pe):
            for w in range(n // LANES):
                for k in range(LEVELS):
                    for part in range(2):
                        for lane in range(LANES):
                            i = (w * LEVELS + k) * LANES + lane
                            if part == 0:
                                pe.wait_ge(masked, i + 1)
                                if i >= LANES:
                                    pe.wait_ge(grown, i - LANES + 1)
                                    pe.wait_ge(copied, i - LANES + 1)
                                rhs = x[:, lane, 0, :] if k else core.ident[:]
                                nc.tensor.matmul(core.psum[:, lane, 0:P], mt[:, lane, slot(w, k), :], rhs, start=True, stop=True
                                                 ).then_inc(multiplied, 1)
                            elif k:
                                pe.wait_ge(copied, i + 1)
                                if k < LEVELS - 1:
                                    nc.tensor.matmul(core.psum[:, 4 + lane, 0:P], x[:, lane, 1, :], y[:, lane, :],
                                                     start=True, stop=True)
                                nc.tensor.matmul(core.psum[:, 4 + lane, P:2 * P], y[:, lane, :], x[:, lane, 1, :],
                                                 start=True, stop=True).then_inc(squared, 1)

        @st.block.scalar
        def _(act):
            for i, (w, k, lane) in enumerate(steps):
                act.wait_ge(multiplied, i + 1)
                if i >= LANES:
                    act.wait_ge(grown, i - LANES + 1)
                nc.scalar.activation(y[:, lane, :], core.psum[:, lane, 0:P], ACT.Copy).then_inc(copied, 1)

        @st.block.vector
        def _(dve):
            for i, (w, k, lane) in enumerate(steps):
                both = x[:, lane, :, :].rearrange("p a b -> p (a b)")
                if k == 0:
                    dve.wait_ge(copied, i + 1)
                    if w:
                        dve.wait_ge(grown, i - LANES + 1)
                    nc.vector.tensor_tensor(x[:, lane, 0, :], core.ident[:], y[:, lane, :], op).then_inc(finished, 1)
                    nc.vector.tensor_tensor(x[:, lane, 1, :], core.ident[:], mt[:, lane, slot(w, k), :], op).then_inc(grown, 1)
                elif k < LEVELS - 1:
                    dve.wait_ge(squared, w * (LEVELS - 1) * LANES + (k - 1) * LANES + lane + 1)
                    nc.vector.tensor_tensor(both, both, core.psum[:, 4 + lane, 0:2 * P], op).then_inc(grown, 1)
                else:
                    dve.wait_ge(squared, w * (LEVELS - 1) * LANES + (k - 1) * LANES + lane + 1)
                    nc.vector.tensor_tensor(xt(w * LANES + lane), x[:, lane, 1, :], core.psum[:, 4 + lane, P:2 * P], op
                                            ).then_inc(grown, 1)


def rwkv_gates(core, p, sw, a, g):
    nc = core.nc
    with core.stage("rwkv_gates") as st:
        wa, g2 = st.sb("wa", [P, T]), st.sb("g2", [P, T])
        loaded, squashed, logits, out = (st.sem(s) for s in ("loaded", "squashed", "logits", "out"))

        @st.block.sync
        def _(sp):
            sp.dma_start(wa[:], core.dram["rwkv_w2_a2"]).then_inc(loaded, 16)
            sp.dma_start(g2[:], core.dram["rwkv_g2"]).then_inc(loaded, 16)

        @st.block.scalar
        def _(act):
            nc.scalar.activation(p[0:64, 12, :], p[0:64, 12, :], ACT.Tanh).then_inc(squashed, 1)
            nc.scalar.activation(p[:, 13, :], p[:, 13, :], ACT.Sigmoid).then_inc(squashed, 1)
            for i in range(4):
                act.wait_ge(logits, 3 * i + 3)
                nc.scalar.activation(sw[:, i, :], core.bank(3 * i % 6), ACT.Sigmoid, bias=core.col("rwkv_w0", i)).then_inc(out, 1)
                nc.scalar.activation(a[:, i, :], core.bank((3 * i + 1) % 6), ACT.Sigmoid, bias=core.col("rwkv_a0", i)).then_inc(out, 1)
                nc.scalar.activation(g[:, i, :], core.bank((3 * i + 2) % 6), ACT.Copy).then_inc(out, 1)

        @st.block.tensor
        def _(pe):
            pe.wait_ge(loaded, 32)
            pe.wait_ge(squashed, 2)
            for i in range(4):
                c = slice(i * P, (i + 1) * P)
                if i >= 2:
                    pe.wait_ge(out, 3 * (i - 1))
                for j, (w, x) in enumerate(((wa[0:64, c], p[0:64, 12, :]), (wa[64:128, c], p[64:128, 12, :]), (g2[:, c], p[:, 13, :]))):
                    nc.tensor.matmul(core.bank((3 * i + j) % 6), w, x, start=True, stop=True).then_inc(logits, 1)


def rwkv_operands(core, p, sw, a, kk, cum, ar, bh, kh, carry, blocks):
    nc = core.nc
    rate = math.exp(-0.5)
    with core.stage("rwkv_operands") as st:
        tmp = st.sb("tmp", [P, 4, T])
        tmp2 = st.sb("tmp2", [P, 4, T])
        d1, d2 = st.sem("d1"), st.sem("d2")
        scans, exps, bonus = st.sem("scans"), st.sem("exps"), st.sem("bonus")
        halves = st.sem("halves")

        def chunks(x, i):
            return x[:, i, :].rearrange("p (c t) -> p c t", t=P)

        @st.block.vector
        def _(dve):
            m = Marks(d1)
            for i in range(4):
                n = m.mark(nc.vector.tensor_scalar(tmp[:, i, :], a[:, i, :], 1.0, core.col("rwkv_k_a", i), ALU.subtract, ALU.mult))
                used = m.mark(nc.vector.tensor_tensor(bh[:, i, :], kk[:, i, :], a[:, i, :], ALU.mult))
                dve.wait_ge(d1, n)
                n = m.mark(nc.vector.scalar_tensor_tensor(out=p[:, 4 + i, :], in0=tmp[:, i, :], scalar=1.0, in1=p[:, 4 + i, :],
                                                          op0=ALU.add, op1=ALU.mult))
                dve.wait_ge(d1, used)
                n2 = m.mark(nc.vector.tensor_scalar(a[:, i, :], sw[:, i, :], -rate, None, ALU.mult))
                dve.wait_ge(d1, n2)
                for c in range(NT):
                    s = slice(c * P, (c + 1) * P)
                    n = m.mark(nc.vector.tensor_tensor_scan(cum[:, i, s], core.ones[:], a[:, i, s], 0.0, ALU.mult, ALU.add))
                dve.wait_ge(d1, n)
                mid = chunks(cum, i)[:, :, 63:64].to_broadcast([P, NT, P])
                n = m.mark(nc.vector.tensor_tensor(chunks(tmp, i), chunks(cum, i), mid, ALU.subtract))
                dve.wait_ge(d1, n)
                n = m.mark(nc.vector.tensor_tensor(tmp2[:, i, :], tmp[:, i, :], a[:, i, :], ALU.subtract))
                n = m.mark(nc.vector.tensor_copy(carry[:, :, i:i + 1], chunks(tmp, i)[:, :, P - 1:P]))
                dve.wait_ge(d1, n)
                n = m.mark(nc.vector.tensor_tensor(carry[:, 0:NT - 1, i:i + 1], carry[:, 0:NT - 1, i:i + 1],
                                                   chunks(cum, i)[:, 1:NT, 63:64], ALU.add))
                dve.wait_ge(d1, n)
                nc.vector.scalar_tensor_tensor(out=sw[:, i, :], in0=p[:, i, :], scalar=core.col("rwkv_r_k", i),
                                               in1=p[:, 4 + i, :], op0=ALU.mult, op1=ALU.mult).then_inc(scans, 1)
            for i in range(4):
                dve.wait_ge(exps, 4 * i + 4)
                r_part, a_part = ar[:, i, :, 1, :], ar[:, i, :, 0, :]
                nc.vector.scalar_tensor_tensor(out=a_part, in0=chunks(kk, i), scalar=-1.0, in1=chunks(tmp2, i), op0=ALU.mult,
                                               op1=ALU.mult).then_inc(d2, 1)
                nc.vector.tensor_tensor(r_part, chunks(p, i), chunks(tmp, i), ALU.mult).then_inc(d2, 1)
                nc.vector.tensor_tensor(bh[:, i, :], bh[:, i, :], cum[:, i, :], ALU.mult).then_inc(d2, 1)
                nc.vector.tensor_tensor(kh[:, i, :], p[:, 4 + i, :], cum[:, i, :], ALU.mult).then_inc(d2, 1)
            for i in range(4):
                dve.wait_ge(bonus, i + 1)
                dve.wait_ge(d2, 4 * i + 2)
                nc.vector.tensor_tensor(p[:, i, :], core.bank(i), p[:, 8 + i, :], ALU.mult).then_inc(halves, 1)

        @st.block.tensor
        def _(pe):
            for i in range(4):
                pe.wait_ge(scans, i + 1)
                nc.tensor.matmul(core.bank(i), blocks, sw[:, i, :], start=True, stop=True).then_inc(bonus, 1)

        @st.block.scalar
        def _(act):
            for i in range(4):
                act.wait_ge(scans, i + 1)
                nc.scalar.activation(cum[:, i, :], tmp[:, i, :], ACT.Exp, scale=-1.0).then_inc(exps, 1)
                act.wait_ge(exps, 4 * i + 1)
                nc.scalar.activation(tmp[:, i, :], tmp[:, i, :], ACT.Exp).then_inc(exps, 1)
                nc.scalar.activation(tmp2[:, i, :], tmp2[:, i, :], ACT.Exp).then_inc(exps, 1)
                nc.scalar.activation(carry[:, :, i:i + 1], carry[:, :, i:i + 1], ACT.Exp).then_inc(exps, 1)


def rwkv_chunk(core, c, ar, bh, kh, vt, bt, kt, state, carry, y, masks):
    nc = core.nc
    H = 8
    s = slice(c * P, (c + 1) * P)
    with buffers(core) as b:
        pairs = b.sb(f"wkv_pairs{c}", [P, H, 4, P])
        xt = b.sb(f"wkv_xt{c}", [P, H, P])

        with core.stage(f"wkv_pairs_{c}") as st:
            multiplied, masked = st.sem("multiplied"), st.sem("masked")

            @st.block.tensor
            def _(pe):
                for h in range(H):
                    r, i = slice(64 * (h % 2), 64 * (h % 2) + 64), h // 2
                    both = ar[r, i, c, :, :].rearrange("p a t -> p (a t)")
                    nc.tensor.matmul(core.psum[:, h, 0:256], bh[r, i, s], both, start=True, stop=True)
                    nc.tensor.matmul(core.psum[:, h, 256:512], kh[r, i, s], both, start=True, stop=True).then_inc(multiplied, 1)

            @st.block.vector
            def _(dve):
                for h in range(H):
                    dve.wait_ge(multiplied, h + 1)
                    nc.vector.tensor_tensor(pairs[:, h, :, :].rearrange("p a t -> p (a t)"), core.bank(h), masks, ALU.mult
                                            ).then_inc(masked, 1)

        solve(core, f"wkv_solve{c}", H, lambda u: pairs[:, u, 0, :], lambda u: xt[:, u, :], -1)

        with core.stage(f"wkv_scan{c}") as st:
            z, u_ = st.sb("z", [P, H, 64]), st.sb("u", [P, H, 64])
            first, zc, second, uc, mixed, stored_, grew, added_, scaled = (st.sem(n) for n in (
                "first", "z_copied", "second", "u_copied", "mixed", "stored", "grew", "added", "scaled"))

            @st.block.tensor
            def _(pe):
                for phase, h in skewed(H, 3):
                    r, i = slice(64 * (h % 2), 64 * (h % 2) + 64), h // 2
                    v = vt[:, c, h * 64:(h + 1) * 64]
                    if phase == 0:
                        if h >= 2:
                            pe.wait_ge(zc, h - 1)
                        out = core.psum[:, h % 2, 0:64]
                        if c:
                            nc.tensor.matmul(out, ar[r, i, c, 0, :], state[r, i, :], start=True, stop=False)
                        nc.tensor.matmul(out, pairs[:, h, 2, :], v, start=(c == 0), stop=True).then_inc(first, 1)
                    elif phase == 1:
                        pe.wait_ge(zc, h + 1)
                        if h >= 2:
                            pe.wait_ge(uc, h - 1)
                        nc.tensor.matmul(core.psum[:, 2 + h % 2, 0:64], xt[:, h, :], z[:, h, :], start=True, stop=True
                                         ).then_inc(second, 1)
                    else:
                        pe.wait_ge(uc, h + 1)
                        if h >= 4:
                            pe.wait_ge(stored_, i - 1)
                        out = core.psum[r, 4 + i % 2, 0:P]
                        if c:
                            nc.tensor.matmul(out, state[r, i, :], ar[r, i, c, 1, :], start=True, stop=False)
                        nc.tensor.matmul(out, u_[:, h, :], pairs[:, h, 1, :], start=(c == 0), stop=False)
                        nc.tensor.matmul(out, v, pairs[:, h, 3, :], start=False, stop=True).then_inc(mixed, 1)
                        if c < NT - 1:
                            if h >= 4:
                                pe.wait_ge(added_, i - 1)
                            out = core.psum[r, 6 + i % 2, 0:64]
                            nc.tensor.matmul(out, bt[:, c, h * 64:(h + 1) * 64], u_[:, h, :], start=True, stop=False)
                            nc.tensor.matmul(out, kt[:, c, h * 64:(h + 1) * 64], v, start=False, stop=True).then_inc(grew, 1)

            @st.block.scalar
            def _(act):
                for phase, h in skewed(H, 3):
                    if phase == 0:
                        act.wait_ge(first, h + 1)
                        nc.scalar.activation(z[:, h, :], core.psum[:, h % 2, 0:64], ACT.Copy).then_inc(zc, 1)
                    elif phase == 1:
                        act.wait_ge(second, h + 1)
                        nc.scalar.activation(u_[:, h, :], core.psum[:, 2 + h % 2, 0:64], ACT.Copy).then_inc(uc, 1)
                    elif h % 2:
                        act.wait_ge(mixed, h + 1)
                        nc.scalar.activation(y[:, h // 2, s], core.psum[:, 4 + h // 2 % 2, 0:P], ACT.Copy).then_inc(stored_, 1)

            @st.block.vector
            def _(dve):
                if c < NT - 1:
                    for i in range(H // 2):
                        dve.wait_ge(grew, 2 * i + 2)
                        dve.wait_ge(mixed, 2 * i + 2)
                        x = state[:, i, :]
                        if c:
                            nc.vector.tensor_tensor(x, core.psum[:, 6 + i % 2, 0:64], x, ALU.add).then_inc(added_, 1)
                        else:
                            nc.vector.tensor_copy(x, core.psum[:, 6 + i % 2, 0:64]).then_inc(added_, 1)
                        dve.wait_ge(added_, i + 1)
                        nc.vector.tensor_scalar(x, x, carry[:, c, i:i + 1], None, ALU.mult).then_inc(scaled, 1)


def scaled_columns(core, name, n, out, x, col):
    nc = core.nc
    with core.stage(name) as st:
        done = st.sem("done")

        @st.block.vector
        def _(dve):
            for i in range(n):
                nc.vector.tensor_scalar(out(i), x(i), col(i), None, ALU.mult).then_inc(done, 1)


def rwkv(core, p, y):
    with buffers(core) as b:
        g, blocks = b.sb("rwkv_g", [P, 4, T]), b.sb("blocks", [P, P])
        mean64, masks = b.sb("mean64", [P, P]), b.sb("wkv_masks", [P, T])
        fill(core, "rwkv_tables", [], [(blocks, "blocks64"), (mean64, "mean64"), (masks, "wkv_masks")])
        with buffers(core) as c:
            ar, bh, kh = c.sb("wkv_ar", [P, 4, NT, 2, P]), c.sb("wkv_b", [P, 4, T]), c.sb("wkv_k", [P, 4, T])
            carry = c.sb("wkv_carry", [P, NT, 4])
            with buffers(core) as d:
                kk = d.sb("rwkv_kk", [P, 4, T])
                sw, a, cum = d.sb("rwkv_sw", [P, 4, T]), d.sb("rwkv_a", [P, 4, T]), d.sb("rwkv_cum", [P, 4, T])
                rwkv_gates(core, p, sw, a, g)
                scaled_columns(core, "rwkv_kk_", 4, lambda i: kk[:, i, :], lambda i: p[:, 4 + i, :], lambda i: core.col("rwkv_k_k", i))
                norm(core, "rwkv_l2", lambda i: kk[:, i, :], [[i] for i in range(4)], blocks[:], lambda i: kk[:, i, :], core.col("eps"))
                rwkv_operands(core, p, sw, a, kk, cum, ar, bh, kh, carry, blocks[:])
            with buffers(core) as d:
                vt, bt, kt = p[:, 4:8, :], d.sb("wkv_bt", [P, NT, T]), d.sb("wkv_kt", [P, NT, T])
                state = d.sb("wkv_state", [P, 4, 64])
                jobs = [([x[:, t + i, ch * P:(ch + 1) * P] for i in range(4)], out[:, ch, :])
                        for x, t, out in ((p, 8, vt), (bh, 0, bt), (kh, 0, kt)) for ch in range(NT)]
                turned(core, "wkv_turn", jobs)
                for ch in range(NT):
                    rwkv_chunk(core, ch, ar, bh, kh, vt, bt, kt, state, carry, y, masks[:])
        norm(core, "rwkv_gn", lambda i: y[:, i, :], [[i] for i in range(4)], mean64[:], lambda i: y[:, i, :],
             core.col("gn_eps"), gain=lambda i: core.col("rwkv_ln_w", i), shift=lambda i: core.col("rwkv_ln_b", i),
             center=mean64[:])
        nc = core.nc
        with core.stage("rwkv_out") as st:
            summed, done = st.sem("summed"), st.sem("done")

            @st.block.vector
            def _(dve):
                for i in range(4):
                    nc.vector.tensor_tensor(y[:, i, :], y[:, i, :], p[:, i, :], ALU.add).then_inc(summed, 1)
                    dve.wait_ge(summed, i + 1)
                    nc.vector.tensor_tensor(y[:, i, :], y[:, i, :], g[:, i, :], ALU.mult).then_inc(done, 1)


def gated_delta(core, qkv, ab, y):
    nc = core.nc
    H = 4
    U = NT * H
    scale = 128.0 ** -0.5
    with buffers(core) as b:
        beta, ga, acs, ein, dec, etot, eneg = (b.sb(f"gdn_{n}", [P, NT, H]) for n in ("beta", "ga", "acs", "ein", "dec", "etot", "be"))
        upper, strict, masked = b.sb("gdn_upper", [P, P]), b.sb("gdn_strict", [P, P]), b.sb("gdn_masked", [P, P])
        vt, kt = b.sb("gdn_vt", [P, NT, T]), b.sb("gdn_kt", [P, NT, T])
        lt, att, qd, xt = (b.sb(f"gdn_{n}", [P, U, P]) for n in ("lt", "att", "qd", "xt"))
        fill(core, "gdn_tables", [], [(upper, "upper"), (strict, "strict_upper"), (masked, "lower_masked")])
        for n, t in (("q", 0), ("k", 4)):
            norm(core, f"gdn_l2{n}", lambda i, t=t: qkv[:, t + i, :], [[i] for i in range(4)], core.ones[:],
                 lambda i, t=t: qkv[:, t + i, :], core.col("eps"))
        turned(core, "gdn_turn", [([qkv[:, t + i, c * P:(c + 1) * P] for i in range(4)], out[:, c, :])
                                  for t, out in ((8, vt), (4, kt)) for c in range(NT)])

        with core.stage("gdn_rates") as st:
            tmp, rate = st.sb("tmp", [P, NT, H]), st.sb("rate", [P, NT * H])
            dve_done, act_done, pe_done = st.sem("dve_done"), st.sem("act_done"), st.sem("pe_done")

            def flat(x):
                return x[:].rearrange("p c h -> p (c h)")

            @st.block.vector
            def _(dve):
                nc.vector.tensor_tensor(ga[:], ab[:, :, 0:4], core.colblock("gdn_dt_bias").rearrange("p (c h) -> p c h", h=H), ALU.add
                                        ).then_inc(dve_done, 1)
                dve.wait_ge(act_done, 5)
                nc.vector.scalar_tensor_tensor(out=flat(ga), in0=flat(ga), scalar=0.0, in1=flat(tmp), op0=ALU.max, op1=ALU.add
                                               ).then_inc(dve_done, 1)
                dve.wait_ge(dve_done, 2)
                nc.vector.scalar_tensor_tensor(out=flat(ga), in0=flat(ga), scalar=-1.0, in1=rate[:], op0=ALU.mult, op1=ALU.mult
                                               ).then_inc(dve_done, 1)
                dve.wait_ge(pe_done, 2)
                nc.vector.tensor_copy(flat(acs), core.psum[:, 0, 0:U]).then_inc(dve_done, 1)
                dve.wait_ge(dve_done, 4)
                nc.vector.tensor_tensor(flat(dec), core.psum[:, 1, 0:U], flat(acs), ALU.subtract).then_inc(dve_done, 1)
                dve.wait_ge(act_done, 6)
                nc.vector.tensor_tensor(flat(eneg), flat(ein), flat(beta), ALU.mult).then_inc(dve_done, 1)

            @st.block.scalar
            def _(act):
                nc.scalar.activation(beta[:], ab[:, :, 4:8], ACT.Sigmoid).then_inc(act_done, 1)
                nc.scalar.activation(rate[:], core.colblock("gdn_a_log"), ACT.Exp).then_inc(act_done, 1)
                act.wait_ge(dve_done, 1)
                nc.scalar.activation(tmp[:], ga[:], ACT.Abs).then_inc(act_done, 1)
                act.wait_ge(act_done, 3)
                nc.scalar.activation(tmp[:], tmp[:], ACT.Exp, scale=-1.0).then_inc(act_done, 1)
                act.wait_ge(act_done, 4)
                nc.scalar.activation(tmp[:], tmp[:], ACT.Ln, bias=core.col("one")).then_inc(act_done, 1)
                act.wait_ge(dve_done, 5)
                nc.scalar.activation(flat(ein), flat(acs), ACT.Exp).then_inc(act_done, 1)
                nc.scalar.activation(flat(dec), flat(dec), ACT.Exp).then_inc(act_done, 1)
                nc.scalar.activation(flat(etot), core.psum[:, 1, 0:U], ACT.Exp).then_inc(act_done, 1)

            @st.block.tensor
            def _(pe):
                pe.wait_ge(dve_done, 3)
                nc.tensor.matmul(core.psum[:, 0, 0:U], upper[:], flat(ga), start=True, stop=True).then_inc(pe_done, 1)
                nc.tensor.matmul(core.psum[:, 1, 0:U], core.ones[:], flat(ga), start=True, stop=True).then_inc(pe_done, 1)

        with core.stage("gdn_pairs") as st:
            R = 3
            decay, row_in, beta_row = st.sb("decay", [P, R, P]), st.sb("row_in", [P, R, P]), st.sb("beta_row", [P, R, P])
            rows_done, diffed, read, exped, pairs_done, part, finished = (st.sem(s) for s in (
                "rows_done", "diffed", "read", "exped", "pairs_done", "part", "finished"))

            @st.block.tensor
            def _(pe):
                for u in range(U):
                    c, h, s = u // H, u % H, slice(u // H * P, (u // H + 1) * P)
                    if u >= 2:
                        pe.wait_ge(read, u - 1)
                    fga, fb = ga[:, c, h:h + 1].to_broadcast([P, P]), beta[:, c, h:h + 1].to_broadcast([P, P])
                    nc.tensor.matmul(core.psum[:, u % 2, 0:P], fga, upper[:], start=True, stop=True)
                    nc.tensor.matmul(core.psum[:, u % 2, P:2 * P], fb, core.ident[:], start=True, stop=True).then_inc(rows_done, 1)
                    if u >= 2:
                        pe.wait_ge(finished, 2 * (u - 1))
                    k = qkv[:, 4 + h, s]
                    nc.tensor.matmul(core.psum[:, 2 + u % 2, 0:P], k, k, start=True, stop=True)
                    nc.tensor.matmul(core.psum[:, 2 + u % 2, P:2 * P], k, qkv[:, h, s], start=True, stop=True).then_inc(pairs_done, 1)

            @st.block.vector
            def _(dve):
                for phase, u in skewed(U, 2):
                    c, h, s = u // H, u % H, slice(u // H * P, (u // H + 1) * P)
                    if phase == 0:
                        dve.wait_ge(rows_done, u + 1)
                        if u >= R:
                            dve.wait_ge(finished, 2 * (u - R + 1))
                        nc.vector.scalar_tensor_tensor(out=decay[:, u % R, :], in0=core.psum[:, u % 2, 0:P],
                                                       scalar=acs[:, c, h:h + 1], in1=masked[:], op0=ALU.subtract, op1=ALU.add
                                                       ).then_inc(diffed, 1)
                        nc.vector.tensor_tensor(beta_row[:, u % R, :], core.psum[:, u % 2, P:2 * P], strict[:], ALU.mult
                                                ).then_inc(diffed, 1)
                    else:
                        dve.wait_ge(exped, u + 1)
                        dve.wait_ge(pairs_done, u + 1)
                        d = decay[:, u % R, :]
                        nc.vector.tensor_tensor(lt[:, u, :], core.psum[:, 2 + u % 2, 0:P], d, ALU.mult).then_inc(part, 1)
                        nc.vector.scalar_tensor_tensor(out=att[:, u, :], in0=core.psum[:, 2 + u % 2, P:2 * P], scalar=scale, in1=d,
                                                       op0=ALU.mult, op1=ALU.mult).then_inc(finished, 1)
                        dve.wait_ge(part, 2 * u + 1)
                        nc.vector.tensor_tensor(lt[:, u, :], lt[:, u, :], beta_row[:, u % R, :], ALU.mult).then_inc(finished, 1)
                        dve.wait_ge(read, u + 1)
                        nc.vector.scalar_tensor_tensor(out=qd[:, u, :], in0=qkv[:, h, s], scalar=scale, in1=row_in[:, u % R, :],
                                                       op0=ALU.mult, op1=ALU.mult).then_inc(part, 1)

            @st.block.scalar
            def _(act):
                for u in range(U):
                    act.wait_ge(diffed, 2 * u + 2)
                    if u >= R:
                        act.wait_ge(part, 2 * (u - R + 1))
                    nc.scalar.activation(row_in[:, u % R, :], core.psum[:, u % 2, 0:P], ACT.Exp).then_inc(read, 1)
                    nc.scalar.activation(decay[:, u % R, :], decay[:, u % R, :], ACT.Exp).then_inc(exped, 1)

        solve(core, "gdn_solve", U, lambda u: lt[:, u, :], lambda u: xt[:, u, :], 1)

        uu = b.sb("gdn_u", [P, U, P])
        with core.stage("gdn_apply") as st:
            vb, kb = st.sb("vb", [P, 2, P]), st.sb("kb", [P, 2, P])
            ready, multiplied, out = st.sem("ready"), st.sem("multiplied"), st.sem("out")

            @st.block.vector
            def _(dve):
                for u in range(U):
                    c, h = u // H, u % H
                    if u >= 2:
                        dve.wait_ge(multiplied, u - 1)
                    nc.vector.tensor_scalar(vb[:, u % 2, :], vt[:, c, h * P:(h + 1) * P], beta[:, c, h:h + 1], None, ALU.mult
                                            ).then_inc(ready, 1)
                    nc.vector.tensor_scalar(kb[:, u % 2, :], kt[:, c, h * P:(h + 1) * P], eneg[:, c, h:h + 1], None, ALU.mult
                                            ).then_inc(ready, 1)
                    dve.wait_ge(ready, 2 * u + 2)

            @st.block.tensor
            def _(pe):
                for u in range(U):
                    pe.wait_ge(ready, 2 * u + 2)
                    if u >= 4:
                        pe.wait_ge(out, 2 * (u - 3))
                    nc.tensor.matmul(core.psum[:, u % 4, 0:P], xt[:, u, :], vb[:, u % 2, :], start=True, stop=True)
                    nc.tensor.matmul(core.psum[:, u % 4, P:2 * P], kb[:, u % 2, :], xt[:, u, :], start=True, stop=True
                                     ).then_inc(multiplied, 1)

            @st.block.scalar
            def _(act):
                for u in range(U):
                    act.wait_ge(multiplied, u + 1)
                    nc.scalar.activation(uu[:, u, :], core.psum[:, u % 4, 0:P], ACT.Copy).then_inc(out, 1)
                    nc.scalar.activation(lt[:, u, :], core.psum[:, u % 4, P:2 * P], ACT.Copy).then_inc(out, 1)

        with core.stage("gdn_scan") as st:
            state = st.sb("state", [P, H, P])
            kd = st.sb("kd", [P, 4, P])
            zeroed, decayed, first, renewed, mixed, stored_, added_, updated = (st.sem(s) for s in (
                "zeroed", "decayed", "first", "renewed", "mixed", "stored", "added", "updated"))

            @st.block.tensor
            def _(pe):
                for phase, u in skewed(U, 2):
                    c, h = u // H, u % H
                    if phase == 0:
                        if u == 0:
                            pe.wait_ge(zeroed, 1)
                        if u >= 2:
                            pe.wait_ge(renewed, u - 1)
                        if c:
                            pe.wait_ge(updated, u - H + 1)
                        nc.tensor.matmul(core.psum[:, u % 2, 0:P], lt[:, u, :], state[:, h, :], start=True, stop=True).then_inc(first, 1)
                    else:
                        pe.wait_ge(renewed, u + 1)
                        if u >= 2:
                            pe.wait_ge(stored_, u - 1)
                            pe.wait_ge(updated, u - 1)
                        nc.tensor.matmul(core.psum[:, 2 + u % 2, 0:P], state[:, h, :], qd[:, u, :], start=True, stop=False)
                        nc.tensor.matmul(core.psum[:, 2 + u % 2, 0:P], uu[:, u, :], att[:, u, :], start=False, stop=True
                                         ).then_inc(mixed, 1)
                        pe.wait_ge(decayed, u + 1)
                        nc.tensor.matmul(core.psum[:, 4 + u % 2, 0:P], kd[:, u % 4, :], uu[:, u, :], start=True, stop=True
                                         ).then_inc(added_, 1)

            @st.block.vector
            def _(dve):
                nc.vector.memset(state[:], 0.0).then_inc(zeroed, 1)
                for phase, u in skewed(U, 2):
                    c, h = u // H, u % H
                    if phase == 0:
                        dve.wait_ge(first, u + 1)
                        nc.vector.tensor_tensor(uu[:, u, :], uu[:, u, :], core.psum[:, u % 2, 0:P], ALU.subtract).then_inc(renewed, 1)
                    else:
                        dve.wait_ge(added_, u + 1)
                        dve.wait_ge(mixed, u + 1)
                        nc.vector.scalar_tensor_tensor(out=state[:, h, :], in0=state[:, h, :], scalar=etot[:, c, h:h + 1],
                                                       in1=core.psum[:, 4 + u % 2, 0:P], op0=ALU.mult, op1=ALU.add
                                                       ).then_inc(updated, 1)

            @st.block.scalar
            def _(act):
                for phase, u in skewed(U, 2):
                    c, h = u // H, u % H
                    if phase == 0:
                        if u >= 4:
                            act.wait_ge(added_, u - 3)
                        nc.scalar.activation(kd[:, u % 4, :], kt[:, c, h * P:(h + 1) * P], ACT.Copy, scale=dec[:, c, h:h + 1]
                                             ).then_inc(decayed, 1)
                    else:
                        act.wait_ge(mixed, u + 1)
                        nc.scalar.activation(y[:, h, c * P:(c + 1) * P], core.psum[:, 2 + u % 2, 0:P], ACT.Copy).then_inc(stored_, 1)


def block3(core, xT, mean):
    with buffers(core) as b:
        h, ya = b.pair("b3_h", KD), b.sb("b3_ya", [P, 4, T])
        norm(core, "b3_pre", lambda i: xT[:, i, :], [list(range(KD))], mean, None, core.col("eps"),
             gain=lambda i: core.col("b3_norm1_g", i), pair=h)
        with buffers(core) as c:
            p = c.sb("rwkv_p", [P, 14, T])
            linear(core, "b3_p", h, token_shifted(lambda i: core.col("rwkv_mu", i), lambda i: p[:, i, :]))
            rwkv(core, p, ya)
        yb = b.sb("b3_yb", [P, 4, T])
        with buffers(core) as c:
            zT = c.sb("gdn_z", [P, 4, T])
            with buffers(core) as d:
                qkv, ab = d.sb("gdn_qkv", [P, 12, T]), d.sb("gdn_ab", [P, NT, 8])
                linear(core, "b3_qkv", h, convolved(4, lambda i, j: core.col("gdn_conv_w", 4 * i + j),
                                                    lambda i: core.col("zero"), lambda i, at: qkv[:, i, :]))
                linear(core, "b3_z", h, stored(lambda i, at: zT[:, i, :], ACT.Silu))
                linear(core, "b3_ab", h, stored(lambda i, at: ab[:, i, :]), by_tokens=True)
                gated_delta(core, qkv, ab, yb)
            m128 = c.sb("mean128", [P, P])
            fill(core, "gdn_m128", [(m128, 1.0 / 128)])
            norm(core, "gdn_norm", lambda i: yb[:, i, :], [[i] for i in range(4)], m128[:], lambda i: yb[:, i, :],
                 core.col("eps"), gain=lambda i: core.col("gdn_norm_w"), times=lambda i: zT[:, i, :])
        with buffers(core) as c:
            gT, mixed = c.sb("b3_gates", [P, KD, T]), c.sb("b3_mixed", [P, KD, T])
            gate, mix = (lambda i: gT[:, i, :]), (lambda i: mixed[:, i, :])
            linear(core, "b3_ga", h, stored(lambda i, at: gT[:, i, :], ACT.Sigmoid))
            linear(core, "b3_rproj", lambda k: ya[:, k, :], scaled_to(mix, gate), raw=True)
            linear(core, "b3_gb", h, stored(lambda i, at: gT[:, i, :], ACT.Sigmoid))
            linear(core, "b3_gproj", lambda k: yb[:, k, :], added(mix, gate), raw=True)
            linear(core, "b3_out", lambda k: mixed[:, k, :], added(lambda i: xT[:, i, :]), raw=True)
    conv_ffn(core, "b3", xT, mean)


def tiles_of(v):
    return v.reshape(-1, P).T


def taps_of(w):
    taps, f = w.shape
    return w.reshape(taps, f // P, P).transpose(2, 1, 0).reshape(P, -1)


def slabs_of(w, cols):
    k, f = w.shape
    return np.ascontiguousarray(w.reshape(k // P, P, f // cols, cols).transpose(2, 1, 0, 3).reshape(f // cols, P, -1))


def pairs_of(a, b):
    lead = a.shape[:-1]
    both = np.stack([a.reshape(lead + (-1, P)), b.reshape(lead + (-1, P))], axis=-2)
    return both.reshape(lead + (-1,))


def rows_of(v, times=1):
    return np.broadcast_to(np.tile(v, times)[None], (P, v.size * times))


def zeros(*shape):
    return np.zeros(shape, np.float32)


def weights_of(a):
    w = a["l0_w_in"]
    k1, k2 = w[:, 3216:3232], w[:, 3232:3248]
    low = np.concatenate([w[:, 2576:3216], zeros(D, 64), k1, k2, k2, k1], 1)
    q = a["l0_w_q_b"].reshape(384, 8, 96)
    q = np.concatenate([q[:, :, 0:96], q[:, :, 80:96], q[:, :, 64:80]], 2).reshape(384, 1024)
    kv = a["l0_w_kv_b"].reshape(256, 8, 128)
    out = {
        "l0_ada": (a["l0_ada_w"], 256, P),
        "l0_xbc": (w[:, 1024:2560], 256, P),
        "l0_z": (w[:, 0:1024], 256, P),
        "l0_low": (low, 256, P),
        "l0_dt": (w[:, 2560:2576], 16, 16),
        "l0_q": (q, 512, P),
        "l0_k": (kv[:, :, 0:64].reshape(256, 512), 512, 64),
        "l0_v": (kv[:, :, 64:128].reshape(256, 512), 512, 512),
        "l0_out": (a["l0_w_out"], 128, P),
        "l0_up": (pairs_of(a["l0_w_gate"], a["l0_w_up"]), 256, P),
        "l0_down": (a["l0_w_down"], P, P),
    }
    w = a["l1_w_in"]
    n = 3088
    nq = w[:, n:n + 512].reshape(D, 2, 4, 64).swapaxes(1, 2).reshape(D, 512)
    kc, vc, ks, vs, kw, vw = (w[:, 3600 + 128 * i:3728 + 128 * i] for i in range(6))
    wo = a["l1_w_out"]
    nsa_out = wo[1024:].reshape(2, 4, 64, D).swapaxes(0, 1).reshape(512, D)
    out |= {
        "l1_ada": (a["l1_ada_w"], 256, P),
        "l1_qk": (w[:, 0:1024], 256, P),
        "l1_v": (w[:, 1024:2048], 256, 256),
        "l1_lr": (w[:, 2048:2064], 16, 16),
        "l1_gg": (w[:, 2064:3088], 256, P),
        "l1_nf": (np.concatenate([nq, kc, vc, ks, kw], 1), 256, P),
        "l1_nt": (np.concatenate([vs, vw, w[:, 4368:4392]], 1), 280, 280),
        "l1_cmp_k": (a["l1_cmp_k_w1"], 128, P),
        "l1_cmp_v": (a["l1_cmp_v_w1"], 128, P),
        "l1_out": (np.concatenate([wo[:1024], nsa_out], 0), 128, P),
        "l1_up": (pairs_of(a["l1_w_gate"], a["l1_w_up"]), 256, P),
        "l1_down": (a["l1_w_down"], P, P),
    }
    w = a["w_in_2"][0]
    q, k, v, conf_a, conf_gate, sc_b, sc_c, sc_x = (w[:, 768 * i:768 * (i + 1)] for i in range(8))
    threes = np.stack([x.reshape(D, 6, P) for x in (sc_c, sc_x, sc_b)], 2).reshape(D, 2304)
    gates = [w[:, 6144 + D * i:6144 + D * (i + 1)] for i in range(3)]
    out |= {
        "b2_qk": (np.concatenate([q, k], 1), 256, P),
        "b2_v": (v, 256, 256),
        "b2_conf": (pairs_of(conf_gate, conf_a), 256, P),
        "b2_sc": (threes, 256, P),
        "b2_gate0": (gates[0], 256, P),
        "b2_attn_out": (a["w_attn_out_2"][0], 1024, P),
        "b2_gate1": (gates[1], 256, P),
        "b2_conf_out": (a["w_conf_out_2"][0], 256, P),
        "b2_gate2": (gates[2], 256, P),
        "b2_sc_out": (a["w_sc_out_2"][0], 256, P),
        "b2_o": (a["w_o_2"][0], 256, P),
        "b2_up": (pairs_of(*np.split(a["w_up_2"][0], 2, 1)), 256, P),
        "b2_down": (a["w_down_2"][0], P, P),
    }
    w = a["w_in_3"][0]
    out |= {
        "b3_p": (w[:, 0:1792], 256, P),
        "b3_qkv": (w[:, 1792:3328], 256, P),
        "b3_z": (w[:, 3328:3840], 256, P),
        "b3_ab": (w[:, 3840:3848], 8, 8),
        "b3_ga": (w[:, 3848:4872], 256, P),
        "b3_rproj": (a["rwkv_proj_3"][0], 512, P),
        "b3_gb": (w[:, 4872:5896], 256, P),
        "b3_gproj": (a["gdn_proj_3"][0], 512, P),
        "b3_out": (a["w_out_3"][0], 256, P),
        "b3_up": (pairs_of(*np.split(a["ffn_up_3"][0], 2, 1)), 256, P),
        "b3_down": (a["ffn_down_3"][0], P, P),
    }
    return out


def columns_of(a):
    c = {
        "eps": np.full((P, 1), EPS, np.float32), "one": np.ones((P, 1), np.float32),
        "c": tiles_of(a["c"][0]),
        "l0_dt_bias": rows_of(a["l0_dt_bias"], NT), "l0_a_log": rows_of(a["l0_a_log"], NT),
        "l0_d_skip": tiles_of(np.repeat(a["l0_d_skip"], 64)),
        "l0_conv_w": taps_of(a["l0_conv_w"]), "l0_conv_b": tiles_of(a["l0_conv_b"]),
    }
    for n in ("l0_ada_b", "l0_mix_pre_g", "l0_mix_post_g", "l0_ffn_pre_g", "l0_ffn_post_g", "l0_ssm_norm_g",
              "l0_q_a_norm_g", "l0_kv_a_norm_g", "l1_ada_b", "l1_mix_pre_g", "l1_mix_post_g", "l1_ffn_pre_g",
              "l1_ffn_post_g", "l1_b_gk", "l1_gla_norm_g"):
        c[n] = tiles_of(a[n])
    c["l1_cmp_pos"] = a["l1_cmp_pos"].reshape(16, P).T
    c["zero"] = zeros(P, 1)
    c["gn_eps"] = np.full((P, 1), 64e-5, np.float32)
    for n, v in (("b2_norm1_g", "norm1_g_2"), ("b2_conf_b", "conf_dw_b_2"), ("b2_ln_g", "conf_ln_g_2"), ("b2_ln_b", "conf_ln_b_2"),
                 ("b2_norm2_g", "norm2_g_2"), ("b3_norm1_g", "norm1_g_3"), ("rwkv_mu", "rwkv_mu_3"), ("rwkv_w0", "rwkv_w0_3"),
                 ("rwkv_a0", "rwkv_a0_3"), ("rwkv_k_k", "rwkv_k_k_3"), ("rwkv_k_a", "rwkv_k_a_3"), ("rwkv_r_k", "rwkv_r_k_3"),
                 ("rwkv_ln_w", "rwkv_ln_w_3"), ("rwkv_ln_b", "rwkv_ln_b_3"), ("gdn_norm_w", "gdn_norm_w_3"),
                 ("b3_norm2_g", "norm2_g_3")):
        c[n] = tiles_of(a[v][0])
    c["b2_final_g"], c["b3_final_g"] = tiles_of(a["final_g_2"]), tiles_of(a["final_g_3"])
    c["b2_conf_w"], c["b2_sc_w"] = taps_of(a["conf_dw_w_2"][0]), taps_of(a["sc_dw_w_2"][0])
    c["b2_ffn_dw_w"] = taps_of(pairs_of(*np.split(a["ffn_dw_w_2"][0], 2, 1)))
    c["b3_ffn_dw_w"] = taps_of(pairs_of(*np.split(a["ffn_conv_w_3"][0], 2, 1)))
    c["gdn_conv_w"] = taps_of(a["gdn_conv_w_3"][0])
    c["gdn_dt_bias"], c["gdn_a_log"] = rows_of(a["gdn_dt_bias_3"][0], NT), rows_of(a["gdn_a_log_3"][0], NT)
    inv = (10000.0 ** (-np.arange(0, 32, 2) / 32)).astype(np.float32)
    c["rope_inv"] = np.concatenate([np.tile(inv, 8)])[:, None]
    c["rope_sign"] = np.concatenate([np.ones(96), -np.ones(16), np.ones(16)]).astype(np.float32)[:, None]
    return c


def tables_of(a):
    i, j = np.arange(P)[:, None], np.arange(P)[None]
    x = np.arange(T)[None] - (T - P)
    t = {
        "ident": np.eye(P), "upper": i <= j, "lower_masked": np.where(i <= j, 0.0, MASKED),
        "fold": (i % 32 == j % 32) & (i >= 64) & (j >= 64),
        "causal": np.where(x <= i, 0.0, MASKED),
    }
    t["alibi"] = np.where(x <= i, x - i, MASKED)
    token = i + P * np.arange(NT)[:, None, None]
    dist = token - (16 * np.arange(CMP)[None] + 31)
    t["cmp_bias"] = np.where(dist >= 0, -dist, MASKED).swapaxes(0, 1)
    t["cmp_valid"] = (dist >= 0).swapaxes(0, 1)
    t["cmp_w2"] = np.stack([a["l1_cmp_k_w2"][:P], a["l1_cmp_k_w2"][P:], a["l1_cmp_v_w2"][:P], a["l1_cmp_v_w2"][P:]], 1)
    t["gk2"] = a["l1_w_gk2"]
    far, bias = i - x, []
    for g, d in enumerate((1, 4, 16)):
        ok = (far >= 0) & (far % d == 0) & (far <= 128 * d)
        for n in range(4):
            slope = np.exp2(np.float32(-8.0 * (4 * g + n + 1) / 12))
            bias.append(np.where(ok, -slope * far, MASKED))
    t["dilated"] = np.stack(bias, 1)
    t["blocks64"] = i // 64 == j // 64
    t["mean64"] = t["blocks64"] / 64.0
    t["strict_upper"] = i < j
    t["wkv_masks"] = np.concatenate([i < j, i <= j, i < j, i <= j], 1)
    t["joins"] = np.stack([(i // (2 << k) == j // (2 << k)) & (i // (1 << k) % 2 == 0) & (j // (1 << k) % 2 == 1)
                           for k in range(LEVELS)], 1)
    t["rwkv_w2_a2"] = np.concatenate([a["rwkv_w2_3"][0], a["rwkv_a2_3"][0]], 0)
    t["rwkv_g2"] = a["rwkv_g2_3"][0]
    t = {n: np.ascontiguousarray(v, np.float32) for n, v in t.items()}
    t["positions"] = np.ascontiguousarray(np.broadcast_to(a["positions"].reshape(1, T), (P, T)))
    return t


def lay_out(a, only=None):
    arrays, plan, columns, at = {}, [], {}, 0
    for n, (w, cols, gcols) in weights_of(a).items():
        if only is not None and not n.startswith(only):
            continue
        arrays[n] = slabs_of(w, cols)
        plan.append((n, w.shape[1] // cols, w.shape[0] // P, cols, gcols))
    cs = columns_of(a)
    for n, v in cs.items():
        columns[n] = (at, v.shape[1])
        at += v.shape[1]
    arrays["columns"] = np.ascontiguousarray(np.concatenate(list(cs.values()), 1))
    arrays.update(tables_of(a))
    return arrays, plan, columns


def start(core, xT, mean):
    nc = core.nc
    with core.stage("start") as st:
        loaded, filled = st.sem("loaded"), st.sem("filled")

        @st.block.sync
        def _(sp):
            sp.dma_start(core.cols[:], core.dram["columns"]).then_inc(loaded, 16)
            for s in range(RING):
                core.load_slab(sp, s)
            sp.dma_start(core.ident[:], core.dram["ident"]).then_inc(loaded, 16)
            sp.dma_start(xT[:], core.dram["x"].rearrange("(k p) t -> p k t", p=P)).then_inc(loaded, 16)
            sp.wait_ge(loaded, 48)

        @st.block.vector
        def _(dve):
            nc.vector.memset(mean[:], 1.0 / D).then_inc(filled, 1)
            nc.vector.memset(core.ones[:], 1.0).then_inc(filled, 1)


def finish(core, xT, out):
    with core.stage("finish") as st:
        written = st.sem("written")

        @st.block.sync
        def _(sp):
            sp.dma_start(out.rearrange("(k p) t -> p k t", p=P), xT[:]).then_inc(written, 16)
            sp.wait_ge(written, 16)


def silu_of_c(core, silu_c):
    nc = core.nc
    with core.stage("silu_c") as st:
        done = st.sem("done")

        @st.block.scalar
        def _(act):
            nc.scalar.activation(silu_c[:], core.colblock("c"), ACT.Silu).then_inc(done, 1)



def build_program(nc, dram, plan, columns, out):
    with ExitStack() as ctx:
        core = Core(nc, ctx, dram, plan, columns)
        buf = Pool(nc, ctx)
        xT = buf.sb("xT", [P, KD, T])
        mean = buf.sb("mean", [P, P])
        silu_c = buf.sb("silu_of_c", [P, KD])
        start(core, xT, mean)
        silu_of_c(core, silu_c)
        layer0(core, xT, silu_c, mean[:])
        layer1(core, xT, silu_c, mean[:])
        block2(core, xT, mean[:])
        block3(core, xT, mean[:])
        finish(core, xT, out)


def kernel(**inputs):
    import concourse.bacc as bacc
    from concourse.bass_utils import run_bass_kernel_spmd

    a = {name: np.asarray(v) for name, v in inputs.items()}
    arrays, plan, columns = lay_out(a)
    arrays["x"] = np.ascontiguousarray(a["x"][0].T)
    nc = bacc.Bacc("TRN2", target_bir_lowering=False, num_devices=1)
    dram = {name: nc.dram_tensor(f"in_{name}", v.shape, mybir.dt.from_np(v.dtype), kind="ExternalInput").ap()
            for name, v in arrays.items()}
    out = nc.dram_tensor("out_x", (D, T), F32, kind="ExternalOutput").ap()
    build_program(nc, dram, plan, columns, out)
    got = run_bass_kernel_spmd(nc, [{f"in_{name}": v for name, v in arrays.items()}], core_ids=[0])
    return np.ascontiguousarray(got.results[0]["out_x"].T)[None]
```

```python
import math
from contextlib import ExitStack, contextmanager

import numpy as np
import concourse.bass as bass
from concourse import mybir

F32 = mybir.dt.float32
F32R = mybir.dt.float32r
I32 = mybir.dt.int32
ALU = mybir.AluOpType
ACT = mybir.ActivationFunctionType
X_AXIS = mybir.AxisListType.X

P = 128
T = 512
NT = T // P
D = 1024
KD = D // P
BANKS = 8
RING = 3
SLAB = 2816
EPS = 1e-6
MASKED = -1e30


class Core:

    def __init__(self, nc, ctx, dram, plan, columns):
        self.nc, self.dram, self.plan, self.columns = nc, dram, plan, columns
        self.used = []
        self.slabs = [(name, s, kt * cols) for name, n, kt, cols, _ in plan for s in range(n)]
        self.linears = 0
        self.first_slab = 0
        self.psum = ctx.enter_context(nc.psum_tensor("banks", [P, BANKS, 512], F32))
        self.ring = ctx.enter_context(nc.sbuf_tensor("weight_ring", [P, RING, SLAB], F32))
        self.slab_loaded = [ctx.enter_context(nc.semaphore(f"slab_loaded{s}")) for s in range(RING)]
        ncol = sum(n for _, n in columns.values())
        self.cols = ctx.enter_context(nc.sbuf_tensor("columns", [P, ncol], F32))
        self.ident = ctx.enter_context(nc.sbuf_tensor("ident", [P, P], F32))
        self.ones = ctx.enter_context(nc.sbuf_tensor("ones", [P, P], F32))

    def bank(self, b):
        return self.psum[:, b, :]

    def col(self, name, i=0):
        return self.cols[:, self.columns[name][0] + i:self.columns[name][0] + i + 1] if isinstance(i, int) \
            else self.cols[:, bass.ds(i + self.columns[name][0], 1)]

    def colblock(self, name):
        a, n = self.columns[name]
        return self.cols[:, a:a + n]

    @contextmanager
    def stage(self, name):
        nc = self.nc
        with ExitStack() as ctx:
            st = Stage(nc, ctx, name)
            st.block = ctx.enter_context(nc.Block())
            old, self.used = self.used, st.semaphores

            @st.block.gpsimd
            def _(pool):
                for handle in old:
                    pool.sem_clear(handle)

            yield st
        for handle in old:
            nc.release_semaphore(handle)

    def load_slab(self, eng, number):
        if number >= len(self.slabs):
            return
        name, s, words = self.slabs[number]
        eng.dma_start(self.ring[:, number % RING, 0:words], self.dram[name][s]
                      ).then_inc(self.slab_loaded[number % RING], 16)


class Stage:
    def __init__(self, nc, ctx, name):
        self.nc, self.ctx, self.name, self.semaphores = nc, ctx, name, []

    def sb(self, name, shape, dtype=F32):
        return self.ctx.enter_context(self.nc.sbuf_tensor(f"{self.name}_{name}", shape, dtype))

    def sem(self, name):
        handle = self.nc.alloc_semaphore(f"{self.name}_{name}")
        self.semaphores.append(handle)
        return handle


class Marks:

    def __init__(self, semaphore):
        self.semaphore, self.count = semaphore, 0

    def mark(self, instruction):
        instruction.then_inc(self.semaphore, 1)
        self.count += 1
        return self.count


def looped(count, lead):
    return (count - 1) // lead - 1 >= 2


def in_turns(eng, count, lead, body):
    turns = (count - 1) // lead - 1
    if not looped(count, lead):
        for i in range(count):
            body(i, i, None)
        return
    for i in range(lead):
        body(i, i, None)
    with eng.Fori(1, turns + 1) as turn:
        for i in range(lead):
            body(turn * lead + i, lead + i, turn)
    for i in range(lead * (turns + 1), count):
        body(i, i, None)


def lagged(n, lags):
    for s in range(n + max(lags.values())):
        for phase, lag in lags.items():
            if 0 <= s - lag < n:
                yield phase, s - lag


def linear(core, name, source, epilogue, by_tokens=False, width=T, raw=False, room=None,
           straight=False):
    nc = core.nc
    weights, nslab, kt, cols, gcols = core.plan[core.linears]
    assert weights == name, (weights, name)
    first = core.first_slab
    per = NT if by_tokens else cols // gcols
    lead = 2 * RING * per
    banks = 6
    count = nslab * per
    if straight:
        lead = count
    if not looped(count, lead):
        banks = min(BANKS, count)
    cut = raw or isinstance(source, Pair)
    unit = per if by_tokens else 1
    units, ucols = count // unit, (cols if by_tokens else gcols)
    assert not looped(count, lead) or (lead % banks == 0 and lead % (2 * unit) == 0)

    def slab_count(at, turn):
        seen = 16 * ((first + at // per) // RING + 1)
        if turn is None:
            return seen
        return (turn - 1) * (16 * (lead // per) // RING) + seen

    with core.stage(name) as st:
        group_done = st.sem("group_done")
        bank_free = st.sem("bank_free")
        high_cut = st.sem("high_cut")
        low_cut = st.sem("low_cut")
        tile_high, tile_low = st.sem("tile_high"), st.sem("tile_low")
        lows = 1 if by_tokens else 2
        if cut:
            w_high = st.sb("w_high", [P, 2, kt * ucols], F32R)
            w_low = st.sb("w_low", [P, lows, kt * ucols], F32R)
        if room is not None:
            pair = room
        elif raw:
            pair = Pair(st.sb("high", [P, kt, width], F32R), st.sb("low", [P, kt, width], F32R))
        else:
            pair = source

        def slab_columns(at):
            w = core.ring[:, (first + at // per) % RING, 0:kt * cols].rearrange("p (k c) -> p k c", k=kt)
            f = at % per
            return w if by_tokens else w[:, :, f * gcols:(f + 1) * gcols]

        def piece(t, at):
            return t[:, at // unit % (2 if t is w_high else lows), :].rearrange("p (k c) -> p k c", k=kt)

        @st.block.sync
        def _(sp):
            def refill(s, at, turn):
                if cut:
                    sp.wait_ge(high_cut, (s + 1) * (per // unit))
                    sp.wait_ge(low_cut, (s + 1) * (per // unit))
                else:
                    sp.wait_ge(group_done, (s + 1) * per)
                if turn is None:
                    core.load_slab(sp, first + at + RING)
                else:
                    slot = (first + at) % RING
                    sp.dma_start(core.ring[:, slot, 0:kt * cols], core.dram[weights][bass.ds(s + RING, 1)]
                                 ).then_inc(core.slab_loaded[slot], 16)

            inside = max(0, nslab - RING)
            in_turns(sp, inside, RING, refill)
            for s in range(inside, nslab):
                refill(s, s, None)

        def cut_high(act, i, at, turn):
            u = i if unit == 1 else i // unit
            act.wait_ge(core.slab_loaded[(first + at // per) % RING], slab_count(at, turn))
            if at >= 2 * unit:
                act.wait_ge(group_done, (u - 1) * unit)
            nc.scalar.activation(piece(w_high, at), slab_columns(at), ACT.Copy).then_inc(high_cut, 1)

        if cut:
            @st.block.scalar
            def _(act):
                cut_high(act, 0, 0, None)

        if raw:
            @st.block.scalar
            def _(act):
                for k in range(kt):
                    nc.scalar.activation(pair.high[:, k, :], source(k), ACT.Copy).then_inc(tile_high, 1)

            @st.block.vector
            def _(dve):
                for k in range(kt):
                    dve.wait_ge(tile_high, k + 1)
                    nc.vector.tensor_tensor(pair.low[:, k, :], source(k), pair.high[:, k, :], ALU.subtract
                                            ).then_inc(tile_low, 1)
        if cut:
            @st.block.gpsimd
            def _(pool):
                def cut_low(i, at, turn):
                    u = i
                    pool.wait_ge(high_cut, u + 1)
                    if at >= lows:
                        pool.wait_ge(group_done, (u - lows + 1) * unit)
                    g = at * unit
                    nc.gpsimd.tensor_tensor(piece(w_low, g), slab_columns(g), piece(w_high, g), ALU.subtract
                                            ).then_inc(low_cut, 1)
                in_turns(pool, units, lead // unit, cut_low)

        @st.block.tensor
        def _(pe):
            def group(i, at, turn):
                f, b = at % per, at % banks
                if at >= banks:
                    pe.wait_ge(bank_free, i - (banks - 1))
                if by_tokens:
                    out = core.psum[:, b, 0:cols]
                    tokens = slice(f * P, (f + 1) * P)
                else:
                    out = core.psum[0:gcols, b, 0:width]
                if not cut:
                    if f == 0:
                        pe.wait_ge(core.slab_loaded[(first + at // per) % RING], slab_count(at, turn))
                    w = slab_columns(at)
                    for k in range(kt):
                        lhs, rhs = (source(k)[:, tokens], w[:, k, :]) if by_tokens else (w[:, k, :], source(k))
                        mm = nc.tensor.matmul(out, lhs, rhs, start=(k == 0), stop=(k == kt - 1))
                    mm.then_inc(group_done, 1)
                    return
                u = i if unit == 1 else i // unit
                starts_unit = at % unit == 0
                if starts_unit:
                    pe.wait_ge(high_cut, u + 1)
                for n, (w, x) in enumerate(((w_high, pair.high), (w_high, pair.low), (w_low, pair.high))):
                    if n == 2 and starts_unit:
                        pe.wait_ge(low_cut, u + 1)
                    w = piece(w, at)
                    for k in range(kt):
                        if raw and at == 0 and n < 2:
                            pe.wait_ge(tile_low if n else tile_high, k + 1)
                        lhs, rhs = (x[:, k, tokens], w[:, k, :]) if by_tokens else (w[:, k, :], x[:, k, :])
                        mm = nc.tensor.matmul(out, lhs, rhs, start=(n == 0 and k == 0), stop=(n == 2 and k == kt - 1))
                mm.then_inc(group_done, 1)

            in_turns(pe, count, lead, group)

        g = Groups(core, count, lead, banks, cols if by_tokens else width, gcols if not by_tokens else P,
                   group_done, bank_free, unit, cut_high if cut else None)
        epilogue(core, st, g)
        if cut and not g.high_cut_run:
            @st.block.scalar
            def _(act):
                g.run_scalar(act, lambda i, at, turn: None)
    core.linears += 1
    core.first_slab += nslab


class Pair:

    def __init__(self, high, low):
        self.high, self.low = high, low


class Groups:

    def __init__(self, core, count, lead, banks, width, rows, done, free, unit, cut_high):
        self.core, self.count, self.lead, self.banks = core, count, lead, banks
        self.width, self.rows, self.done, self.free = width, rows, done, free
        self.unit, self.cut_high, self.high_cut_run = unit, cut_high, False
        self.start, self.total = 0, count
        self.later = []

    def bank(self, at):
        return self.core.psum[0:self.rows, at % self.banks, 0:self.width]

    def part(self, start, count):
        assert not looped(self.count, self.lead)
        g = Groups(self.core, count, count, self.banks, self.width, self.rows, self.done, self.free, self.unit, self.cut_high)
        g.start, g.total, g.later = start, self.total, self.later
        return g

    def own(self, i):
        return i - self.start if self.start else i

    def run(self, eng, body):
        if self.start or self.count < self.total:
            for i in range(self.start, self.start + self.count):
                body(i, i, None)
        else:
            in_turns(eng, self.count, self.lead, body)

    def run_scalar(self, act, body):
        self.high_cut_run = True

        def step(i, at, turn):
            if self.cut_high and at % self.unit == 0 and (turn is not None or at + self.unit < self.total):
                self.cut_high(act, i + self.unit, at + self.unit, turn)
            body(i, at, turn)
            for when, work in self.later:
                if when == at:
                    work()
        self.run(act, step)


def parts(*items):
    def epilogue(core, st, g):
        start = 0
        for count, one in items:
            one(core, st, g.part(start, count))
            start += count
        assert start == g.count
        g.high_cut_run = True
    return epilogue


def stored(dst, func=ACT.Copy, bias=None):
    def epilogue(core, st, g):
        @st.block.scalar
        def _(act):
            def take(i, at, turn):
                act.wait_ge(g.done, i + 1)
                if g.start and at == g.start:
                    act.wait_ge(g.free, at)
                if bias is None:
                    ins = core.nc.scalar.activation(dst(g.own(i), at), g.bank(at), func)
                else:
                    ins = core.nc.scalar.activation(dst(g.own(i), at), g.bank(at), func, bias=bias(g.own(i)))
                ins.then_inc(g.free, 1)
            g.run_scalar(act, take)
    return epilogue


def convolved(taps, weight, bias, dst, mu=False):
    def epilogue(core, st, g):
        nc = core.nc
        pad = taps - 1
        raw = st.sb("raw", [P, 2, pad + T])
        acc = st.sb("acc", [P, 2, T])
        tap_done, conv_done, silu_done, zeroed = (st.sem(n) for n in ("tap_done", "conv_done", "silu_done", "zeroed"))

        @st.block.scalar
        def _(act):
            def take(i, at, turn):
                act.wait_ge(g.done, i + 1)
                if at >= 2:
                    act.wait_ge(conv_done, i - 1)
                nc.scalar.activation(raw[:, at % 2, pad:], g.bank(at), ACT.Copy).then_inc(g.free, 1)
                act.wait_ge(conv_done, i + 1)
                nc.scalar.activation(dst(i, at), acc[:, at % 2, :], ACT.Silu, bias=bias(i)).then_inc(silu_done, 1)
            g.run_scalar(act, take)

        @st.block.vector
        def _(dve):
            nc.vector.memset(raw[:, :, 0:pad], 0.0).then_inc(zeroed, 1)
            dve.wait_ge(zeroed, 1)

            def conv(i, at, turn):
                dve.wait_ge(g.free, i + 1)
                if at >= 2:
                    dve.wait_ge(silu_done, i - 1)
                a = acc[:, at % 2, :]
                for j in range(taps):
                    x = raw[:, at % 2, j:j + T]
                    if j == 0:
                        ins = nc.vector.tensor_scalar(a, x, weight(i, 0), None, ALU.mult)
                    else:
                        dve.wait_ge(tap_done, i * (taps - 1) + j)
                        ins = nc.vector.scalar_tensor_tensor(out=a, in0=x, scalar=weight(i, j), in1=a,
                                                             op0=ALU.mult, op1=ALU.add)
                    ins.then_inc(conv_done if j == taps - 1 else tap_done, 1)
            g.run(dve, conv)
    return epilogue


def added(dst, scale=None):
    def epilogue(core, st, g):
        nc = core.nc
        scaled = st.sem("scaled")

        if scale is not None:
            tmp = st.sb("scaled_group", [P, 2, T])

        @st.block.vector
        def _(dve):
            def take(i, at, turn):
                dve.wait_ge(g.done, i + 1)
                if scale is None:
                    nc.vector.tensor_tensor(dst(i), g.bank(at), dst(i), ALU.add).then_inc(g.free, 1)
                else:
                    nc.vector.tensor_tensor(tmp[:, at % 2, :], g.bank(at), scale(i), ALU.mult).then_inc(g.free, 1)
                    dve.wait_ge(g.free, i + 1)
                    nc.vector.tensor_tensor(dst(i), tmp[:, at % 2, :], dst(i), ALU.add).then_inc(scaled, 1)
            g.run(dve, take)
    return epilogue


def gated(dst, func, taps=0, weight=None):
    def epilogue(core, st, g):
        nc = core.nc
        gate = st.sb("gate", [P, 2, T])
        gate_done, product_done = st.sem("gate_done"), st.sem("product_done")
        high_cut, low_cut = st.sem("result_high_cut"), st.sem("result_low_cut")
        product_ = st.sb("product", [P, 2, T])

        def cut_high(act, h, slot):
            if taps:
                act.wait_ge(product_done, h + 1)
            else:
                act.wait_ge(g.free, 2 * h + 2)
            nc.scalar.activation(row(dst.high, h), product_[:, slot, :], ACT.Copy).then_inc(high_cut, 1)

        def cut_low(dve, h, slot):
            dve.wait_ge(high_cut, h + 1)
            nc.vector.tensor_tensor(row(dst.low, h), product_[:, slot, :], row(dst.high, h), ALU.subtract).then_inc(low_cut, 1)

        if not taps:
            @st.block.scalar
            def _(act):
                def take(i, at, turn):
                    if at % 2 == 0:
                        act.wait_ge(g.done, i + 1)
                        if at >= 4:
                            act.wait_ge(g.free, i - 2)
                        nc.scalar.activation(gate[:, at // 2 % 2, :], g.bank(at), func).then_inc(gate_done, 1)
                        if at >= 2:
                            cut_high(act, half(i, at, turn, g.lead) - 1, (at // 2 - 1) % 2)
                g.run_scalar(act, take)
                cut_high(act, g.count // 2 - 1, (g.count // 2 - 1) % 2)

            @st.block.vector
            def _(dve):
                def take(i, at, turn):
                    if at % 2:
                        h = half(i, at, turn, g.lead)
                        dve.wait_ge(g.done, i + 1)
                        dve.wait_ge(gate_done, h + 1)
                        if at >= 4:
                            dve.wait_ge(low_cut, h - 1)
                        nc.vector.tensor_tensor(product_[:, at // 2 % 2, :], g.bank(at), gate[:, at // 2 % 2, :], ALU.mult
                                                ).then_inc(g.free, 2)
                        if at >= 2:
                            cut_low(dve, h - 1, (at // 2 - 1) % 2)
                g.run(dve, take)
                cut_low(dve, g.count // 2 - 1, (g.count // 2 - 1) % 2)
            return

        pad = taps - 1
        raw = st.sb("raw", [P, 2, pad + T])
        acc = st.sb("acc", [P, 2, T])
        tap_done, conv_done, zeroed = (st.sem(n) for n in ("tap_done", "conv_done", "zeroed"))

        @st.block.scalar
        def _(act):
            def take(i, at, turn):
                act.wait_ge(g.done, i + 1)
                if at >= 2:
                    act.wait_ge(conv_done, i - 1)
                nc.scalar.activation(raw[:, at % 2, pad:], g.bank(at), ACT.Copy).then_inc(g.free, 1)
                if at % 2 == 0:
                    act.wait_ge(conv_done, i + 1)
                    if at >= 4:
                        act.wait_ge(product_done, half(i, at, turn, g.lead) - 1)
                    nc.scalar.activation(gate[:, at // 2 % 2, :], acc[:, 0, :], func).then_inc(gate_done, 1)
                    if at >= 2:
                        cut_high(act, half(i, at, turn, g.lead) - 1, (at // 2 - 1) % 2)
            g.run_scalar(act, take)
            cut_high(act, g.count // 2 - 1, (g.count // 2 - 1) % 2)

        @st.block.vector
        def _(dve):
            nc.vector.memset(raw[:, :, 0:pad], 0.0).then_inc(zeroed, 1)
            dve.wait_ge(zeroed, 1)

            def conv(i, at, turn):
                h = half(i, at, turn, g.lead)
                dve.wait_ge(g.free, i + 1)
                a = acc[:, at % 2, :]
                if at >= 2:
                    if at % 2 == 0:
                        dve.wait_ge(gate_done, h)
                    else:
                        dve.wait_ge(product_done, h)
                for j in range(taps):
                    x = raw[:, at % 2, j:j + T]
                    if j == 0:
                        ins = nc.vector.tensor_scalar(a, x, weight(i, 0), None, ALU.mult)
                    else:
                        dve.wait_ge(tap_done, i * (taps - 1) + j)
                        ins = nc.vector.scalar_tensor_tensor(out=a, in0=x, scalar=weight(i, j), in1=a,
                                                             op0=ALU.mult, op1=ALU.add)
                    ins.then_inc(conv_done if j == taps - 1 else tap_done, 1)
                if at % 2:
                    dve.wait_ge(gate_done, h + 1)
                    dve.wait_ge(conv_done, i + 1)
                    if at >= 4:
                        dve.wait_ge(low_cut, h - 1)
                    nc.vector.tensor_tensor(product_[:, at // 2 % 2, :], a, gate[:, at // 2 % 2, :], ALU.mult
                                            ).then_inc(product_done, 1)
                    if at >= 2:
                        cut_low(dve, h - 1, (at // 2 - 1) % 2)
            g.run(dve, conv)
            cut_low(dve, g.count // 2 - 1, (g.count // 2 - 1) % 2)
    return epilogue


def half(i, at, turn, lead):
    return at // 2 if turn is None else turn * (lead // 2) + (at - lead) // 2


def norm(core, name, x, sets, stat, out, eps, gain=None, shift=None, times=None, residual=False, center=None,
         last=ACT.Identity, pair=None):
    nc = core.nc
    tiles = [i for s in sets for i in s]
    n = len(tiles)
    where = {i: s for s, ts in enumerate(sets) for i in ts}
    with core.stage(name) as st:
        sq = st.sb("squares", [P, n, T])
        plain = times is None and not residual and pair is None
        over = [sq[:, tiles.index(ts[0]), :] for ts in sets]
        rstd_tiles = None if plain else st.sb("rstd", [P, len(sets), T])
        rstd = lambda s: over[s] if plain else rstd_tiles[:, s, :]
        xc = st.sb("centred", [P, n, T]) if center is not None else None
        squared, summed, rooted, inverted, scaled, stored_, shifted, meaned, centred, high_cut, low_cut = (
            st.sem(s) for s in ("squared", "summed", "rooted", "inverted", "scaled", "stored", "shifted", "meaned",
                                "centred", "high_cut", "low_cut"))
        src = (lambda i: xc[:, tiles.index(i), :]) if center is not None else x

        @st.block.tensor
        def _(pe):
            if center is not None:
                for s, ts in enumerate(sets):
                    if s >= 4:
                        pe.wait_ge(centred, sum(len(q) for q in sets[:s - 3]))
                    for j, i in enumerate(ts):
                        mm = nc.tensor.matmul(core.bank(4 + s % 4), center, x(i), start=(j == 0), stop=(j == len(ts) - 1))
                    mm.then_inc(meaned, 1)
            m = 0
            for s, ts in enumerate(sets):
                if s >= 4:
                    pe.wait_ge(rooted, s - 3)
                for j, i in enumerate(ts):
                    m += 1
                    pe.wait_ge(squared, m)
                    mm = nc.tensor.matmul(core.bank(s % 4), stat, sq[:, m - 1, :], start=(j == 0), stop=(j == len(ts) - 1))
                mm.then_inc(summed, 1)

        @st.block.scalar
        def _(act):
            for m, i in enumerate(tiles):
                if center is not None:
                    act.wait_ge(centred, m + 1)
                nc.scalar.activation(sq[:, m, :], src(i), ACT.Square).then_inc(squared, 1)
            for s in range(len(sets)):
                act.wait_ge(summed, s + 1)
                nc.scalar.activation(rstd(s), core.bank(s % 4), ACT.Sqrt, bias=eps).then_inc(rooted, 1)
            if pair is not None:
                for m, i in enumerate(tiles):
                    act.wait_ge(scaled, m + 1)
                    kw = {} if shift is None else {"bias": shift(i)}
                    nc.scalar.activation(pair.high[:, i, :], sq[:, m, :], ACT.Copy if shift is None else ACT.Identity, **kw
                                         ).then_inc(high_cut, 1)
            elif shift is not None:
                for m, i in enumerate(tiles):
                    act.wait_ge(stored_, m + 1)
                    nc.scalar.activation(out(i), out(i), last, bias=shift(i)).then_inc(shifted, 1)

        @st.block.vector
        def _(dve):
            if center is not None:
                for m, i in enumerate(tiles):
                    dve.wait_ge(meaned, where[i] + 1)
                    nc.vector.tensor_tensor(xc[:, m, :], x(i), core.bank(4 + where[i] % 4), ALU.subtract).then_inc(centred, 1)
            def cut_low(m):
                i = tiles[m]
                dve.wait_ge(high_cut, m + 1)
                if shift is None:
                    ins = nc.vector.tensor_tensor(pair.low[:, i, :], sq[:, m, :], pair.high[:, i, :], ALU.subtract)
                else:
                    ins = nc.vector.scalar_tensor_tensor(out=pair.low[:, i, :], in0=sq[:, m, :], scalar=shift(i),
                                                         in1=pair.high[:, i, :], op0=ALU.add, op1=ALU.subtract)
                ins.then_inc(low_cut, 1)

            last = -1
            for m, i in enumerate(tiles):
                s = where[i]
                if s != last:
                    last = s
                    if center is not None:
                        dve.wait_ge(centred, n)
                    dve.wait_ge(rooted, s + 1)
                    nc.vector.reciprocal(rstd(s), rstd(s)).then_inc(inverted, 1)
                    dve.wait_ge(inverted, s + 1)
                dst = out(i) if plain else sq[:, m, :]
                if not plain:
                    dve.wait_ge(summed, s + 1)
                if gain is None:
                    ins = nc.vector.tensor_tensor(dst, src(i), rstd(s), ALU.mult)
                else:
                    ins = nc.vector.scalar_tensor_tensor(out=dst, in0=src(i), scalar=gain(i), in1=rstd(s),
                                                         op0=ALU.mult, op1=ALU.mult)
                ins.then_inc(stored_ if plain else scaled, 1)
                if pair is not None:
                    if m >= 2:
                        cut_low(m - 2)
                elif not plain:
                    dve.wait_ge(scaled, m + 1)
                    nc.vector.tensor_tensor(out(i), sq[:, m, :], out(i) if residual else times(i),
                                            ALU.add if residual else ALU.mult).then_inc(stored_, 1)
            if pair is not None:
                for m in range(max(0, n - 2), n):
                    cut_low(m)


def row(t, i):
    return t[:, i, :]


def turned(core, name, jobs, times=None):
    nc = core.nc
    with core.stage(name) as st:
        turned_, copied = st.sem("turned"), st.sem("copied")

        @st.block.tensor
        def _(pe):
            for i, (sources, _) in enumerate(jobs):
                if i >= BANKS:
                    pe.wait_ge(copied, i - BANKS + 1)
                for j, src in enumerate(sources):
                    mm = nc.tensor.transpose(core.psum[:, i % BANKS, j * P:(j + 1) * P], src, core.ident[:])
                mm.then_inc(turned_, 1)

        @st.block.scalar
        def _(act):
            for i, (sources, out) in enumerate(jobs):
                act.wait_ge(turned_, i + 1)
                nc.scalar.activation(out, core.psum[:, i % BANKS, 0:len(sources) * P], ACT.Copy).then_inc(copied, 1)


class Keys:

    def __init__(self, q, k, v, n, bias, scale, slope=1.0, gate=None, valid=None):
        self.q, self.k, self.v, self.n, self.bias = q, k, v, n, bias
        self.scale, self.slope, self.gate, self.valid = scale, slope, gate, valid
        self.blocks = -(-n // P)


def attention(core, name, units, dv=64, joint=False, W=2):
    nc = core.nc
    ns = len(units[0][0])
    n_units = len(units)
    masked_sets = [j for j in range(ns) if units[0][0][j].valid is not None]
    short_sets = [j for j in range(ns) if units[0][0][j].n % P]
    nm = len(masked_sets)
    sloped = any(s.slope != 1.0 for s in units[0][0])
    with core.stage(name) as st:
        SB = 3
        R = W + 2
        probs = st.sb("probs", [P, R, ns, 512])
        turned_p = st.sb("turned_p", [P, 2, ns, 512])
        top = st.sb("top", [P, R, ns])
        total = st.sb("total", [P, R, ns])
        inv = st.sb("inv", [P, R, ns])
        (scored, biased, topped, exped, valid_done, summed, inverted, weighed, normed, turned_, copied, mixed,
         stored_, zeroed) = (st.sem(s) for s in (
             "scored", "biased", "topped", "exped", "valid_done", "summed", "inverted", "weighed", "normed",
             "turned", "copied", "mixed", "stored", "zeroed"))
        steps = range(n_units + W + 2)

        @st.block.tensor
        def _(pe):
            for step in steps:
                if step < n_units:
                    sets, _ = units[step]
                    for j, s in enumerate(sets):
                        m = step * ns + j
                        if m >= SB:
                            pe.wait_ge(biased, m - SB + 1)
                        nc.tensor.matmul(core.psum[:, m % SB, 0:s.n], s.q, s.k, start=True, stop=True).then_inc(scored, 1)
                if 0 <= step - W - 1 < n_units:
                    u = step - W - 1
                    pe.wait_ge(normed, u + 1)
                    for j, s in enumerate(units[u][0]):
                        m = u * ns + j
                        if m >= 3:
                            pe.wait_ge(copied, m - 2)
                        for b in range(s.blocks):
                            mm = nc.tensor.transpose(core.psum[:, 3 + m % 3, b * P:(b + 1) * P],
                                                     probs[:, u % R, j, b * P:(b + 1) * P], core.ident[:])
                        mm.then_inc(turned_, 1)
                if 0 <= step - W - 2 < n_units:
                    u = step - W - 2
                    sets, out = units[u]
                    base = out.base_partition()
                    pe.wait_ge(copied, (u + 1) * ns)
                    if u >= 2:
                        pe.wait_ge(stored_, u - 1)
                    for j, s in enumerate(sets):
                        for b in range(s.blocks):
                            mm = nc.tensor.matmul(core.psum[base:base + dv, 6 + u % 2, 0:P], s.v(b),
                                                  turned_p[:, u % 2, j, b * P:(b + 1) * P],
                                                  start=(j == 0 and b == 0), stop=(j == ns - 1 and b == s.blocks - 1))
                    mm.then_inc(mixed, 1)

        @st.block.vector
        def _(dve):
            for n, j in enumerate(short_sets):
                nc.vector.memset(probs[:, :, j, 0:P], 0.0).then_inc(zeroed, 1)
                dve.wait_ge(zeroed, n + 1)

            def tops(u):
                sets, _ = units[u]
                if u >= R:
                    dve.wait_ge(turned_, (u - R + 1) * ns)
                    dve.wait_ge(exped, (u - R + 1) * ns)
                for j, s in enumerate(sets):
                    m = u * ns + j
                    dve.wait_ge(scored, m + 1)
                    nc.vector.scalar_tensor_tensor(
                        out=probs[:, u % R, j, 0:s.n], in0=core.psum[:, m % SB, 0:s.n], scalar=s.scale / s.slope,
                        in1=s.bias, op0=ALU.mult, op1=ALU.add).then_inc(biased, 1)
                if joint:
                    n = sets[0].n
                    dve.wait_ge(biased, (u + 1) * ns)
                    nc.vector.tensor_reduce(top[:, u % R, 0:1], probs[:, u % R, :, 0:n], mybir.AxisListType.XY, ALU.max,
                                            negate=True).then_inc(topped, 1)
                    return
                for j, s in enumerate(sets):
                    dve.wait_ge(biased, u * ns + j + 1)
                    nc.vector.tensor_reduce(top[:, u % R, j:j + 1], probs[:, u % R, j, 0:s.n], X_AXIS, ALU.max,
                                            negate=True).then_inc(topped, 1)
                if sloped:
                    dve.wait_ge(topped, (u + 1) * ns + u)
                    nc.vector.tensor_scalar(top[:, u % R, :], top[:, u % R, :], sets[0].slope, None, ALU.mult
                                            ).then_inc(topped, 1)

            def weights(u):
                sets, _ = units[u]
                dve.wait_ge(exped, (u + 1) * ns)
                for i, j in enumerate(masked_sets):
                    s = sets[j]
                    nc.vector.tensor_tensor(probs[:, u % R, j, 0:s.n], probs[:, u % R, j, 0:s.n], s.valid, ALU.mult
                                            ).then_inc(valid_done, 1)
                    dve.wait_ge(valid_done, 2 * (u * nm + i) + 1)
                    nc.vector.tensor_reduce(total[:, u % R, j:j + 1], probs[:, u % R, j, 0:s.n], X_AXIS, ALU.add
                                            ).then_inc(valid_done, 1)
                    dve.wait_ge(valid_done, 2 * (u * nm + i) + 2)
                if joint:
                    nc.vector.tensor_reduce(inv[:, u % R, 0:1], total[:, u % R, :], X_AXIS, ALU.add).then_inc(summed, 1)
                    dve.wait_ge(summed, u + 1)
                    nc.vector.reciprocal(inv[:, u % R, 0:1], inv[:, u % R, 0:1]).then_inc(inverted, 1)
                else:
                    nc.vector.tensor_scalar(total[:, u % R, :], total[:, u % R, :], 1e-30, None, ALU.max).then_inc(summed, 1)
                    dve.wait_ge(summed, u + 1)
                    nc.vector.reciprocal(inv[:, u % R, :], total[:, u % R, :]).then_inc(inverted, 1)
                dve.wait_ge(inverted, u + 1)
                if joint:
                    n = sets[0].n
                    nc.vector.tensor_scalar(probs[:, u % R, :, 0:n], probs[:, u % R, :, 0:n], inv[:, u % R, 0:1], None,
                                            ALU.mult).then_inc(normed, 1)
                    return
                for j, s in enumerate(sets):
                    x = probs[:, u % R, j, 0:s.n]
                    if s.gate is None:
                        ins = nc.vector.tensor_scalar(x, x, inv[:, u % R, j:j + 1], None, ALU.mult)
                    else:
                        ins = nc.vector.tensor_scalar(x, x, inv[:, u % R, j:j + 1], s.gate, ALU.mult, ALU.mult)
                    ins.then_inc(normed if j == ns - 1 else weighed, 1)

            for step in steps:
                if step < n_units:
                    tops(step)
                if 0 <= step - W < n_units:
                    weights(step - W)

        @st.block.scalar
        def _(act):
            for step in steps:
                if step < n_units:
                    u = step
                    if u >= R:
                        act.wait_ge(inverted, u - R + 1)
                    for j, s in enumerate(units[u][0]):
                        if joint:
                            act.wait_ge(topped, u + 1)
                        elif sloped:
                            act.wait_ge(topped, (u + 1) * (ns + 1))
                        else:
                            act.wait_ge(topped, u * ns + j + 1)
                        t = 0 if joint else j
                        nc.scalar.activation(probs[:, u % R, j, 0:s.n], probs[:, u % R, j, 0:s.n], ACT.Exp,
                                             bias=top[:, u % R, t:t + 1], scale=s.slope,
                                             accum_out=total[:, u % R, j:j + 1]).then_inc(exped, 1)
                if 0 <= step - W - 1 < n_units:
                    u = step - W - 1
                    if u >= 2:
                        act.wait_ge(mixed, u - 1)
                    for j, s in enumerate(units[u][0]):
                        m = u * ns + j
                        act.wait_ge(turned_, m + 1)
                        nc.scalar.activation(turned_p[:, u % 2, j, 0:s.blocks * P], core.psum[:, 3 + m % 3, 0:s.blocks * P],
                                             ACT.Copy).then_inc(copied, 1)
                if 0 <= step - W - 2 < n_units:
                    u = step - W - 2
                    out = units[u][1]
                    base = out.base_partition()
                    act.wait_ge(mixed, u + 1)
                    nc.scalar.activation(out, core.psum[base:base + dv, 6 + u % 2, 0:P], ACT.Copy).then_inc(stored_, 1)


SSD_H, SSD_P = 16, 64


def ssd(core, pool, xbc, dt_raw, y):
    nc = core.nc
    H, HG = SSD_H, SSD_H // 2
    dt = pool.sb("ssd_dt", [P, NT * H])
    dta = pool.sb("ssd_dta", [P, NT * H])
    acs = pool.sb("ssd_acs", [P, NT * H])
    dec = pool.sb("ssd_dec", [P, NT * H])
    etot = pool.sb("ssd_etot", [P, NT * H])
    xd = pool.sb("ssd_xd", [P, NT, 1024])
    btok = pool.sb("ssd_btok", [P, NT, 256])
    upper = pool.sb("ssd_upper", [P, P])
    masked = pool.sb("ssd_masked", [P, P])
    gt = pool.sb("ssd_gt", [P, NT, 2, P])

    with core.stage("ssd_dt") as st:
        tmp = st.sb("tmp", [P, NT * H])
        rate = st.sb("rate", [P, NT * H])
        tables, dve_done, act_done, pe_done = (st.sem(s) for s in ("tables", "dve_done", "act_done", "pe_done"))

        @st.block.sync
        def _(sp):
            sp.dma_start(upper[:], core.dram["upper"]).then_inc(tables, 16)
            sp.dma_start(masked[:], core.dram["lower_masked"]).then_inc(tables, 16)

        @st.block.vector
        def _(dve):
            nc.vector.tensor_tensor(dt[:], dt_raw[:], core.colblock("l0_dt_bias"), ALU.add).then_inc(dve_done, 1)
            dve.wait_ge(act_done, 4)
            nc.vector.scalar_tensor_tensor(out=dt[:], in0=dt[:], scalar=0.0, in1=tmp[:], op0=ALU.max, op1=ALU.add
                                           ).then_inc(dve_done, 1)
            dve.wait_ge(dve_done, 2)
            nc.vector.scalar_tensor_tensor(out=dta[:], in0=rate[:], scalar=-1.0, in1=dt[:], op0=ALU.mult, op1=ALU.mult
                                           ).then_inc(dve_done, 1)
            dve.wait_ge(pe_done, 2)
            nc.vector.tensor_copy(acs[:], core.psum[:, 0, 0:NT * H]).then_inc(dve_done, 1)
            dve.wait_ge(dve_done, 4)
            nc.vector.tensor_tensor(dec[:], core.psum[:, 1, 0:NT * H], acs[:], ALU.subtract).then_inc(dve_done, 1)

        @st.block.scalar
        def _(act):
            nc.scalar.activation(rate[:], core.colblock("l0_a_log"), ACT.Exp).then_inc(act_done, 1)
            act.wait_ge(dve_done, 1)
            nc.scalar.activation(tmp[:], dt[:], ACT.Abs).then_inc(act_done, 1)
            act.wait_ge(act_done, 2)
            nc.scalar.activation(tmp[:], tmp[:], ACT.Exp, scale=-1.0).then_inc(act_done, 1)
            act.wait_ge(act_done, 3)
            nc.scalar.activation(tmp[:], tmp[:], ACT.Ln, bias=core.col("one")).then_inc(act_done, 1)
            act.wait_ge(dve_done, 5)
            nc.scalar.activation(dec[:], dec[:], ACT.Exp).then_inc(act_done, 1)
            nc.scalar.activation(etot[:], core.psum[:, 1, 0:NT * H], ACT.Exp).then_inc(act_done, 1)

        @st.block.tensor
        def _(pe):
            pe.wait_ge(tables, 32)
            pe.wait_ge(dve_done, 3)
            nc.tensor.matmul(core.psum[:, 0, 0:NT * H], upper[:], dta[:], start=True, stop=True).then_inc(pe_done, 1)
            nc.tensor.matmul(core.psum[:, 1, 0:NT * H], core.ones[:], dta[:], start=True, stop=True).then_inc(pe_done, 1)

    with core.stage("ssd_turn") as st:
        turned_, taken, products, gt_out = (st.sem(s) for s in ("turned", "taken", "products", "gt_out"))

        @st.block.tensor
        def _(pe):
            for i in range(3 * NT):
                c, part = i // 3, i % 3
                if i >= 6:
                    pe.wait_ge(taken, i - 5)
                tiles = [4 * part + f for f in range(4)] if part < 2 else [8, 9]
                for j, f in enumerate(tiles):
                    mm = nc.tensor.transpose(core.psum[:, i % 6, j * P:(j + 1) * P], xbc[:, f, c * P:(c + 1) * P], core.ident[:])
                mm.then_inc(turned_, 1)
            for c in range(NT):
                if c >= 2:
                    pe.wait_ge(gt_out, c - 1)
                for g in range(2):
                    mm = nc.tensor.matmul(core.psum[:, 6 + c % 2, g * P:(g + 1) * P], xbc[:, 8 + g, c * P:(c + 1) * P],
                                          xbc[:, 10 + g, c * P:(c + 1) * P], start=True, stop=True)
                mm.then_inc(products, 1)

        @st.block.vector
        def _(dve):
            for i in range(3 * NT):
                c, part = i // 3, i % 3
                dve.wait_ge(turned_, i + 1)
                if part < 2:
                    rates = dt[:, c * H + part * HG:c * H + (part + 1) * HG].unsqueeze(2).to_broadcast([P, HG, SSD_P])
                    nc.vector.tensor_tensor(xd[:, c, part * 512:(part + 1) * 512].rearrange("p (h d) -> p h d", h=HG),
                                            core.psum[:, i % 6, :].rearrange("p (h d) -> p h d", h=HG), rates, ALU.mult
                                            ).then_inc(taken, 1)
                else:
                    nc.vector.tensor_copy(btok[:, c, :], core.psum[:, i % 6, 0:256]).then_inc(taken, 1)

        @st.block.scalar
        def _(act):
            for c in range(NT):
                act.wait_ge(products, c + 1)
                nc.scalar.activation(gt[:, c, :, :].rearrange("p g l -> p (g l)"), core.psum[:, 6 + c % 2, 0:256], ACT.Copy
                                     ).then_inc(gt_out, 1)

    with core.stage("ssd_scan") as st:
        R = 6
        decay_in = st.sb("decay_in", [P, R, P])
        lmat = st.sb("lmat", [P, R, P])
        mt = st.sb("mt", [P, R, P])
        cdec = st.sb("cdec", [P, R, P])
        state = st.sb("state", [P, 1024])
        xdd = st.sb("xdd", [P, 2, 1024])
        (sums, diffed, grown, decayed, mixed_m, mixed_c, products, stored_, decayed_x, updated, grew, zeroed, state_scaled) = (
            st.sem(s) for s in ("sums", "diffed", "grown", "decayed", "mixed_m", "mixed_c", "products", "stored",
                                "decayed_x", "updated", "grew", "zeroed", "state_scaled"))
        U = NT * H

        def sums_bank(u):
            return (0, 1, 6, 7)[u % 4]

        @st.block.tensor
        def _(pe):
            for phase, u in lagged(U, {0: 0, 2: 4}):
                c, h = u // H, u % H
                if phase == 0:
                    if u >= 4:
                        pe.wait_ge(grown, u - 3)
                    nc.tensor.matmul(core.psum[:, sums_bank(u), 0:P], dta[:, u:u + 1].to_broadcast([P, P]), upper[:],
                                     start=True, stop=True).then_inc(sums, 1)
                elif phase == 2:
                    b, half_ = 2 + (u // 2) % 2, 64 * (h % 2)
                    if h % 2 == 0 and u >= 4:
                        pe.wait_ge(stored_, u // 2 - 1)
                    pe.wait_ge(mixed_m, u + 1)
                    mm = nc.tensor.matmul(core.psum[half_:half_ + 64, b, 0:P], xd[:, c, h * 64:(h + 1) * 64], mt[:, u % R, :],
                                          start=True, stop=(c == 0))
                    if c > 0:
                        pe.wait_ge(mixed_c, (c - 1) * H + h + 1)
                        pe.wait_ge(grew, 2 * c)
                        mm = nc.tensor.matmul(core.psum[half_:half_ + 64, b, 0:P], state[:, h * 64:(h + 1) * 64],
                                              cdec[:, u % R, :], start=False, stop=True)
                    mm.then_inc(products, 1)
                    if h == H - 1 and c < NT - 1:
                        pe.wait_ge(decayed_x, c + 1)
                        for g in range(2):
                            nc.tensor.matmul(core.psum[:, 4 + g, :], btok[:, c, g * P:(g + 1) * P],
                                             xdd[:, c % 2, g * 512:(g + 1) * 512], start=True, stop=True).then_inc(updated, 1)

        @st.block.vector
        def _(dve):
            nc.vector.memset(state[:], 0.0).then_inc(zeroed, 1)
            for phase, u in lagged(U, {0: 0, 1: 2, 2: 5}):
                c, h = u // H, u % H
                if phase == 0:
                    dve.wait_ge(sums, u + 1)
                    if u >= R:
                        dve.wait_ge(mixed_m, u - R + 1)
                    nc.vector.scalar_tensor_tensor(out=lmat[:, u % R, :], in0=core.psum[:, sums_bank(u), 0:P], scalar=acs[:, u:u + 1],
                                                   in1=masked[:], op0=ALU.subtract, op1=ALU.add).then_inc(diffed, 1)
                    if h == 0 and c < NT - 1:
                        if c >= 2:
                            dve.wait_ge(updated, 2 * (c - 1))
                        nc.vector.tensor_tensor(xdd[:, c % 2, :].rearrange("p (h d) -> p h d", h=H),
                                                xd[:, c, :].rearrange("p (h d) -> p h d", h=H),
                                                dec[:, c * H:(c + 1) * H].unsqueeze(2).to_broadcast([P, H, SSD_P]), ALU.mult
                                                ).then_inc(decayed_x, 1)
                elif phase == 1:
                    dve.wait_ge(decayed, u + 1)
                    if u >= R:
                        dve.wait_ge(products, u - R + 1)
                    nc.vector.tensor_tensor(mt[:, u % R, :], gt[:, c, h // HG, :], lmat[:, u % R, :], ALU.mult
                                            ).then_inc(mixed_m, 1)
                elif h % 2 == 1:
                    dve.wait_ge(products, u + 1)
                    nc.vector.scalar_tensor_tensor(
                        out=y[:, h // 2, c * P:(c + 1) * P], in0=xbc[:, h // 2, c * P:(c + 1) * P],
                        scalar=core.col("l0_d_skip", h // 2), in1=core.psum[:, 2 + (u // 2) % 2, 0:P],
                        op0=ALU.mult, op1=ALU.add).then_inc(stored_, 1)
                    if h == H - 1 and c < NT - 1:
                        dve.wait_ge(zeroed, 1)
                        if c > 0:
                            dve.wait_ge(grew, 2 * c)
                        by_head = state[:].rearrange("p (h d) -> p h d", h=H)
                        nc.vector.tensor_tensor(by_head, by_head, etot[:, c * H:(c + 1) * H].unsqueeze(2).to_broadcast([P, H, SSD_P]),
                                                ALU.mult).then_inc(state_scaled, 1)
                        dve.wait_ge(state_scaled, c + 1)
                        for g in range(2):
                            dve.wait_ge(updated, 2 * c + g + 1)
                            s = state[:, g * 512:(g + 1) * 512]
                            nc.vector.tensor_tensor(s, core.psum[:, 4 + g, :], s, ALU.add).then_inc(grew, 1)

        @st.block.scalar
        def _(act):
            for u in range(U):
                act.wait_ge(diffed, u + 1)
                if u - R >= H:
                    act.wait_ge(mixed_c, u - R - H + 1)
                nc.scalar.activation(decay_in[:, u % R, :], core.psum[:, sums_bank(u), 0:P], ACT.Exp).then_inc(grown, 1)
                nc.scalar.activation(lmat[:, u % R, :], lmat[:, u % R, :], ACT.Exp).then_inc(decayed, 1)

        @st.block.gpsimd
        def _(pool_):
            for u in range(H, U):
                c, h = u // H, u % H
                pool_.wait_ge(grown, u + 1)
                if u >= H + R:
                    pool_.wait_ge(products, u - R + 1)
                nc.gpsimd.tensor_tensor(cdec[:, u % R, :], xbc[:, 10 + h // HG, c * P:(c + 1) * P], decay_in[:, u % R, :],
                                        ALU.mult).then_inc(mixed_c, 1)


class Pool:

    def __init__(self, nc, ctx):
        self.nc, self.ctx = nc, ctx

    def sb(self, name, shape, dtype=F32):
        return self.ctx.enter_context(self.nc.sbuf_tensor(name, shape, dtype))

    def pair(self, name, n):
        return Pair(self.sb(name + "_high", [P, n, T], F32R), self.sb(name + "_low", [P, n, T], F32R))


@contextmanager
def buffers(core):
    with ExitStack() as ctx:
        yield Pool(core.nc, ctx)


def product(core, name, n, out, a, b):
    nc = core.nc
    with core.stage(name) as st:
        dve_done, pool_done = st.sem("dve_done"), st.sem("pool_done")

        @st.block.vector
        def _(dve):
            for i in range(n):
                if i % 3 != 2:
                    nc.vector.tensor_tensor(out(i), a(i), b(i), ALU.mult).then_inc(dve_done, 1)

        @st.block.gpsimd
        def _(pool):
            for i in range(2, n, 3):
                nc.gpsimd.tensor_tensor(out(i), a(i), b(i), ALU.mult).then_inc(pool_done, 1)


def ada(core, name, silu_c, mod):
    nc = core.nc
    weights, nslab, kt, cols, gcols = core.plan[core.linears]
    assert weights == name + "_ada" and cols == 2 * P
    first = core.first_slab
    with core.stage(name + "_ada") as st:
        acc = st.sb("acc", [P, 2, 2, cols])
        begun, added_, joined, summed, placed = (st.sem(n) for n in ("begun", "added", "joined", "summed", "placed"))

        def rows(s):
            return core.ring[:, (first + s) % RING, 0:kt * cols].rearrange("p (k c) -> p k c", k=kt)

        @st.block.sync
        def _(sp):
            for s in range(nslab):
                sp.wait_ge(added_, (s + 1) * (kt - 2))
                core.load_slab(sp, first + s + RING)

        @st.block.scalar
        def _(act):
            for s in range(nslab):
                act.wait_ge(core.slab_loaded[(first + s) % RING], 16 * ((first + s) // RING + 1))
                if s >= 2:
                    act.wait_ge(summed, s - 1)
                for k in range(2):
                    nc.scalar.activation(acc[:, s % 2, k, :], rows(s)[:, k, :], ACT.Copy, scale=silu_c[:, k:k + 1]
                                         ).then_inc(begun, 1)

        @st.block.vector
        def _(dve):
            for s in range(nslab):
                for k in range(2, kt):
                    if k < 4:
                        dve.wait_ge(begun, 2 * s + k - 1)
                    else:
                        dve.wait_ge(added_, s * (kt - 2) + k - 3)
                    a = acc[:, s % 2, k % 2, :]
                    nc.vector.scalar_tensor_tensor(out=a, in0=rows(s)[:, k, :], scalar=silu_c[:, k:k + 1], in1=a,
                                                   op0=ALU.mult, op1=ALU.add).then_inc(added_, 1)
                dve.wait_ge(added_, (s + 1) * (kt - 2))
                a = acc[:, s % 2, :, :]
                nc.vector.tensor_tensor(a[:, 0, :], a[:, 0, :], a[:, 1, :], ALU.add).then_inc(joined, 1)
            dve.wait_ge(summed, nslab)
            nc.vector.tensor_tensor(mod[:], core.psum[:, 0, 0:2 * nslab], core.colblock(name + "_ada_b"), ALU.add
                                    ).then_inc(placed, 1)

        @st.block.tensor
        def _(pe):
            for s in range(nslab):
                pe.wait_ge(joined, s + 1)
                for n in range(2):
                    mm = nc.tensor.matmul(core.psum[:, 0, 2 * s + n:2 * s + n + 1], acc[:, s % 2, 0, n * P:(n + 1) * P],
                                          core.ones[:, 0:1], start=True, stop=True)
                mm.then_inc(summed, 1)
    core.linears += 1
    core.first_slab += nslab


def modulation(core, name, mod, pre_m, post_m, pre_f, post_f):
    nc = core.nc
    with core.stage(name + "_mod") as st:
        done = st.sem("done")

        @st.block.vector
        def _(dve):
            for at, pre, post in ((0, pre_m, post_m), (24, pre_f, post_f)):
                scale, gate = mod[:, at + 8:at + 16], mod[:, at + 16:at + 24]
                nc.vector.scalar_tensor_tensor(out=scale, in0=scale, scalar=1.0, in1=core.colblock(pre), op0=ALU.add,
                                               op1=ALU.mult).then_inc(done, 1)
                nc.vector.tensor_tensor(gate, gate, core.colblock(post), ALU.mult).then_inc(done, 1)


def swiglu(core, name, xT, mod, mean):
    with buffers(core) as b:
        a = b.pair(name + "_act", 22)
        with buffers(core) as c:
            h = c.pair(name + "_fh", KD)
            norm(core, name + "_fpre", lambda i: xT[:, i, :], [list(range(KD))], mean, None, core.col("eps"),
                 gain=lambda i: mod[:, 32 + i:33 + i], shift=lambda i: mod[:, 24 + i:25 + i], pair=h)
            linear(core, name + "_up", h, gated(a, ACT.Silu))
        y = b.sb(name + "_y", [P, KD, T])
        linear(core, name + "_down", a, stored(lambda i, at: y[:, i, :]))
        norm(core, name + "_fpost", lambda i: y[:, i, :], [list(range(KD))], mean, lambda i: xT[:, i, :], core.col("eps"),
             gain=lambda i: mod[:, 40 + i:41 + i], residual=True)


def rope_table(core, cs):
    nc = core.nc
    H, Q = slice(64, 128), slice(96, 128)
    with core.stage("rope") as st:
        pos_i = st.sb("pos_i", [P, T], I32)
        ang = st.sb("ang", [P, T])
        turns = st.sb("turns", [P, T])
        loaded, done, looked = st.sem("loaded"), st.sem("done"), st.sem("looked")

        @st.block.sync
        def _(sp):
            sp.dma_start(pos_i[:], core.dram["positions"]).then_inc(loaded, 16)

        @st.block.vector
        def _(dve):
            d = Marks(done)

            def after(ins):
                dve.wait_ge(done, d.mark(ins))

            dve.wait_ge(loaded, 16)
            a, n = ang[H, :], turns[H, :]
            after(nc.vector.tensor_copy(a, pos_i[H, :]))
            after(nc.vector.tensor_scalar(a, a, core.col("rope_inv")[H, :], None, ALU.mult))
            after(nc.vector.tensor_scalar(n, a, 1.0 / (2.0 * math.pi), 12582912.0, ALU.mult, ALU.add))
            after(nc.vector.tensor_scalar(n, n, 12582912.0, None, ALU.subtract))
            first, second = 6.28125, 0.001934051513671875
            third = 2.0 * math.pi - first - second
            for part in (first, second, third):
                after(nc.vector.scalar_tensor_tensor(out=a, in0=n, scalar=-part, in1=a, op0=ALU.mult, op1=ALU.add))
            after(nc.vector.tensor_scalar(a, a, 3.1415925, -3.1415925, ALU.min, ALU.max))
            c = ang[64:96, :]
            after(nc.vector.tensor_scalar(turns[64:96, :], c, -1.0, None, ALU.mult))
            after(nc.vector.tensor_tensor(c, c, turns[64:96, :], ALU.max))
            after(nc.vector.tensor_scalar(c, c, -1.0, math.pi / 2.0, ALU.mult, ALU.add))
            after(nc.vector.tensor_scalar(ang[Q, :], ang[Q, :], core.col("rope_sign")[Q, :], None, ALU.mult))

        @st.block.scalar
        def _(act):
            act.wait_ge(done, 12)
            nc.scalar.activation(cs[H, :], ang[H, :], ACT.Sin).then_inc(looked, 1)


def layer0(core, xT, silu_c, mean):
    nc = core.nc
    with buffers(core) as outer:
        mod = outer.sb("l0_modulation", [P, 48])
        ada(core, "l0", silu_c, mod)
        modulation(core, "l0", mod, "l0_mix_pre_g", "l0_mix_post_g", "l0_ffn_pre_g", "l0_ffn_post_g")
        with buffers(core) as b:
            catT = b.sb("l0_cat", [P, 12, T])
            lowT = b.sb("l0_lowT", [P, 6, T])
            with buffers(core) as c:
                xbc = c.sb("l0_xbcT", [P, 12, T])
                zT = c.sb("l0_zT", [P, KD, T])
                dt_raw = c.sb("l0_dt_raw", [P, NT * 16])
                with buffers(core) as e:
                    h = e.pair("l0_h", KD)
                    norm(core, "l0_pre", lambda i: xT[:, i, :], [list(range(KD))], mean, None, core.col("eps"),
                         gain=lambda i: mod[:, 8 + i:9 + i], shift=lambda i: mod[:, i:i + 1], pair=h)
                    linear(core, "l0_in", h, parts(
                        (12, convolved(4, lambda i, j: core.col("l0_conv_w", 4 * i + j), lambda i: core.col("l0_conv_b", i),
                                       lambda i, at: xbc[:, i, :])),
                        (8, stored(lambda i, at: zT[:, i, :], ACT.Silu)),
                        (6, stored(lambda i, at: lowT[:, i, :]))), straight=True)
                    linear(core, "l0_dt", h, stored(lambda i, at: dt_raw[:, i * 16:(i + 1) * 16]), by_tokens=True)
                with buffers(core) as e:
                    ssd(core, e, xbc, dt_raw, catT)
                product(core, "l0_gate", KD, lambda i: catT[:, i, :], lambda i: catT[:, i, :], lambda i: zT[:, i, :])
                with buffers(core) as e:
                    m512 = e.sb("mean512", [P, P])
                    fill(core, "l0_m512", [(m512, 1.0 / 512)])
                    norm(core, "l0_ssm", lambda i: catT[:, i, :], [[0, 1, 2, 3], [4, 5, 6, 7]], m512[:],
                         lambda i: catT[:, i, :], core.col("eps"), gain=lambda i: core.col("l0_ssm_norm_g", i))
            with buffers(core) as c:
                m384, m256 = c.sb("mean384", [P, P]), c.sb("mean256", [P, P])
                cs, fold, causal = c.sb("rope_cs", [P, T]), c.sb("fold", [P, P]), c.sb("causal", [P, T])
                fill(core, "l0_means", [(m384, 1.0 / 384), (m256, 1.0 / 256)], [(fold, "fold"), (causal, "causal")])
                rope_table(core, cs)
                qT, kT, vt = c.sb("mla_q", [P, 8, T]), c.sb("mla_k", [P, 8, T]), c.sb("mla_v", [P, NT, 512])
                low = lambda i: lowT[:, i, :]
                norm(core, "l0_qa", low, [[0, 1, 2]], m384[:], low, core.col("eps"), gain=lambda i: core.col("l0_q_a_norm_g", i))
                norm(core, "l0_kva", low, [[3, 4]], m256[:], low, core.col("eps"), gain=lambda i: core.col("l0_kv_a_norm_g", i - 3))

                def rotated(core, st, g):
                    rows_done = st.sem("rows_done")

                    @st.block.scalar
                    def _(act):
                        def take(i, at, turn):
                            act.wait_ge(g.done, i + 1)
                            nc.scalar.activation(qT[0:64, i, :], g.bank(i)[0:64, :], ACT.Copy).then_inc(rows_done, 1)
                        g.run_scalar(act, take)

                    @st.block.vector
                    def _(dve):
                        for i in range(g.count):
                            dve.wait_ge(rows_done, i + 1)
                            nc.vector.tensor_tensor(qT[64:128, i, :], g.bank(i)[64:128, :], cs[64:128, :], ALU.mult
                                                    ).then_inc(g.free, 1)

                linear(core, "l0_q", low, rotated, raw=True)
                linear(core, "l0_k", lambda k: lowT[:, 3 + k, :], stored(lambda i, at: kT[0:64, i, :]))
                linear(core, "l0_v", lambda k: lowT[:, 3 + k, :], stored(lambda i, at: vt[:, i, :]), by_tokens=True)
                with core.stage("l0_krope") as st:
                    rotated_k, folded, spread = st.sem("rotated"), st.sem("folded"), st.sem("spread")

                    @st.block.vector
                    def _(dve):
                        nc.vector.tensor_tensor(lowT[64:128, 5, :], lowT[64:128, 5, :], cs[64:128, :], ALU.mult
                                                ).then_inc(rotated_k, 1)

                    @st.block.tensor
                    def _(pe):
                        pe.wait_ge(rotated_k, 1)
                        nc.tensor.matmul(core.bank(0), fold[64:128, :], lowT[64:128, 5, :], start=True, stop=True
                                         ).then_inc(folded, 1)

                    @st.block.scalar
                    def _(act):
                        act.wait_ge(folded, 1)
                        for i in range(8):
                            nc.scalar.activation(kT[64:128, i, :], core.psum[64:128, 0, :], ACT.Copy).then_inc(spread, 1)
                units = []
                for i in range(8):
                    for q in range(NT):
                        n = (q + 1) * P
                        keys = Keys(qT[:, i, q * P:n], kT[:, i, 0:n], lambda kb, i=i: vt[:, kb, 64 * i:64 * i + 64], n,
                                    causal[:, T - n:T], 96.0 ** -0.5)
                        units.append(([keys], catT[64 * (i % 2):64 * (i % 2) + 64, 8 + i // 2, q * P:n]))
                attention(core, "mla", units)
            mixT = b.sb("l0_mixT", [P, KD, T])
            linear(core, "l0_out", lambda k: catT[:, k, :], stored(lambda i, at: mixT[:, i, :]), raw=True)
            norm(core, "l0_post", lambda i: mixT[:, i, :], [list(range(KD))], mean, lambda i: xT[:, i, :], core.col("eps"),
                 gain=lambda i: mod[:, 16 + i:17 + i], residual=True)
        swiglu(core, "l0", xT, mod, mean)


def fill(core, name, constants, tables=()):
    nc = core.nc
    with core.stage(name) as st:
        filled, loaded = st.sem("filled"), st.sem("loaded")

        @st.block.vector
        def _(dve):
            for buf, value in constants:
                nc.vector.memset(buf[:], value).then_inc(filled, 1)

        @st.block.sync
        def _(sp):
            for buf, table in tables:
                src = core.dram[table] if isinstance(table, str) else table
                sp.dma_start(buf[:], src).then_inc(loaded, 16)
            if tables:
                sp.wait_ge(loaded, 16 * len(tables))


GLA_H = 4
SUB = 32
NSUB = P // SUB
CMP = 31


def gla_decays(core, lr, cum):
    nc = core.nc
    with core.stage("gla_decays") as st:
        gk2 = st.sb("gk2", [16, T])
        z = st.sb("z", [P, GLA_H, T])
        soft = st.sb("soft", [P, GLA_H, T])
        loaded, logits, raw, looked, low, scaled, scanned = (st.sem(s) for s in (
            "loaded", "logits", "raw", "looked", "low", "scaled", "scanned"))

        @st.block.sync
        def _(sp):
            sp.dma_start(gk2[:], core.dram["gk2"]).then_inc(loaded, 16)

        @st.block.tensor
        def _(pe):
            pe.wait_ge(loaded, 16)
            for i in range(GLA_H):
                nc.tensor.matmul(core.bank(i), gk2[:, i * P:(i + 1) * P], lr[:], start=True, stop=True).then_inc(logits, 1)

        @st.block.scalar
        def _(act):
            for i in range(GLA_H):
                act.wait_ge(logits, i + 1)
                nc.scalar.activation(z[:, i, :], core.bank(i), ACT.Identity, bias=core.col("l1_b_gk", i)).then_inc(raw, 1)
            for n, (func, scale, bias) in enumerate(((ACT.Abs, 1.0, None), (ACT.Exp, -1.0, None), (ACT.Ln, 1.0, core.col("one")))):
                for i in range(GLA_H):
                    act.wait_ge(raw, i + 1)
                    if n:
                        act.wait_ge(looked, (n - 1) * GLA_H + i + 1)
                    src = z[:, i, :] if n == 0 else soft[:, i, :]
                    kw = {} if bias is None else {"bias": bias}
                    nc.scalar.activation(soft[:, i, :], src, func, scale=scale, **kw).then_inc(looked, 1)

        @st.block.vector
        def _(dve):
            for i in range(GLA_H):
                dve.wait_ge(looked, 2 * GLA_H + i + 1)
                nc.vector.scalar_tensor_tensor(out=z[:, i, :], in0=z[:, i, :], scalar=0.0, in1=soft[:, i, :], op0=ALU.min,
                                               op1=ALU.subtract).then_inc(low, 1)
                dve.wait_ge(low, i + 1)
                nc.vector.tensor_scalar(z[:, i, :], z[:, i, :], 1.0 / 16.0, None, ALU.mult).then_inc(scaled, 1)
                dve.wait_ge(scaled, i + 1)
                for c in range(NT):
                    s = slice(c * P, (c + 1) * P)
                    nc.vector.tensor_tensor_scan(cum[:, i, s], core.ones[:], z[:, i, s], 0.0, ALU.mult, ALU.add
                                                 ).then_inc(scanned, 1)


def gla(core, qk, v, cum, y):
    nc = core.nc
    H = GLA_H
    scale = 128.0 ** -0.5
    with core.stage("gla") as st:
        R = 5
        near = st.sb("near", [P, R, P])
        end = st.sb("end", [P, R, P])
        far = st.sb("far", [P, R, 192])
        near_k = st.sb("near_k", [P, R, P])
        start_q = st.sb("start_q", [P, R, P])
        q_in = st.sb("q_in", [P, R, P])
        left = st.sb("left", [P, R, P])
        left_tok = st.sb("left_tok", [P, R, P])
        att = st.sb("att", [P, R, P])
        upper = st.sb("upper", [P, P])
        state = st.sb("state", [P, H, 256])
        (tables, zeroed, diffed, clamped, grown, q_scaled, k_scaled, scored, left_turned, left_out, masked, mixed, stored_,
         added_, updated) = (st.sem(s) for s in (
             "tables", "zeroed", "diffed", "clamped", "grown", "q_scaled", "k_scaled", "scored", "left_turned", "left_out",
             "masked", "mixed", "stored", "added", "updated"))
        U = NT * H
        off = [0, 96, 160]

        def of(u):
            return u // H, u % H, slice(u // H * P, (u // H + 1) * P)

        @st.block.sync
        def _(sp):
            sp.dma_start(upper[:], core.dram["upper"]).then_inc(tables, 16)

        @st.block.tensor
        def _(pe):
            for phase, u in lagged(U, {1: 2, 2: 3}):
                c, h, s = of(u)
                if phase == 1:
                    pe.wait_ge(q_scaled, 5 * (u + 1))
                    pe.wait_ge(k_scaled, 3 * (u + 1))
                    if u >= 2:
                        pe.wait_ge(masked, 4 * (u - 1))
                    for j in range(NSUB):
                        a, b = SUB * j, SUB * (j + 1)
                        mm = nc.tensor.matmul(core.psum[a:b, u % 2, a:b], near_k[:, u % R, a:b], near[:, u % R, a:b],
                                              start=True, stop=True)
                        if j < NSUB - 1:
                            mm = nc.tensor.matmul(core.psum[a:b, u % 2, b:P], end[:, u % R, a:b],
                                                  far[:, u % R, off[j]:off[j] + P - b], start=True, stop=True)
                    mm.then_inc(scored, 1)
                    if u >= 2:
                        pe.wait_ge(left_out, u - 1)
                    nc.tensor.transpose(core.psum[:, 2 + u % 2, 0:P], left[:, u % R, :], core.ident[:]).then_inc(left_turned, 1)
                elif phase == 2:
                    pe.wait_ge(masked, 4 * (u + 1))
                    if u >= 2:
                        pe.wait_ge(stored_, u - 1)
                    if c > 0:
                        pe.wait_ge(updated, u - H + 1)
                    for n in range(2):
                        out = core.psum[:, 4 + u % 2, n * P:(n + 1) * P]
                        if c > 0:
                            nc.tensor.matmul(out, state[:, h, n * P:(n + 1) * P], q_in[:, u % R, :], start=True, stop=False)
                        mm = nc.tensor.matmul(out, v[:, c, h * 256 + n * P:h * 256 + (n + 1) * P], att[:, u % R, :],
                                              start=(c == 0), stop=True)
                    mm.then_inc(mixed, 1)
                    pe.wait_ge(left_out, u + 1)
                    if u >= 2:
                        pe.wait_ge(updated, u - 1)
                    nc.tensor.matmul(core.psum[:, 6 + u % 2, 0:256], left_tok[:, u % R, :], v[:, c, h * 256:(h + 1) * 256],
                                     start=True, stop=True).then_inc(added_, 1)

        @st.block.vector
        def _(dve):
            nc.vector.memset(att[:], 0.0).then_inc(zeroed, 1)
            nc.vector.memset(state[:], 0.0).then_inc(zeroed, 1)
            dve.wait_ge(zeroed, 2)
            dve.wait_ge(tables, 16)
            for phase, u in lagged(U, {0: 0, 1: 2, 2: 3, 3: 4}):
                c, h, s = of(u)
                b = cum[:, h, s].rearrange("p (j t) -> p j t", t=SUB)
                if phase == 0:
                    if u >= R:
                        dve.wait_ge(scored, u - R + 1)
                    slot = lambda x: x[:, u % R, :].rearrange("p (j t) -> p j t", t=SUB)
                    mid, last = b[:, :, 15:16].to_broadcast([P, NSUB, SUB]), b[:, :, 31:32].to_broadcast([P, NSUB, SUB])
                    nc.vector.tensor_tensor(slot(near), b, mid, ALU.subtract).then_inc(clamped, 1)
                    nc.vector.tensor_tensor(slot(end), last, b, ALU.subtract).then_inc(diffed, 1)
                    for j in range(NSUB - 1):
                        a, z = SUB * (j + 1), off[j]
                        nc.vector.tensor_scalar(far[:, u % R, z:z + P - a], cum[:, h, c * P + a:(c + 1) * P],
                                                cum[:, h, c * P + a - 1:c * P + a], None, ALU.subtract).then_inc(diffed, 1)
                    dve.wait_ge(clamped, u + 1)
                    nc.vector.tensor_scalar(near[:, u % R, :], near[:, u % R, :], 80.0, -80.0, ALU.min, ALU.max
                                            ).then_inc(diffed, 1)
                elif phase == 1:
                    dve.wait_ge(grown, 6 * (u + 1))
                    if u >= R:
                        dve.wait_ge(mixed, u - R + 1)
                    q = qk[:, h, s]

                    def scaled(out, x, e):
                        nc.vector.scalar_tensor_tensor(out=out, in0=x, scalar=scale, in1=e, op0=ALU.mult, op1=ALU.mult
                                                       ).then_inc(q_scaled, 1)

                    scaled(near[:, u % R, :], q, near[:, u % R, :])
                    for j in range(NSUB - 1):
                        f = far[:, u % R, off[j]:off[j] + P - SUB * (j + 1)]
                        scaled(f, qk[:, h, c * P + SUB * (j + 1):(c + 1) * P], f)
                    scaled(q_in[:, u % R, :], q, start_q[:, u % R, :])
                elif phase == 2:
                    dve.wait_ge(scored, u + 1)
                    for j in range(NSUB):
                        a, z = SUB * j, SUB * (j + 1)
                        nc.vector.tensor_tensor(att[a:z, u % R, a:P], core.psum[a:z, u % 2, a:P], upper[a:z, a:P], ALU.mult
                                                ).then_inc(masked, 1)
                else:
                    dve.wait_ge(added_, u + 1)
                    if u >= H:
                        dve.wait_ge(updated, u - H + 1)
                    nc.vector.scalar_tensor_tensor(out=state[:, h, :], in0=state[:, h, :], scalar=start_q[:, u % R, P - 1:P],
                                                   in1=core.psum[:, 6 + u % 2, 0:256], op0=ALU.mult, op1=ALU.add
                                                   ).then_inc(updated, 1)

        @st.block.scalar
        def _(act):
            for phase, u in lagged(U, {0: 0, 1: 2, 2: 4}):
                c, h, s = of(u)
                if phase == 0:
                    act.wait_ge(diffed, 5 * (u + 1))
                    if u >= R:
                        act.wait_ge(updated, u - R + 1)
                        act.wait_ge(left_turned, u - R + 1)
                        act.wait_ge(scored, u - R + 1)
                        act.wait_ge(q_scaled, 5 * (u - R + 1))
                    b = cum[:, h, s]
                    for out, src, sc, bias in ((near_k, near, -1.0, None), (near, near, 1.0, None), (end, end, 1.0, None),
                                               (far, far, 1.0, None), (start_q, None, 1.0, None), (left, None, -1.0, 1)):
                        x = b if src is None else src[:, u % R, :]
                        kw = {"bias": cum[:, h, (c + 1) * P - 1:(c + 1) * P]} if bias else {}
                        if out is near:
                            act.wait_ge(grown, 6 * u + 1)
                        nc.scalar.activation(out[:, u % R, :], x, ACT.Exp, scale=sc, **kw).then_inc(grown, 1)
                elif phase == 1:
                    act.wait_ge(left_turned, u + 1)
                    if u >= R:
                        act.wait_ge(added_, u - R + 1)
                    nc.scalar.activation(left_tok[:, u % R, :], core.psum[:, 2 + u % 2, 0:P], ACT.Copy).then_inc(left_out, 1)
                else:
                    act.wait_ge(mixed, u + 1)
                    nc.scalar.activation(y[:, 2 * h:2 * h + 2, s], core.psum[:, 4 + u % 2, 0:256].rearrange(
                        "p (n t) -> p n t", n=2), ACT.Copy).then_inc(stored_, 1)

        @st.block.gpsimd
        def _(pool):
            for u in range(U):
                c, h, s = of(u)
                pool.wait_ge(grown, 6 * (u + 1))
                for x in (near_k, end, left):
                    nc.gpsimd.tensor_tensor(x[:, u % R, :], qk[:, 4 + h, s], x[:, u % R, :], ALU.mult).then_inc(k_scaled, 1)


def windows(core, name, src, z):
    nc = core.nc
    with core.stage(name) as st:
        copied, placed = st.sem("copied"), st.sem("placed")

        @st.block.scalar
        def _(act):
            for g in range(2):
                for odd in range(2):
                    rows = src[64 * g:64 * g + 64, :].rearrange("p (n l) -> p l n", l=16)
                    for far in range(2):
                        nc.scalar.activation(z[64 * odd:64 * odd + 64, 8 * far:8 * far + 8, g * CMP:(g + 1) * CMP],
                                             rows[:, odd:16:2, far:far + CMP], ACT.Copy).then_inc(copied, 1)

        @st.block.vector
        def _(dve):
            dve.wait_ge(copied, 8)
            nc.vector.tensor_tensor(z[:], z[:], core.colblock("l1_cmp_pos").unsqueeze(2).to_broadcast([P, 16, 2 * CMP]), ALU.add
                                    ).then_inc(placed, 1)


def layer1(core, xT, silu_c, mean):
    nc = core.nc
    with buffers(core) as outer:
        mod = outer.sb("l1_modulation", [P, 48])
        ada(core, "l1", silu_c, mod)
        modulation(core, "l1", mod, "l1_mix_pre_g", "l1_mix_post_g", "l1_ffn_pre_g", "l1_ffn_post_g")
        with buffers(core) as b:
            catT = b.sb("l1_cat", [P, 12, T])
            nfT = b.sb("nsa_f", [P, 8, T])
            ntk = b.sb("nsa_t", [P, NT, 280])
            with buffers(core) as c:
                qk, gv, gg, lr = c.sb("gla_qk", [P, 8, T]), c.sb("gla_v", [P, NT, 1024]), c.sb("gla_g", [P, 8, T]), c.sb("gla_lr", [16, T])
                with buffers(core) as e:
                    h = e.pair("l1_h", KD)
                    norm(core, "l1_pre", lambda i: xT[:, i, :], [list(range(KD))], mean, None, core.col("eps"),
                         gain=lambda i: mod[:, 8 + i:9 + i], shift=lambda i: mod[:, i:i + 1], pair=h)
                    linear(core, "l1_v", h, stored(lambda i, at: gv[:, i % NT, i // NT * 256:(i // NT + 1) * 256]), by_tokens=True)
                    linear(core, "l1_lr", h, stored(lambda i, at: lr[:, :]))
                    linear(core, "l1_in", h, parts((8, stored(lambda i, at: qk[:, i, :])),
                                                   (8, stored(lambda i, at: gg[:, i, :], ACT.Silu)),
                                                   (8, stored(lambda i, at: nfT[:, i, :]))))
                    linear(core, "l1_nt", h, stored(lambda i, at: ntk[:, i, :]), by_tokens=True)
                with buffers(core) as e:
                    cum = e.sb("gla_cum", [P, GLA_H, T])
                    gla_decays(core, lr, cum)
                    gla(core, qk, gv, cum, catT)
                with buffers(core) as e:
                    m256 = e.sb("mean256_l1", [P, P])
                    fill(core, "l1_m256", [(m256, 1.0 / 256)])
                    norm(core, "l1_gla", lambda i: catT[:, i, :], [[0, 1], [2, 3], [4, 5], [6, 7]], m256[:],
                         lambda i: catT[:, i, :], core.col("eps"), gain=lambda i: core.col("l1_gla_norm_g", i % 2),
                         times=lambda i: gg[:, i, :])
            with buffers(core) as c:
                alibi, cmp_bias, cmp_valid = c.sb("alibi", [P, T]), c.sb("cmp_bias", [P, NT, CMP]), c.sb("cmp_valid", [P, NT, CMP])
                w2 = c.sb("cmp_w2", [P, 4, 64])
                hid = c.sb("cmp_hidden", [P, 2, 2, 2 * CMP])
                k_cmp, v_cmp = c.sb("k_cmp", [P, CMP]), c.sb("v_cmp", [P, 2, 64])
                fill(core, "nsa_tables", [(v_cmp, 0.0)], [(alibi, "alibi"), (cmp_bias, "cmp_bias"), (cmp_valid, "cmp_valid"),
                                                          (w2, "cmp_w2")])
                with buffers(core) as e:
                    z = [e.sb(f"windows{n}", [P, 16, 2 * CMP]) for n in range(2)]
                    for n, kind in enumerate("kv"):
                        windows(core, f"cmp_{kind}_windows", nfT[:, 4 + n, :], z[n])
                        linear(core, f"l1_cmp_{kind}", lambda k, n=n: z[n][:, k, :],
                               stored(lambda i, at, n=n: hid[:, n, i, :], ACT.Silu), width=2 * CMP)
                with core.stage("cmp_out") as st:
                    multiplied, out_done, gates_done = st.sem("multiplied"), st.sem("out_done"), st.sem("gates_done")

                    @st.block.tensor
                    def _(pe):
                        for g in range(2):
                            cols = slice(g * CMP, (g + 1) * CMP)
                            for k in range(2):
                                mm = nc.tensor.matmul(core.psum[64 * g:64 * g + 64, g, 0:CMP], w2[:, k, :], hid[:, 0, k, cols],
                                                      start=(k == 0), stop=(k == 1))
                            mm.then_inc(multiplied, 1)
                            for k in range(2):
                                mm = nc.tensor.matmul(core.psum[0:CMP, 2 + g, 0:64], hid[:, 1, k, cols], w2[:, 2 + k, :],
                                                      start=(k == 0), stop=(k == 1))
                            mm.then_inc(multiplied, 1)

                    @st.block.scalar
                    def _(act):
                        nc.scalar.activation(ntk[:, :, 256:280], ntk[:, :, 256:280], ACT.Sigmoid).then_inc(gates_done, 1)
                        for g in range(2):
                            act.wait_ge(multiplied, 2 * g + 2)
                            nc.scalar.activation(k_cmp[64 * g:64 * g + 64, :], core.psum[64 * g:64 * g + 64, g, 0:CMP], ACT.Copy
                                                 ).then_inc(out_done, 1)
                            nc.scalar.activation(v_cmp[0:CMP, g, :], core.psum[0:CMP, 2 + g, 0:64], ACT.Copy).then_inc(out_done, 1)
                units = []
                for g in range(2):
                    for j in range(4):
                        rows, head = slice(64 * g, 64 * g + 64), 4 * g + j
                        slope = 2.0 ** -(head + 1)
                        for q in range(NT):
                            n = (q + 1) * P
                            query = nfT[rows, j, q * P:n]
                            gate = lambda s: ntk[:, q, 256 + 3 * head + s:257 + 3 * head + s]
                            bias = alibi[:, T - n:T]
                            sets = [
                                Keys(query, k_cmp[rows, :], lambda kb, g=g: v_cmp[:, g, :], CMP, cmp_bias[:, q, :], 0.125,
                                     slope, gate(0), cmp_valid[:, q, :]),
                                Keys(query, nfT[rows, 6, 0:n], lambda kb, g=g: ntk[:, kb, 64 * g:64 * g + 64], n, bias, 0.125,
                                     slope, gate(1)),
                                Keys(query, nfT[rows, 7, 0:n], lambda kb, g=g: ntk[:, kb, 128 + 64 * g:192 + 64 * g], n, bias,
                                     0.125, slope, gate(2)),
                            ]
                            units.append((sets, catT[rows, 8 + j, q * P:n]))
                attention(core, "nsa", units)
            mixT = b.sb("l1_mixT", [P, KD, T])
            linear(core, "l1_out", lambda k: catT[:, k, :], stored(lambda i, at: mixT[:, i, :]), raw=True)
            norm(core, "l1_post", lambda i: mixT[:, i, :], [list(range(KD))], mean, lambda i: xT[:, i, :], core.col("eps"),
                 gain=lambda i: mod[:, 16 + i:17 + i], residual=True)
        swiglu(core, "l1", xT, mod, mean)


def two_convolutions(long_taps, long_weight, long_bias, long_dst, short_taps, short_weight, short_dst):
    def epilogue(core, st, g):
        nc = core.nc
        long_pad, short_pad = long_taps - 1, short_taps - 1
        gate, c = st.sb("gate", [P, 2, T]), st.sb("c", [P, 2, T])
        long_raw, short_raw = st.sb("long_raw", [P, long_pad + T]), st.sb("short_raw", [P, short_pad + T])
        long_acc, short_acc = st.sb("long_acc", [P, 2, T]), st.sb("short_acc", [P, T])
        gate_done, c_done, filled, long_tap, short_tap, tile_done, zeroed = (st.sem(n) for n in (
            "gate_done", "c_done", "filled", "long_tap", "short_tap", "tile_done", "zeroed"))
        tiles = g.count // 5

        @st.block.scalar
        def _(act):
            def finished(i):
                act.wait_ge(long_tap, (i + 1) * long_taps)
                nc.scalar.activation(long_dst(i), long_acc[:, i % 2, :], ACT.Identity, bias=long_bias(i)).then_inc(tile_done, 1)

            def take(group, at, turn):
                i, part = at // 5, at % 5
                if part == 0:
                    act.wait_ge(g.done, at + 1)
                    if i >= 2:
                        act.wait_ge(g.free, 5 * (i - 2) + 2)
                    nc.scalar.activation(gate[:, i % 2, :], g.bank(at), ACT.Sigmoid).then_inc(gate_done, 1)
                elif part == 2:
                    act.wait_ge(g.done, at + 1)
                    if i >= 2:
                        act.wait_ge(filled, i - 1)
                    nc.scalar.activation(c[:, i % 2, :], g.bank(at), ACT.Copy).then_inc(c_done, 1)
                elif part == 4 and i >= 1:
                    finished(i - 1)
            g.run_scalar(act, take)
            if g.count < g.total:
                g.later.append((g.count + 5, lambda: finished(tiles - 1)))
            else:
                finished(tiles - 1)

        @st.block.vector
        def _(dve):
            nc.vector.memset(long_raw[:, 0:long_pad], 0.0).then_inc(zeroed, 1)
            nc.vector.memset(short_raw[:, 0:short_pad], 0.0).then_inc(zeroed, 1)
            dve.wait_ge(zeroed, 2)

            def convolve(i, taps, raw, acc, weight, tap_done):
                for j in range(taps):
                    x = raw[:, j:j + T]
                    if j == 0:
                        ins = nc.vector.tensor_scalar(acc, x, weight(i, 0), None, ALU.mult)
                    else:
                        dve.wait_ge(tap_done, i * taps + j)
                        ins = nc.vector.scalar_tensor_tensor(out=acc, in0=x, scalar=weight(i, j), in1=acc, op0=ALU.mult,
                                                             op1=ALU.add)
                    ins.then_inc(tap_done, 1)

            def short_part(i):
                dve.wait_ge(g.done, 5 * i + 4)
                dve.wait_ge(c_done, i + 1)
                if i >= 1:
                    dve.wait_ge(short_tap, i * short_taps)
                nc.vector.tensor_tensor(short_raw[:, short_pad:], g.bank(5 * i + 3), c[:, i % 2, :], ALU.mult
                                        ).then_inc(filled, 1)
                dve.wait_ge(filled, i + 1)
                if i >= 1:
                    dve.wait_ge(g.free, 5 * i)
                convolve(i, short_taps, short_raw, short_acc[:], short_weight, short_tap)
                dve.wait_ge(short_tap, (i + 1) * short_taps)
                dve.wait_ge(g.done, 5 * i + 5)
                nc.vector.tensor_tensor(short_dst(i), g.bank(5 * i + 4), short_acc[:], ALU.mult).then_inc(g.free, 3)

            for i in range(tiles):
                dve.wait_ge(g.done, 5 * i + 2)
                dve.wait_ge(gate_done, i + 1)
                if i >= 1:
                    dve.wait_ge(long_tap, i * long_taps)
                nc.vector.tensor_tensor(long_raw[:, long_pad:], g.bank(5 * i + 1), gate[:, i % 2, :], ALU.mult
                                        ).then_inc(g.free, 2)
                dve.wait_ge(g.free, 5 * i + 2)
                if i == tiles - 1:
                    short_part(i)
                if i >= 2:
                    dve.wait_ge(tile_done, i - 1)
                convolve(i, long_taps, long_raw, long_acc[:, i % 2, :], long_weight, long_tap)
                if i < tiles - 1:
                    short_part(i)
    return epilogue


def scaled_to(dst, scale):
    def epilogue(core, st, g):
        @st.block.vector
        def _(dve):
            for i in range(g.count):
                dve.wait_ge(g.done, i + 1)
                core.nc.vector.tensor_tensor(dst(i), g.bank(i), scale(i), ALU.mult).then_inc(g.free, 1)
    return epilogue


def conv_ffn(core, name, xT, mean):
    with buffers(core) as b:
        a = b.pair(name + "_act", 22)

        def tap(i, j):
            return core.col(name + "_ffn_dw_w", i * 3 + j)

        with buffers(core) as c:
            h = c.pair(name + "_fh", KD)
            norm(core, name + "_fpre", lambda i: xT[:, i, :], [list(range(KD))], mean, None, core.col("eps"),
                 gain=lambda i: core.col(name + "_norm2_g", i), pair=h)
            linear(core, name + "_up", h, gated(a, ACT.Silu, 3, tap))
        linear(core, name + "_down", a, added(lambda i: xT[:, i, :]))
        norm(core, name + "_final", lambda i: xT[:, i, :], [list(range(KD))], mean, lambda i: xT[:, i, :], core.col("eps"),
             gain=lambda i: core.col(name + "_final_g", i))


def block2(core, xT, mean):
    nc = core.nc
    with buffers(core) as b:
        h = b.pair("b2_h", KD)
        attT, confT, shortT = b.sb("b2_att", [P, 2, T]), b.sb("b2_confT", [P, 6, T]), b.sb("b2_short", [P, 6, T])
        norm(core, "b2_pre", lambda i: xT[:, i, :], [list(range(KD))], mean, None, core.col("eps"),
             gain=lambda i: core.col("b2_norm1_g", i), pair=h)
        with buffers(core) as c:
            qk, v, bias = c.sb("b2_q_k", [P, 12, T]), c.sb("b2_v_t", [P, NT, 768]), c.sb("b2_bias", [P, 12, T])
            fill(core, "b2_tables", [], [(bias, "dilated")])
            linear(core, "b2_qk", h, stored(lambda i, at: qk[:, i, :]))
            linear(core, "b2_v", h, stored(lambda i, at: v[:, i % NT, i // NT * 256:(i // NT + 1) * 256]), by_tokens=True)
            units = []
            for hd in range(4):
                rows = slice(64 * (hd % 2), 64 * (hd % 2) + 64)
                for q in range(NT):
                    n = (q + 1) * P
                    sets = [Keys(qk[rows, 2 * g + hd // 2, q * P:n], qk[rows, 6 + 2 * g + hd // 2, 0:n],
                                 lambda kb, g=g, hd=hd: v[:, kb, 256 * g + 64 * hd:256 * g + 64 * hd + 64], n,
                                 bias[:, 4 * g + hd, T - n:T], 0.125) for g in range(3)]
                    units.append((sets, attT[rows, hd // 2, q * P:n]))
            attention(core, "dilated", units, joint=True, W=1)
        gT = b.sb("b2_gates", [P, 3 * KD, T])
        linear(core, "b2_conf_sc", h, parts((30, two_convolutions(
            31, lambda i, j: core.col("b2_conf_w", 31 * i + j), lambda i: core.col("b2_conf_b", i), lambda i: confT[:, i, :],
            3, lambda i, j: core.col("b2_sc_w", 3 * i + j), lambda i: shortT[:, i, :])),
            (3 * KD, stored(lambda i, at: gT[:, i, :], ACT.Sigmoid))), straight=True)
        with buffers(core) as c:
            m768 = c.sb("mean768", [P, P])
            fill(core, "b2_m768", [(m768, 1.0 / 768)])
            norm(core, "b2_ln", lambda i: confT[:, i, :], [list(range(6))], m768[:], lambda i: confT[:, i, :], core.col("eps"),
                 gain=lambda i: core.col("b2_ln_g", i), shift=lambda i: core.col("b2_ln_b", i), center=m768[:], last=ACT.Silu)
        mix = lambda i: gT[:, i, :]
        for n, (branch, src) in enumerate((("b2_attn_out", attT), ("b2_conf_out", confT), ("b2_sc_out", shortT))):
            gate = lambda i, n=n: gT[:, KD * n + i, :]
            linear(core, branch, lambda k, src=src: src[:, k, :], added(mix, gate) if n else scaled_to(mix, gate),
                   raw=True, room=h)
        linear(core, "b2_o", mix, added(lambda i: xT[:, i, :]), raw=True, room=h)
    conv_ffn(core, "b2", xT, mean)


LEVELS = 7


def token_shifted(mu, dst):
    def epilogue(core, st, g):
        nc = core.nc
        raw = st.sb("raw", [P, 2, 1 + T])
        diff = st.sb("diff", [P, 2, T])
        diffed, moved, zeroed = st.sem("diffed"), st.sem("moved"), st.sem("zeroed")

        @st.block.scalar
        def _(act):
            def take(i, at, turn):
                act.wait_ge(g.done, i + 1)
                if at >= 2:
                    act.wait_ge(moved, i - 1)
                nc.scalar.activation(raw[:, at % 2, 1:], g.bank(at), ACT.Copy).then_inc(g.free, 1)
            g.run_scalar(act, take)

        @st.block.vector
        def _(dve):
            nc.vector.memset(raw[:, :, 0:1], 0.0).then_inc(zeroed, 1)
            dve.wait_ge(zeroed, 1)
            for i in range(g.count):
                dve.wait_ge(g.free, i + 1)
                x = raw[:, i % 2, 1:]
                nc.vector.tensor_tensor(diff[:, i % 2, :], raw[:, i % 2, 0:T], x, ALU.subtract).then_inc(diffed, 1)
                dve.wait_ge(diffed, i + 1)
                nc.vector.scalar_tensor_tensor(out=dst(i), in0=diff[:, i % 2, :], scalar=mu(i), in1=x, op0=ALU.mult,
                                               op1=ALU.add).then_inc(moved, 1)
    return epilogue


def solve(core, name, n, lt, xt, sign, lanes=4, room=None):
    nc = core.nc
    LANES = lanes

    def banks(lane):
        first = core.psum[:, lane, 0:P]
        return (first, core.psum[:, 4 + lane, 0:2 * P]) if LANES == 4 else (first, core.psum[:, lane, P:3 * P])

    assert n % LANES == 0
    with core.stage(name) as st:
        joins = st.sb("joins", [P, LEVELS, P])
        mt = st.sb("mt", [P, LANES, 2, P])
        y = st.sb("y", [P, LANES, P])
        x = room if room is not None else st.sb("x", [P, LANES, 2, P])
        tables, masked, multiplied, copied, squared, grown, finished = (st.sem(s) for s in (
            "tables", "masked", "multiplied", "copied", "squared", "grown", "finished"))
        steps = [(w, k, lane) for w in range(n // LANES) for k in range(LEVELS) for lane in range(LANES)]
        op = ALU.subtract if sign > 0 else ALU.add

        @st.block.sync
        def _(sp):
            sp.dma_start(joins[:], core.dram["joins"]).then_inc(tables, 16)

        @st.block.gpsimd
        def _(pool):
            pool.wait_ge(tables, 16)
            for i, (w, k, lane) in enumerate(steps):
                if i >= 2 * LANES:
                    pool.wait_ge(multiplied, i - 2 * LANES + 1)
                    pool.wait_ge(grown, i - 2 * LANES + 1)
                nc.gpsimd.tensor_tensor(mt[:, lane, k % 2 if w % 2 == 0 else (k + 1) % 2, :], lt(w * LANES + lane),
                                        joins[:, k, :], ALU.mult).then_inc(masked, 1)

        def slot(w, k):
            return (w * LEVELS + k) % 2

        @st.block.tensor
        def _(pe):
            for w in range(n // LANES):
                for k in range(LEVELS):
                    for part in range(2):
                        for lane in range(LANES):
                            i = (w * LEVELS + k) * LANES + lane
                            if part == 0:
                                pe.wait_ge(masked, i + 1)
                                if i >= LANES:
                                    pe.wait_ge(grown, i - LANES + 1)
                                    pe.wait_ge(copied, i - LANES + 1)
                                m = mt[:, lane, slot(w, k), :]
                                if k:
                                    mm = nc.tensor.matmul(banks(lane)[0], m, x[:, lane, 0, :], start=True, stop=True)
                                else:
                                    mm = nc.tensor.transpose(banks(lane)[0], m, core.ident[:])
                                mm.then_inc(multiplied, 1)
                            elif k:
                                pe.wait_ge(copied, i + 1)
                                if k < LEVELS - 1:
                                    nc.tensor.matmul(banks(lane)[1][:, 0:P], x[:, lane, 1, :], y[:, lane, :],
                                                     start=True, stop=True)
                                nc.tensor.matmul(banks(lane)[1][:, P:2 * P], y[:, lane, :], x[:, lane, 1, :],
                                                 start=True, stop=True).then_inc(squared, 1)

        @st.block.scalar
        def _(act):
            for i, (w, k, lane) in enumerate(steps):
                act.wait_ge(multiplied, i + 1)
                if i >= LANES:
                    act.wait_ge(grown, i - LANES + 1)
                nc.scalar.activation(y[:, lane, :], banks(lane)[0], ACT.Copy).then_inc(copied, 1)

        @st.block.vector
        def _(dve):
            for i, (w, k, lane) in enumerate(steps):
                both = x[:, lane, :, :].rearrange("p a b -> p (a b)")
                if k == 0:
                    dve.wait_ge(copied, i + 1)
                    if w:
                        dve.wait_ge(grown, i - LANES + 1)
                    nc.vector.tensor_tensor(x[:, lane, 0, :], core.ident[:], y[:, lane, :], op).then_inc(finished, 1)
                    nc.vector.tensor_tensor(x[:, lane, 1, :], core.ident[:], mt[:, lane, slot(w, k), :], op).then_inc(grown, 1)
                elif k < LEVELS - 1:
                    dve.wait_ge(squared, w * (LEVELS - 1) * LANES + (k - 1) * LANES + lane + 1)
                    nc.vector.tensor_tensor(both, both, banks(lane)[1], op).then_inc(grown, 1)
                else:
                    dve.wait_ge(squared, w * (LEVELS - 1) * LANES + (k - 1) * LANES + lane + 1)
                    nc.vector.tensor_tensor(xt(w * LANES + lane), x[:, lane, 1, :], banks(lane)[1][:, P:2 * P], op
                                            ).then_inc(grown, 1)


def rwkv_gates(core, p, sw, a, g):
    nc = core.nc
    with core.stage("rwkv_gates") as st:
        wa, g2 = st.sb("wa", [P, T]), st.sb("g2", [P, T])
        loaded, squashed, logits, out = (st.sem(s) for s in ("loaded", "squashed", "logits", "out"))

        @st.block.sync
        def _(sp):
            sp.dma_start(wa[:], core.dram["rwkv_w2_a2"]).then_inc(loaded, 16)
            sp.dma_start(g2[:], core.dram["rwkv_g2"]).then_inc(loaded, 16)

        @st.block.scalar
        def _(act):
            nc.scalar.activation(p[0:64, 12, :], p[0:64, 12, :], ACT.Tanh).then_inc(squashed, 1)
            nc.scalar.activation(p[:, 13, :], p[:, 13, :], ACT.Sigmoid).then_inc(squashed, 1)
            for i in range(4):
                act.wait_ge(logits, 3 * i + 3)
                nc.scalar.activation(sw[:, i, :], core.bank(3 * i % 6), ACT.Sigmoid, bias=core.col("rwkv_w0", i)).then_inc(out, 1)
                nc.scalar.activation(a[:, i, :], core.bank((3 * i + 1) % 6), ACT.Sigmoid, bias=core.col("rwkv_a0", i)).then_inc(out, 1)
                nc.scalar.activation(g[:, i, :], core.bank((3 * i + 2) % 6), ACT.Copy).then_inc(out, 1)

        @st.block.tensor
        def _(pe):
            pe.wait_ge(loaded, 32)
            pe.wait_ge(squashed, 2)
            for i in range(4):
                c = slice(i * P, (i + 1) * P)
                if i >= 2:
                    pe.wait_ge(out, 3 * (i - 1))
                for j, (w, x) in enumerate(((wa[0:64, c], p[0:64, 12, :]), (wa[64:128, c], p[64:128, 12, :]), (g2[:, c], p[:, 13, :]))):
                    nc.tensor.matmul(core.bank((3 * i + j) % 6), w, x, start=True, stop=True).then_inc(logits, 1)


def rwkv_operands(core, p, sw, a, kk, cum, ar, bh, kh, carry, blocks, tmp2):
    nc = core.nc
    rate = math.exp(-0.5)
    with core.stage("rwkv_operands") as st:
        tmp = st.sb("tmp", [P, 4, T])
        d1, d2 = st.sem("d1"), st.sem("d2")
        scans, exps, bonus = st.sem("scans"), st.sem("exps"), st.sem("bonus")
        halves = st.sem("halves")

        def chunks(x, i):
            return x[:, i, :].rearrange("p (c t) -> p c t", t=P)

        @st.block.vector
        def _(dve):
            m = Marks(d1)
            for i in range(4):
                n = m.mark(nc.vector.tensor_scalar(tmp[:, i, :], a[:, i, :], 1.0, core.col("rwkv_k_a", i), ALU.subtract, ALU.mult))
                used = m.mark(nc.vector.tensor_tensor(bh[:, i, :], kk[:, i, :], a[:, i, :], ALU.mult))
                dve.wait_ge(d1, n)
                n = m.mark(nc.vector.scalar_tensor_tensor(out=p[:, 4 + i, :], in0=tmp[:, i, :], scalar=1.0, in1=p[:, 4 + i, :],
                                                          op0=ALU.add, op1=ALU.mult))
                dve.wait_ge(d1, used)
                n2 = m.mark(nc.vector.tensor_scalar(a[:, i, :], sw[:, i, :], -rate, None, ALU.mult))
                dve.wait_ge(d1, n2)
                for c in range(NT):
                    s = slice(c * P, (c + 1) * P)
                    n = m.mark(nc.vector.tensor_tensor_scan(cum[:, i, s], core.ones[:], a[:, i, s], 0.0, ALU.mult, ALU.add))
                dve.wait_ge(d1, n)
                mid = chunks(cum, i)[:, :, 63:64].to_broadcast([P, NT, P])
                n = m.mark(nc.vector.tensor_tensor(chunks(tmp, i), chunks(cum, i), mid, ALU.subtract))
                dve.wait_ge(d1, n)
                n = m.mark(nc.vector.tensor_tensor(tmp2[:, i, :], tmp[:, i, :], a[:, i, :], ALU.subtract))
                n = m.mark(nc.vector.tensor_copy(carry[:, :, i:i + 1], chunks(tmp, i)[:, :, P - 1:P]))
                dve.wait_ge(d1, n)
                n = m.mark(nc.vector.tensor_tensor(carry[:, 0:NT - 1, i:i + 1], carry[:, 0:NT - 1, i:i + 1],
                                                   chunks(cum, i)[:, 1:NT, 63:64], ALU.add))
                dve.wait_ge(d1, n)
                nc.vector.scalar_tensor_tensor(out=sw[:, i, :], in0=p[:, i, :], scalar=core.col("rwkv_r_k", i),
                                               in1=p[:, 4 + i, :], op0=ALU.mult, op1=ALU.mult).then_inc(scans, 1)
            for i in range(4):
                dve.wait_ge(exps, 4 * i + 4)
                r_part, a_part = ar[:, i, :, 1, :], ar[:, i, :, 0, :]
                nc.vector.scalar_tensor_tensor(out=a_part, in0=chunks(kk, i), scalar=-1.0, in1=chunks(tmp2, i), op0=ALU.mult,
                                               op1=ALU.mult).then_inc(d2, 1)
                nc.vector.tensor_tensor(r_part, chunks(p, i), chunks(tmp, i), ALU.mult).then_inc(d2, 1)
                nc.vector.tensor_tensor(bh[:, i, :], bh[:, i, :], cum[:, i, :], ALU.mult).then_inc(d2, 1)
                nc.vector.tensor_tensor(kh[:, i, :], p[:, 4 + i, :], cum[:, i, :], ALU.mult).then_inc(d2, 1)
            for i in range(4):
                dve.wait_ge(bonus, i + 1)
                dve.wait_ge(d2, 4 * i + 2)
                nc.vector.tensor_tensor(p[:, i, :], core.bank(i), p[:, 8 + i, :], ALU.mult).then_inc(halves, 1)

        @st.block.tensor
        def _(pe):
            for i in range(4):
                pe.wait_ge(scans, i + 1)
                nc.tensor.matmul(core.bank(i), blocks, sw[:, i, :], start=True, stop=True).then_inc(bonus, 1)

        @st.block.scalar
        def _(act):
            for i in range(4):
                act.wait_ge(scans, i + 1)
                nc.scalar.activation(cum[:, i, :], tmp[:, i, :], ACT.Exp, scale=-1.0).then_inc(exps, 1)
                act.wait_ge(exps, 4 * i + 1)
                nc.scalar.activation(tmp[:, i, :], tmp[:, i, :], ACT.Exp).then_inc(exps, 1)
                nc.scalar.activation(tmp2[:, i, :], tmp2[:, i, :], ACT.Exp).then_inc(exps, 1)
                nc.scalar.activation(carry[:, :, i:i + 1], carry[:, :, i:i + 1], ACT.Exp).then_inc(exps, 1)


def rwkv_chunk(core, c, ar, bh, kh, vt, bt, kt, state, carry, y, masks):
    nc = core.nc
    H = 8
    s = slice(c * P, (c + 1) * P)
    with buffers(core) as b:
        pairs = b.sb(f"wkv_pairs{c}", [P, H, 4, P])
        xt = b.sb(f"wkv_xt{c}", [P, H, P])

        with core.stage(f"wkv_pairs_{c}") as st:
            multiplied, masked = st.sem("multiplied"), st.sem("masked")

            @st.block.tensor
            def _(pe):
                for h in range(H):
                    r, i = slice(64 * (h % 2), 64 * (h % 2) + 64), h // 2
                    both = ar[r, i, c, :, :].rearrange("p a t -> p (a t)")
                    nc.tensor.matmul(core.psum[:, h, 0:256], bh[r, i, s], both, start=True, stop=True)
                    nc.tensor.matmul(core.psum[:, h, 256:512], kh[r, i, s], both, start=True, stop=True).then_inc(multiplied, 1)

            @st.block.vector
            def _(dve):
                for h in range(H):
                    dve.wait_ge(multiplied, h + 1)
                    nc.vector.tensor_tensor(pairs[:, h, :, :].rearrange("p a t -> p (a t)"), core.bank(h), masks, ALU.mult
                                            ).then_inc(masked, 1)

        solve(core, f"wkv_solve{c}", H, lambda u: pairs[:, u, 0, :], lambda u: xt[:, u, :], -1)

        with core.stage(f"wkv_scan{c}") as st:
            z, u_ = st.sb("z", [P, H, 64]), st.sb("u", [P, H, 64])
            first, zc, second, uc, mixed, stored_, grew, added_, scaled = (st.sem(n) for n in (
                "first", "z_copied", "second", "u_copied", "mixed", "stored", "grew", "added", "scaled"))

            @st.block.tensor
            def _(pe):
                for phase, h in lagged(H, {0: 0, 1: 1, 2: 2}):
                    r, i = slice(64 * (h % 2), 64 * (h % 2) + 64), h // 2
                    v = vt[:, c, h * 64:(h + 1) * 64]
                    if phase == 0:
                        if h >= 2:
                            pe.wait_ge(zc, h - 1)
                        out = core.psum[:, h % 2, 0:64]
                        if c:
                            nc.tensor.matmul(out, ar[r, i, c, 0, :], state[r, i, :], start=True, stop=False)
                        nc.tensor.matmul(out, pairs[:, h, 2, :], v, start=(c == 0), stop=True).then_inc(first, 1)
                    elif phase == 1:
                        pe.wait_ge(zc, h + 1)
                        if h >= 2:
                            pe.wait_ge(uc, h - 1)
                        nc.tensor.matmul(core.psum[:, 2 + h % 2, 0:64], xt[:, h, :], z[:, h, :], start=True, stop=True
                                         ).then_inc(second, 1)
                    else:
                        pe.wait_ge(uc, h + 1)
                        if h >= 4:
                            pe.wait_ge(stored_, i - 1)
                        out = core.psum[r, 4 + i % 2, 0:P]
                        if c:
                            nc.tensor.matmul(out, state[r, i, :], ar[r, i, c, 1, :], start=True, stop=False)
                        nc.tensor.matmul(out, u_[:, h, :], pairs[:, h, 1, :], start=(c == 0), stop=False)
                        nc.tensor.matmul(out, v, pairs[:, h, 3, :], start=False, stop=True).then_inc(mixed, 1)
                        if c < NT - 1:
                            if h >= 4:
                                pe.wait_ge(added_, i - 1)
                            out = core.psum[r, 6 + i % 2, 0:64]
                            nc.tensor.matmul(out, bt[:, c, h * 64:(h + 1) * 64], u_[:, h, :], start=True, stop=False)
                            nc.tensor.matmul(out, kt[:, c, h * 64:(h + 1) * 64], v, start=False, stop=True).then_inc(grew, 1)

            @st.block.scalar
            def _(act):
                for phase, h in lagged(H, {0: 0, 1: 1, 2: 2}):
                    if phase == 0:
                        act.wait_ge(first, h + 1)
                        nc.scalar.activation(z[:, h, :], core.psum[:, h % 2, 0:64], ACT.Copy).then_inc(zc, 1)
                    elif phase == 1:
                        act.wait_ge(second, h + 1)
                        nc.scalar.activation(u_[:, h, :], core.psum[:, 2 + h % 2, 0:64], ACT.Copy).then_inc(uc, 1)
                    elif h % 2:
                        act.wait_ge(mixed, h + 1)
                        nc.scalar.activation(y[:, h // 2, s], core.psum[:, 4 + h // 2 % 2, 0:P], ACT.Copy).then_inc(stored_, 1)

            @st.block.vector
            def _(dve):
                if c < NT - 1:
                    for i in range(H // 2):
                        dve.wait_ge(grew, 2 * i + 2)
                        dve.wait_ge(mixed, 2 * i + 2)
                        x = state[:, i, :]
                        if c:
                            nc.vector.tensor_tensor(x, core.psum[:, 6 + i % 2, 0:64], x, ALU.add).then_inc(added_, 1)
                        else:
                            nc.vector.tensor_copy(x, core.psum[:, 6 + i % 2, 0:64]).then_inc(added_, 1)
                        dve.wait_ge(added_, i + 1)
                        nc.vector.tensor_scalar(x, x, carry[:, c, i:i + 1], None, ALU.mult).then_inc(scaled, 1)


def scaled_columns(core, name, n, out, x, col):
    nc = core.nc
    with core.stage(name) as st:
        done = st.sem("done")

        @st.block.vector
        def _(dve):
            for i in range(n):
                nc.vector.tensor_scalar(out(i), x(i), col(i), None, ALU.mult).then_inc(done, 1)


def rwkv(core, p, y):
    with buffers(core) as b:
        g, blocks = b.sb("rwkv_g", [P, 4, T]), b.sb("blocks", [P, P])
        mean64, masks = b.sb("mean64", [P, P]), b.sb("wkv_masks", [P, T])
        fill(core, "rwkv_tables", [], [(blocks, "blocks64"), (mean64, "mean64"), (masks, "wkv_masks")])
        with buffers(core) as c:
            ar, bh, kh = c.sb("wkv_ar", [P, 4, NT, 2, P]), c.sb("wkv_b", [P, 4, T]), c.sb("wkv_k", [P, 4, T])
            carry = c.sb("wkv_carry", [P, NT, 4])
            with buffers(core) as d:
                kk = d.sb("rwkv_kk", [P, 4, T])
                sw, a, cum = d.sb("rwkv_sw", [P, 4, T]), d.sb("rwkv_a", [P, 4, T]), d.sb("rwkv_cum", [P, 4, T])
                rwkv_gates(core, p, sw, a, g)
                scaled_columns(core, "rwkv_kk_", 4, lambda i: kk[:, i, :], lambda i: p[:, 4 + i, :], lambda i: core.col("rwkv_k_k", i))
                norm(core, "rwkv_l2", lambda i: kk[:, i, :], [[i] for i in range(4)], blocks[:], lambda i: kk[:, i, :], core.col("eps"))
                rwkv_operands(core, p, sw, a, kk, cum, ar, bh, kh, carry, blocks[:], y)
            with buffers(core) as d:
                vt, bt, kt = p[:, 4:8, :], p[:, 8:12, :], d.sb("wkv_kt", [P, NT, T])
                state = p[:, 12, 0:256].rearrange("p (i d) -> p i d", i=4)
                jobs = [([x[:, t + i, ch * P:(ch + 1) * P] for i in range(4)], out[:, ch, :])
                        for x, t, out in ((p, 8, vt), (bh, 0, bt), (kh, 0, kt)) for ch in range(NT)]
                turned(core, "wkv_turn", jobs)
                for ch in range(NT):
                    rwkv_chunk(core, ch, ar, bh, kh, vt, bt, kt, state, carry, y, masks[:])
        norm(core, "rwkv_gn", lambda i: y[:, i, :], [[i] for i in range(4)], mean64[:], lambda i: y[:, i, :],
             core.col("gn_eps"), gain=lambda i: core.col("rwkv_ln_w", i), shift=lambda i: core.col("rwkv_ln_b", i),
             center=mean64[:])
        nc = core.nc
        with core.stage("rwkv_out") as st:
            summed, done = st.sem("summed"), st.sem("done")

            @st.block.vector
            def _(dve):
                for i in range(4):
                    nc.vector.tensor_tensor(y[:, i, :], y[:, i, :], p[:, i, :], ALU.add).then_inc(summed, 1)
                    dve.wait_ge(summed, i + 1)
                    nc.vector.tensor_tensor(y[:, i, :], y[:, i, :], g[:, i, :], ALU.mult).then_inc(done, 1)


def gated_delta(core, qkv, ab, y):
    nc = core.nc
    H = 4
    U = NT * H
    scale = 128.0 ** -0.5
    with buffers(core) as b:
        beta, ga, acs, ein, dec, etot, eneg = (b.sb(f"gdn_{n}", [P, NT, H]) for n in ("beta", "ga", "acs", "ein", "dec", "etot", "be"))
        upper, strict, masked = b.sb("gdn_upper", [P, P]), b.sb("gdn_strict", [P, P]), b.sb("gdn_masked", [P, P])
        vt, kt = b.sb("gdn_vt", [P, NT, T]), b.sb("gdn_kt", [P, NT, T])
        lt, att, qd, xt = (b.sb(f"gdn_{n}", [P, U, P]) for n in ("lt", "att", "qd", "xt"))
        fill(core, "gdn_tables", [], [(upper, "upper"), (strict, "strict_upper"), (masked, "lower_masked")])
        for n, t in (("q", 0), ("k", 4)):
            norm(core, f"gdn_l2{n}", lambda i, t=t: qkv[:, t + i, :], [[i] for i in range(4)], core.ones[:],
                 lambda i, t=t: qkv[:, t + i, :], core.col("eps"))
        turned(core, "gdn_turn", [([qkv[:, t + i, c * P:(c + 1) * P] for i in range(4)], out[:, c, :])
                                  for t, out in ((8, vt), (4, kt)) for c in range(NT)])

        with core.stage("gdn_rates") as st:
            tmp, rate = st.sb("tmp", [P, NT, H]), st.sb("rate", [P, NT * H])
            dve_done, act_done, pe_done = st.sem("dve_done"), st.sem("act_done"), st.sem("pe_done")

            def flat(x):
                return x[:].rearrange("p c h -> p (c h)")

            @st.block.vector
            def _(dve):
                nc.vector.tensor_tensor(ga[:], ab[:, :, 0:4], core.colblock("gdn_dt_bias").rearrange("p (c h) -> p c h", h=H), ALU.add
                                        ).then_inc(dve_done, 1)
                dve.wait_ge(act_done, 5)
                nc.vector.scalar_tensor_tensor(out=flat(ga), in0=flat(ga), scalar=0.0, in1=flat(tmp), op0=ALU.max, op1=ALU.add
                                               ).then_inc(dve_done, 1)
                dve.wait_ge(dve_done, 2)
                nc.vector.scalar_tensor_tensor(out=flat(ga), in0=flat(ga), scalar=-1.0, in1=rate[:], op0=ALU.mult, op1=ALU.mult
                                               ).then_inc(dve_done, 1)
                dve.wait_ge(pe_done, 2)
                nc.vector.tensor_copy(flat(acs), core.psum[:, 0, 0:U]).then_inc(dve_done, 1)
                dve.wait_ge(dve_done, 4)
                nc.vector.tensor_tensor(flat(dec), core.psum[:, 1, 0:U], flat(acs), ALU.subtract).then_inc(dve_done, 1)
                dve.wait_ge(act_done, 6)
                nc.vector.tensor_tensor(flat(eneg), flat(ein), flat(beta), ALU.mult).then_inc(dve_done, 1)

            @st.block.scalar
            def _(act):
                nc.scalar.activation(beta[:], ab[:, :, 4:8], ACT.Sigmoid).then_inc(act_done, 1)
                nc.scalar.activation(rate[:], core.colblock("gdn_a_log"), ACT.Exp).then_inc(act_done, 1)
                act.wait_ge(dve_done, 1)
                nc.scalar.activation(tmp[:], ga[:], ACT.Abs).then_inc(act_done, 1)
                act.wait_ge(act_done, 3)
                nc.scalar.activation(tmp[:], tmp[:], ACT.Exp, scale=-1.0).then_inc(act_done, 1)
                act.wait_ge(act_done, 4)
                nc.scalar.activation(tmp[:], tmp[:], ACT.Ln, bias=core.col("one")).then_inc(act_done, 1)
                act.wait_ge(dve_done, 5)
                nc.scalar.activation(flat(ein), flat(acs), ACT.Exp).then_inc(act_done, 1)
                nc.scalar.activation(flat(dec), flat(dec), ACT.Exp).then_inc(act_done, 1)
                nc.scalar.activation(flat(etot), core.psum[:, 1, 0:U], ACT.Exp).then_inc(act_done, 1)

            @st.block.tensor
            def _(pe):
                pe.wait_ge(dve_done, 3)
                nc.tensor.matmul(core.psum[:, 0, 0:U], upper[:], flat(ga), start=True, stop=True).then_inc(pe_done, 1)
                nc.tensor.matmul(core.psum[:, 1, 0:U], core.ones[:], flat(ga), start=True, stop=True).then_inc(pe_done, 1)

        with core.stage("gdn_pairs") as st:
            R = 3
            decay, row_in, beta_row = st.sb("decay", [P, R, P]), st.sb("row_in", [P, R, P]), st.sb("beta_row", [P, R, P])
            rows_done, diffed, read, exped, pairs_done, part, finished = (st.sem(s) for s in (
                "rows_done", "diffed", "read", "exped", "pairs_done", "part", "finished"))

            @st.block.tensor
            def _(pe):
                for u in range(U):
                    c, h, s = u // H, u % H, slice(u // H * P, (u // H + 1) * P)
                    if u >= 2:
                        pe.wait_ge(read, u - 1)
                    fga, fb = ga[:, c, h:h + 1].to_broadcast([P, P]), beta[:, c, h:h + 1].to_broadcast([P, P])
                    nc.tensor.matmul(core.psum[:, u % 2, 0:P], fga, upper[:], start=True, stop=True)
                    nc.tensor.matmul(core.psum[:, u % 2, P:2 * P], fb, core.ident[:], start=True, stop=True).then_inc(rows_done, 1)
                    if u >= 2:
                        pe.wait_ge(finished, 2 * (u - 1))
                    k = qkv[:, 4 + h, s]
                    nc.tensor.matmul(core.psum[:, 2 + u % 2, 0:P], k, k, start=True, stop=True)
                    nc.tensor.matmul(core.psum[:, 2 + u % 2, P:2 * P], k, qkv[:, h, s], start=True, stop=True).then_inc(pairs_done, 1)

            @st.block.vector
            def _(dve):
                for phase, u in lagged(U, {0: 0, 1: 1}):
                    c, h, s = u // H, u % H, slice(u // H * P, (u // H + 1) * P)
                    if phase == 0:
                        dve.wait_ge(rows_done, u + 1)
                        if u >= R:
                            dve.wait_ge(finished, 2 * (u - R + 1))
                        nc.vector.scalar_tensor_tensor(out=decay[:, u % R, :], in0=core.psum[:, u % 2, 0:P],
                                                       scalar=acs[:, c, h:h + 1], in1=masked[:], op0=ALU.subtract, op1=ALU.add
                                                       ).then_inc(diffed, 1)
                        nc.vector.tensor_tensor(beta_row[:, u % R, :], core.psum[:, u % 2, P:2 * P], strict[:], ALU.mult
                                                ).then_inc(diffed, 1)
                    else:
                        dve.wait_ge(exped, u + 1)
                        dve.wait_ge(pairs_done, u + 1)
                        d = decay[:, u % R, :]
                        nc.vector.tensor_tensor(lt[:, u, :], core.psum[:, 2 + u % 2, 0:P], d, ALU.mult).then_inc(part, 1)
                        nc.vector.scalar_tensor_tensor(out=att[:, u, :], in0=core.psum[:, 2 + u % 2, P:2 * P], scalar=scale, in1=d,
                                                       op0=ALU.mult, op1=ALU.mult).then_inc(finished, 1)
                        dve.wait_ge(part, 2 * u + 1)
                        nc.vector.tensor_tensor(lt[:, u, :], lt[:, u, :], beta_row[:, u % R, :], ALU.mult).then_inc(finished, 1)
                        dve.wait_ge(read, u + 1)
                        nc.vector.scalar_tensor_tensor(out=qd[:, u, :], in0=qkv[:, h, s], scalar=scale, in1=row_in[:, u % R, :],
                                                       op0=ALU.mult, op1=ALU.mult).then_inc(part, 1)

            @st.block.scalar
            def _(act):
                for u in range(U):
                    act.wait_ge(diffed, 2 * u + 2)
                    if u >= R:
                        act.wait_ge(part, 2 * (u - R + 1))
                    nc.scalar.activation(row_in[:, u % R, :], core.psum[:, u % 2, 0:P], ACT.Exp).then_inc(read, 1)
                    nc.scalar.activation(decay[:, u % R, :], decay[:, u % R, :], ACT.Exp).then_inc(exped, 1)

        solve(core, "gdn_solve", U, lambda u: lt[:, u, :], lambda u: xt[:, u, :], 1, lanes=8,
              room=qkv[:, 0:4, :].rearrange("p k (l b t) -> p (k l) b t", l=2, b=2))

        uu = b.sb("gdn_u", [P, U, P])
        with core.stage("gdn_apply") as st:
            vb, kb = st.sb("vb", [P, 2, P]), st.sb("kb", [P, 2, P])
            ready, multiplied, out = st.sem("ready"), st.sem("multiplied"), st.sem("out")

            @st.block.vector
            def _(dve):
                for u in range(U):
                    c, h = u // H, u % H
                    if u >= 2:
                        dve.wait_ge(multiplied, u - 1)
                    nc.vector.tensor_scalar(vb[:, u % 2, :], vt[:, c, h * P:(h + 1) * P], beta[:, c, h:h + 1], None, ALU.mult
                                            ).then_inc(ready, 1)
                    nc.vector.tensor_scalar(kb[:, u % 2, :], kt[:, c, h * P:(h + 1) * P], eneg[:, c, h:h + 1], None, ALU.mult
                                            ).then_inc(ready, 1)
                    dve.wait_ge(ready, 2 * u + 2)

            @st.block.tensor
            def _(pe):
                for u in range(U):
                    pe.wait_ge(ready, 2 * u + 2)
                    if u >= 4:
                        pe.wait_ge(out, 2 * (u - 3))
                    nc.tensor.matmul(core.psum[:, u % 4, 0:P], xt[:, u, :], vb[:, u % 2, :], start=True, stop=True)
                    nc.tensor.matmul(core.psum[:, u % 4, P:2 * P], kb[:, u % 2, :], xt[:, u, :], start=True, stop=True
                                     ).then_inc(multiplied, 1)

            @st.block.scalar
            def _(act):
                for u in range(U):
                    act.wait_ge(multiplied, u + 1)
                    nc.scalar.activation(uu[:, u, :], core.psum[:, u % 4, 0:P], ACT.Copy).then_inc(out, 1)
                    nc.scalar.activation(lt[:, u, :], core.psum[:, u % 4, P:2 * P], ACT.Copy).then_inc(out, 1)

        with core.stage("gdn_scan") as st:
            state = st.sb("state", [P, H, P])
            kd = st.sb("kd", [P, 4, P])
            zeroed, decayed, first, renewed, mixed, stored_, added_, updated = (st.sem(s) for s in (
                "zeroed", "decayed", "first", "renewed", "mixed", "stored", "added", "updated"))

            @st.block.tensor
            def _(pe):
                for phase, u in lagged(U, {0: 0, 1: 1}):
                    c, h = u // H, u % H
                    if phase == 0:
                        if u == 0:
                            pe.wait_ge(zeroed, 1)
                        if u >= 2:
                            pe.wait_ge(renewed, u - 1)
                        if c:
                            pe.wait_ge(updated, u - H + 1)
                        nc.tensor.matmul(core.psum[:, u % 2, 0:P], lt[:, u, :], state[:, h, :], start=True, stop=True).then_inc(first, 1)
                    else:
                        pe.wait_ge(renewed, u + 1)
                        if u >= 2:
                            pe.wait_ge(stored_, u - 1)
                            pe.wait_ge(updated, u - 1)
                        nc.tensor.matmul(core.psum[:, 2 + u % 2, 0:P], state[:, h, :], qd[:, u, :], start=True, stop=False)
                        nc.tensor.matmul(core.psum[:, 2 + u % 2, 0:P], uu[:, u, :], att[:, u, :], start=False, stop=True
                                         ).then_inc(mixed, 1)
                        pe.wait_ge(decayed, u + 1)
                        nc.tensor.matmul(core.psum[:, 4 + u % 2, 0:P], kd[:, u % 4, :], uu[:, u, :], start=True, stop=True
                                         ).then_inc(added_, 1)

            @st.block.vector
            def _(dve):
                nc.vector.memset(state[:], 0.0).then_inc(zeroed, 1)
                for phase, u in lagged(U, {0: 0, 1: 1}):
                    c, h = u // H, u % H
                    if phase == 0:
                        dve.wait_ge(first, u + 1)
                        nc.vector.tensor_tensor(uu[:, u, :], uu[:, u, :], core.psum[:, u % 2, 0:P], ALU.subtract).then_inc(renewed, 1)
                    else:
                        dve.wait_ge(added_, u + 1)
                        dve.wait_ge(mixed, u + 1)
                        nc.vector.scalar_tensor_tensor(out=state[:, h, :], in0=state[:, h, :], scalar=etot[:, c, h:h + 1],
                                                       in1=core.psum[:, 4 + u % 2, 0:P], op0=ALU.mult, op1=ALU.add
                                                       ).then_inc(updated, 1)

            @st.block.scalar
            def _(act):
                for phase, u in lagged(U, {0: 0, 1: 1}):
                    c, h = u // H, u % H
                    if phase == 0:
                        if u >= 4:
                            act.wait_ge(added_, u - 3)
                        nc.scalar.activation(kd[:, u % 4, :], kt[:, c, h * P:(h + 1) * P], ACT.Copy, scale=dec[:, c, h:h + 1]
                                             ).then_inc(decayed, 1)
                    else:
                        act.wait_ge(mixed, u + 1)
                        nc.scalar.activation(y[:, h, c * P:(c + 1) * P], core.psum[:, 2 + u % 2, 0:P], ACT.Copy).then_inc(stored_, 1)


def block3(core, xT, mean):
    with buffers(core) as b:
        h, ya = b.pair("b3_h", KD), b.sb("b3_ya", [P, 4, T])
        norm(core, "b3_pre", lambda i: xT[:, i, :], [list(range(KD))], mean, None, core.col("eps"),
             gain=lambda i: core.col("b3_norm1_g", i), pair=h)
        with buffers(core) as c:
            p = c.sb("rwkv_p", [P, 14, T])
            linear(core, "b3_p", h, token_shifted(lambda i: core.col("rwkv_mu", i), lambda i: p[:, i, :]))
            rwkv(core, p, ya)
        yb = b.sb("b3_yb", [P, 4, T])
        with buffers(core) as c:
            zT = c.sb("gdn_z", [P, 4, T])
            with buffers(core) as d:
                qkv, ab = d.sb("gdn_qkv", [P, 12, T]), d.sb("gdn_ab", [P, NT, 8])
                linear(core, "b3_qkvz", h, parts(
                    (12, convolved(4, lambda i, j: core.col("gdn_conv_w", 4 * i + j), lambda i: core.col("zero"),
                                   lambda i, at: qkv[:, i, :])),
                    (4, stored(lambda i, at: zT[:, i, :], ACT.Silu))))
                linear(core, "b3_ab", h, stored(lambda i, at: ab[:, i, :]), by_tokens=True)
                gated_delta(core, qkv, ab, yb)
            m128 = c.sb("mean128", [P, P])
            fill(core, "gdn_m128", [(m128, 1.0 / 128)])
            norm(core, "gdn_norm", lambda i: yb[:, i, :], [[i] for i in range(4)], m128[:], lambda i: yb[:, i, :],
                 core.col("eps"), gain=lambda i: core.col("gdn_norm_w"), times=lambda i: zT[:, i, :])
        with buffers(core) as c:
            gT, mixed = c.sb("b3_gates", [P, 2 * KD, T]), c.sb("b3_mixed", [P, KD, T])
            mix = lambda i: mixed[:, i, :]
            linear(core, "b3_gates", h, stored(lambda i, at: gT[:, i, :], ACT.Sigmoid))
            linear(core, "b3_rproj", lambda k: ya[:, k, :], scaled_to(mix, lambda i: gT[:, i, :]), raw=True, room=h)
            linear(core, "b3_gproj", lambda k: yb[:, k, :], added(mix, lambda i: gT[:, KD + i, :]), raw=True, room=h)
            linear(core, "b3_out", lambda k: mixed[:, k, :], added(lambda i: xT[:, i, :]), raw=True, room=h)
    conv_ffn(core, "b3", xT, mean)


def tiles_of(v):
    return v.reshape(-1, P).T


def taps_of(w):
    taps, f = w.shape
    return w.reshape(taps, f // P, P).transpose(2, 1, 0).reshape(P, -1)


def slabs_of(w, cols):
    k, f = w.shape
    return np.ascontiguousarray(w.reshape(k // P, P, f // cols, cols).transpose(2, 1, 0, 3).reshape(f // cols, P, -1))


def pairs_of(a, b):
    lead = a.shape[:-1]
    both = np.stack([a.reshape(lead + (-1, P)), b.reshape(lead + (-1, P))], axis=-2)
    return both.reshape(lead + (-1,))


def rows_of(v, times=1):
    return np.broadcast_to(np.tile(v, times)[None], (P, v.size * times))


def zeros(*shape):
    return np.zeros(shape, np.float32)


def weights_of(a):
    w = a["l0_w_in"]
    k1, k2 = w[:, 3216:3232], w[:, 3232:3248]
    low = np.concatenate([w[:, 2576:3216], zeros(D, 64), k1, k2, k2, k1], 1)
    q = a["l0_w_q_b"].reshape(384, 8, 96)
    q = np.concatenate([q[:, :, 0:96], q[:, :, 80:96], q[:, :, 64:80]], 2).reshape(384, 1024)
    kv = a["l0_w_kv_b"].reshape(256, 8, 128)
    out = {
        "l0_ada": (a["l0_ada_w"], 256, P),
        "l0_in": (np.concatenate([w[:, 1024:2560], w[:, 0:1024], low], 1), 256, P),
        "l0_dt": (w[:, 2560:2576], 16, 16),
        "l0_q": (q, 512, P),
        "l0_k": (kv[:, :, 0:64].reshape(256, 512), 512, 64),
        "l0_v": (kv[:, :, 64:128].reshape(256, 512), 512, 512),
        "l0_out": (a["l0_w_out"], 128, P),
        "l0_up": (pairs_of(a["l0_w_gate"], a["l0_w_up"]), 256, P),
        "l0_down": (a["l0_w_down"], P, P),
    }
    w = a["l1_w_in"]
    n = 3088
    nq = w[:, n:n + 512].reshape(D, 2, 4, 64).swapaxes(1, 2).reshape(D, 512)
    kc, vc, ks, vs, kw, vw = (w[:, 3600 + 128 * i:3728 + 128 * i] for i in range(6))
    wo = a["l1_w_out"]
    nsa_out = wo[1024:].reshape(2, 4, 64, D).swapaxes(0, 1).reshape(512, D)
    out |= {
        "l1_ada": (a["l1_ada_w"], 256, P),
        "l1_v": (w[:, 1024:2048], 256, 256),
        "l1_lr": (w[:, 2048:2064], 16, 16),
        "l1_in": (np.concatenate([w[:, 0:1024], w[:, 2064:3088], nq, kc, vc, ks, kw], 1), 256, P),
        "l1_nt": (np.concatenate([vs, vw, w[:, 4368:4392]], 1), 280, 280),
        "l1_cmp_k": (a["l1_cmp_k_w1"], 128, P),
        "l1_cmp_v": (a["l1_cmp_v_w1"], 128, P),
        "l1_out": (np.concatenate([wo[:1024], nsa_out], 0), 128, P),
        "l1_up": (pairs_of(a["l1_w_gate"], a["l1_w_up"]), 256, P),
        "l1_down": (a["l1_w_down"], P, P),
    }
    w = a["w_in_2"][0]
    q, k, v, conf_a, conf_gate, sc_b, sc_c, sc_x = (w[:, 768 * i:768 * (i + 1)] for i in range(8))
    fives = np.stack([x.reshape(D, 6, P) for x in (conf_gate, conf_a, sc_c, sc_x, sc_b)], 2).reshape(D, 3840)
    out |= {
        "b2_qk": (np.concatenate([q, k], 1), 256, P),
        "b2_v": (v, 256, 256),
        "b2_conf_sc": (np.concatenate([fives, w[:, 6144:9216]], 1), 256, P),
        "b2_attn_out": (a["w_attn_out_2"][0], 1024, P),
        "b2_conf_out": (a["w_conf_out_2"][0], 256, P),
        "b2_sc_out": (a["w_sc_out_2"][0], 256, P),
        "b2_o": (a["w_o_2"][0], 256, P),
        "b2_up": (pairs_of(*np.split(a["w_up_2"][0], 2, 1)), 256, P),
        "b2_down": (a["w_down_2"][0], P, P),
    }
    w = a["w_in_3"][0]
    out |= {
        "b3_p": (w[:, 0:1792], 256, P),
        "b3_qkvz": (w[:, 1792:3840], 256, P),
        "b3_ab": (w[:, 3840:3848], 8, 8),
        "b3_gates": (w[:, 3848:5896], 256, P),
        "b3_rproj": (a["rwkv_proj_3"][0], 512, P),
        "b3_gproj": (a["gdn_proj_3"][0], 512, P),
        "b3_out": (a["w_out_3"][0], 256, P),
        "b3_up": (pairs_of(*np.split(a["ffn_up_3"][0], 2, 1)), 256, P),
        "b3_down": (a["ffn_down_3"][0], P, P),
    }
    return out


def columns_of(a):
    c = {
        "eps": np.full((P, 1), EPS, np.float32), "one": np.ones((P, 1), np.float32),
        "c": tiles_of(a["c"][0]),
        "l0_dt_bias": rows_of(a["l0_dt_bias"], NT), "l0_a_log": rows_of(a["l0_a_log"], NT),
        "l0_d_skip": tiles_of(np.repeat(a["l0_d_skip"], 64)),
        "l0_conv_w": taps_of(a["l0_conv_w"]), "l0_conv_b": tiles_of(a["l0_conv_b"]),
    }
    for n in ("l0_ada_b", "l0_mix_pre_g", "l0_mix_post_g", "l0_ffn_pre_g", "l0_ffn_post_g", "l0_ssm_norm_g",
              "l0_q_a_norm_g", "l0_kv_a_norm_g", "l1_ada_b", "l1_mix_pre_g", "l1_mix_post_g", "l1_ffn_pre_g",
              "l1_ffn_post_g", "l1_b_gk", "l1_gla_norm_g"):
        c[n] = tiles_of(a[n])
    c["l1_cmp_pos"] = a["l1_cmp_pos"].reshape(16, P).T
    c["zero"] = zeros(P, 1)
    c["gn_eps"] = np.full((P, 1), 64e-5, np.float32)
    for n, v in (("b2_norm1_g", "norm1_g_2"), ("b2_conf_b", "conf_dw_b_2"), ("b2_ln_g", "conf_ln_g_2"), ("b2_ln_b", "conf_ln_b_2"),
                 ("b2_norm2_g", "norm2_g_2"), ("b3_norm1_g", "norm1_g_3"), ("rwkv_mu", "rwkv_mu_3"), ("rwkv_w0", "rwkv_w0_3"),
                 ("rwkv_a0", "rwkv_a0_3"), ("rwkv_k_k", "rwkv_k_k_3"), ("rwkv_k_a", "rwkv_k_a_3"), ("rwkv_r_k", "rwkv_r_k_3"),
                 ("rwkv_ln_w", "rwkv_ln_w_3"), ("rwkv_ln_b", "rwkv_ln_b_3"), ("gdn_norm_w", "gdn_norm_w_3"),
                 ("b3_norm2_g", "norm2_g_3")):
        c[n] = tiles_of(a[v][0])
    c["b2_final_g"], c["b3_final_g"] = tiles_of(a["final_g_2"]), tiles_of(a["final_g_3"])
    c["b2_conf_w"], c["b2_sc_w"] = taps_of(a["conf_dw_w_2"][0]), taps_of(a["sc_dw_w_2"][0])
    c["b2_ffn_dw_w"] = taps_of(pairs_of(*np.split(a["ffn_dw_w_2"][0], 2, 1)))
    c["b3_ffn_dw_w"] = taps_of(pairs_of(*np.split(a["ffn_conv_w_3"][0], 2, 1)))
    c["gdn_conv_w"] = taps_of(a["gdn_conv_w_3"][0])
    c["gdn_dt_bias"], c["gdn_a_log"] = rows_of(a["gdn_dt_bias_3"][0], NT), rows_of(a["gdn_a_log_3"][0], NT)
    inv = (10000.0 ** (-np.arange(0, 32, 2) / 32)).astype(np.float32)
    c["rope_inv"] = np.concatenate([np.tile(inv, 8)])[:, None]
    c["rope_sign"] = np.concatenate([np.ones(96), -np.ones(16), np.ones(16)]).astype(np.float32)[:, None]
    return c


def tables_of(a):
    i, j = np.arange(P)[:, None], np.arange(P)[None]
    x = np.arange(T)[None] - (T - P)
    t = {
        "ident": np.eye(P), "upper": i <= j, "lower_masked": np.where(i <= j, 0.0, MASKED),
        "fold": (i % 32 == j % 32) & (i >= 64) & (j >= 64),
        "causal": np.where(x <= i, 0.0, MASKED),
    }
    t["alibi"] = np.where(x <= i, x - i, MASKED)
    token = i + P * np.arange(NT)[:, None, None]
    dist = token - (16 * np.arange(CMP)[None] + 31)
    t["cmp_bias"] = np.where(dist >= 0, -dist, MASKED).swapaxes(0, 1)
    t["cmp_valid"] = (dist >= 0).swapaxes(0, 1)
    t["cmp_w2"] = np.stack([a["l1_cmp_k_w2"][:P], a["l1_cmp_k_w2"][P:], a["l1_cmp_v_w2"][:P], a["l1_cmp_v_w2"][P:]], 1)
    t["gk2"] = a["l1_w_gk2"]
    far, bias = i - x, []
    for g, d in enumerate((1, 4, 16)):
        ok = (far >= 0) & (far % d == 0) & (far <= 128 * d)
        for n in range(4):
            slope = np.exp2(np.float32(-8.0 * (4 * g + n + 1) / 12))
            bias.append(np.where(ok, -slope * far, MASKED))
    t["dilated"] = np.stack(bias, 1)
    t["blocks64"] = i // 64 == j // 64
    t["mean64"] = t["blocks64"] / 64.0
    t["strict_upper"] = i < j
    t["wkv_masks"] = np.concatenate([i < j, i <= j, i < j, i <= j], 1)
    t["joins"] = np.stack([(i // (2 << k) == j // (2 << k)) & (i // (1 << k) % 2 == 0) & (j // (1 << k) % 2 == 1)
                           for k in range(LEVELS)], 1)
    t["rwkv_w2_a2"] = np.concatenate([a["rwkv_w2_3"][0], a["rwkv_a2_3"][0]], 0)
    t["rwkv_g2"] = a["rwkv_g2_3"][0]
    t = {n: np.ascontiguousarray(v, np.float32) for n, v in t.items()}
    t["positions"] = np.ascontiguousarray(np.broadcast_to(a["positions"].reshape(1, T), (P, T)))
    return t


def lay_out(a, only=None):
    arrays, plan, columns, at = {}, [], {}, 0
    for n, (w, cols, gcols) in weights_of(a).items():
        if only is not None and not (n in only if isinstance(only, list) else n.startswith(only)):
            continue
        arrays[n] = slabs_of(w, cols)
        plan.append((n, w.shape[1] // cols, w.shape[0] // P, cols, gcols))
    cs = columns_of(a)
    for n, v in cs.items():
        columns[n] = (at, v.shape[1])
        at += v.shape[1]
    arrays["columns"] = np.ascontiguousarray(np.concatenate(list(cs.values()), 1))
    arrays.update(tables_of(a))
    return arrays, plan, columns


def start(core, xT, mean):
    nc = core.nc
    with core.stage("start") as st:
        loaded, filled = st.sem("loaded"), st.sem("filled")

        @st.block.sync
        def _(sp):
            sp.dma_start(core.cols[:], core.dram["columns"]).then_inc(loaded, 16)
            for s in range(RING):
                core.load_slab(sp, s)
            sp.dma_start(core.ident[:], core.dram["ident"]).then_inc(loaded, 16)
            sp.dma_start(xT[:], core.dram["x"].rearrange("(k p) t -> p k t", p=P)).then_inc(loaded, 16)
            sp.wait_ge(loaded, 48)

        @st.block.vector
        def _(dve):
            nc.vector.memset(mean[:], 1.0 / D).then_inc(filled, 1)
            nc.vector.memset(core.ones[:], 1.0).then_inc(filled, 1)


def finish(core, xT, out):
    with core.stage("finish") as st:
        written = st.sem("written")

        @st.block.sync
        def _(sp):
            sp.dma_start(out.rearrange("(k p) t -> p k t", p=P), xT[:]).then_inc(written, 16)
            sp.wait_ge(written, 16)


def silu_of_c(core, silu_c):
    nc = core.nc
    with core.stage("silu_c") as st:
        done = st.sem("done")

        @st.block.scalar
        def _(act):
            nc.scalar.activation(silu_c[:], core.colblock("c"), ACT.Silu).then_inc(done, 1)



def build_program(nc, dram, plan, columns, out):
    with ExitStack() as ctx:
        core = Core(nc, ctx, dram, plan, columns)
        buf = Pool(nc, ctx)
        xT = buf.sb("xT", [P, KD, T])
        mean = buf.sb("mean", [P, P])
        silu_c = buf.sb("silu_of_c", [P, KD])
        start(core, xT, mean)
        silu_of_c(core, silu_c)
        layer0(core, xT, silu_c, mean[:])
        layer1(core, xT, silu_c, mean[:])
        block2(core, xT, mean[:])
        block3(core, xT, mean[:])
        finish(core, xT, out)


def kernel(**inputs):
    import concourse.bacc as bacc
    from concourse.bass_utils import run_bass_kernel_spmd

    a = {name: np.asarray(v) for name, v in inputs.items()}
    arrays, plan, columns = lay_out(a)
    arrays["x"] = np.ascontiguousarray(a["x"][0].T)
    nc = bacc.Bacc("TRN2", target_bir_lowering=False, num_devices=1)
    dram = {name: nc.dram_tensor(f"in_{name}", v.shape, mybir.dt.from_np(v.dtype), kind="ExternalInput").ap()
            for name, v in arrays.items()}
    out = nc.dram_tensor("out_x", (D, T), F32, kind="ExternalOutput").ap()
    build_program(nc, dram, plan, columns, out)
    got = run_bass_kernel_spmd(nc, [{f"in_{name}": v for name, v in arrays.items()}], core_ids=[0])
    return np.ascontiguousarray(got.results[0]["out_x"].T)[None]
```
